# Optimizing a Trainium2 kernel written in Bass

```python
import jax
import jax.numpy as jnp
from jax import lax
import numpy as np

D_MODEL = 1024
BATCH = 1
SEQ = 256
DEPTH = 2

GRID_W = 64
N_MIXERS = 2
NORM_EPS = 1e-6
ROPE_THETA = 10000.0
RET_HEADS = 4
RET_DK = 256
RET_DV = 512
RET_QK = RET_HEADS * RET_DK
RET_V = RET_HEADS * RET_DV
RET_CHUNK = 128
ATT_HEADS = 8
ATT_KV_HEADS = 2
ATT_HD = 128
ATT_GROUP = ATT_HEADS // ATT_KV_HEADS
ATT_Q = ATT_HEADS * ATT_HD
ATT_KV = ATT_KV_HEADS * ATT_HD
Q_BLOCK = 128
D_FF = 2816
N_EXPERTS = 8
TOP_K = 2
D_FF_EXPERT = 3584

kernel_name = 'hybrid_retention_gqa_moe_adaln_encoder'

def rmsnorm(x, g):
    x32 = x.astype(jnp.float32)
    y = x32 * lax.rsqrt(jnp.mean(x32 * x32, axis=-1, keepdims=True) + NORM_EPS)
    return y.astype(x.dtype) * g

def modulate(h, shift, scale):
    return h * (1 + scale[:, None, :]) + shift[:, None, :]

def rope_1d(x, pos):
    d = x.shape[-1]
    freqs = ROPE_THETA ** (-jnp.arange(0, d // 2, dtype=jnp.float32) * 2.0 / d)
    ang = pos[:, None] * freqs[None, :]
    cos = jnp.cos(ang)[None, :, None, :].astype(x.dtype)
    sin = jnp.sin(ang)[None, :, None, :].astype(x.dtype)
    x1, x2 = jnp.split(x, 2, axis=-1)
    return jnp.concatenate([x1 * cos - x2 * sin, x1 * sin + x2 * cos], axis=-1)

def axial_rope(x, row, col):
    half = x.shape[-1] // 2
    return jnp.concatenate([rope_1d(x[..., :half], row), rope_1d(x[..., half:], col)], axis=-1)

def grid_positions(seq_len):
    rows = seq_len // GRID_W
    row = jnp.repeat(jnp.arange(rows, dtype=jnp.float32), GRID_W)
    col = jnp.tile(jnp.arange(GRID_W, dtype=jnp.float32), rows)
    return row, col

def chunk_retention(q, k, v, gamma, include_diag):
    bsz, seq, heads, dk = q.shape
    dv = v.shape[-1]
    n = seq // RET_CHUNK
    log_g = jnp.log(gamma)
    idx = jnp.arange(RET_CHUNK, dtype=jnp.float32)
    diff = idx[:, None] - idx[None, :]
    mask = diff >= 0 if include_diag else diff > 0
    d_intra = jnp.where(mask[None], jnp.exp(jnp.maximum(diff, 0.0)[None] * log_g[:, None, None]), 0.0).astype(q.dtype)
    xi = jnp.exp((idx[:, None] + 1.0) * log_g[None, :]).astype(q.dtype)
    zeta = jnp.exp((RET_CHUNK - 1.0 - idx[:, None]) * log_g[None, :]).astype(q.dtype)
    chunk_decay = jnp.exp(RET_CHUNK * log_g).astype(q.dtype)
    qc = q.reshape(bsz, n, RET_CHUNK, heads, dk)
    kc = k.reshape(bsz, n, RET_CHUNK, heads, dk)
    vc = v.reshape(bsz, n, RET_CHUNK, heads, dv)
    scores = jnp.einsum('bnihd,bnjhd->bnhij', qc, kc) * d_intra[None, None]
    y_intra = jnp.einsum('bnhij,bnjhe->bnihe', scores, vc)

    def step(state, inp):
        q_i, k_i, v_i = inp
        y_cross = jnp.einsum('bihd,bhde->bihe', q_i, state) * xi[None, :, :, None]
        state = state * chunk_decay[None, :, None, None] + jnp.einsum('bjhd,bjhe->bhde', k_i * zeta[None, :, :, None], v_i)
        return state, y_cross

    xs = (jnp.moveaxis(qc, 1, 0), jnp.moveaxis(kc, 1, 0), jnp.moveaxis(vc, 1, 0))
    state0 = jnp.zeros((bsz, heads, dk, dv), q.dtype)
    _, y_cross = lax.scan(step, state0, xs)
    y = y_intra + jnp.moveaxis(y_cross, 0, 1)
    return y.reshape(bsz, seq, heads, dv)

def retention_mixer(h, w_in, decay_logit, gn_g, w_out, row, col):
    bsz, seq, _ = h.shape
    proj = h @ w_in
    q, k, v, g = jnp.split(proj, [RET_QK, 2 * RET_QK, 2 * RET_QK + RET_V], axis=-1)
    q = axial_rope(q.reshape(bsz, seq, RET_HEADS, RET_DK), row, col)
    k = axial_rope(k.reshape(bsz, seq, RET_HEADS, RET_DK), row, col) * (RET_DK ** -0.5)
    v = v.reshape(bsz, seq, RET_HEADS, RET_DV)
    gamma = jax.nn.sigmoid(decay_logit.astype(jnp.float32))
    fwd = chunk_retention(q, k, v, gamma[0], True)
    bwd = jnp.flip(chunk_retention(jnp.flip(q, 1), jnp.flip(k, 1), jnp.flip(v, 1), gamma[1], False), 1)
    y = (fwd + bwd).astype(jnp.float32)
    mu = jnp.mean(y, axis=-1, keepdims=True)
    var = jnp.mean(jnp.square(y - mu), axis=-1, keepdims=True)
    y = ((y - mu) * lax.rsqrt(var + NORM_EPS)).reshape(bsz, seq, RET_V).astype(h.dtype) * gn_g
    return (jax.nn.silu(g) * y) @ w_out

def gqa_mixer(h, w_qkv, q_norm_g, k_norm_g, w_out, row, col):
    bsz, seq, _ = h.shape
    proj = h @ w_qkv
    q, k, v = jnp.split(proj, [ATT_Q, ATT_Q + ATT_KV], axis=-1)
    q = axial_rope(rmsnorm(q.reshape(bsz, seq, ATT_HEADS, ATT_HD), q_norm_g), row, col)
    k = axial_rope(rmsnorm(k.reshape(bsz, seq, ATT_KV_HEADS, ATT_HD), k_norm_g), row, col)
    v = v.reshape(bsz, seq, ATT_KV_HEADS, ATT_HD)
    nb = seq // Q_BLOCK
    qb = q.reshape(bsz, nb, Q_BLOCK, ATT_KV_HEADS, ATT_GROUP, ATT_HD).transpose(1, 0, 2, 3, 4, 5)
    scale = ATT_HD ** -0.5

    def block(q_blk):
        s = jnp.einsum('bqkgd,bskd->bkgqs', q_blk, k).astype(jnp.float32) * scale
        p = jax.nn.softmax(s, axis=-1).astype(v.dtype)
        return jnp.einsum('bkgqs,bskd->bqkgd', p, v)

    o = lax.map(block, qb)
    o = o.transpose(1, 0, 2, 3, 4, 5).reshape(bsz, seq, ATT_Q)
    return o @ w_out

def swiglu(h, w_gate, w_up, w_down):
    return (jax.nn.silu(h @ w_gate) * (h @ w_up)) @ w_down

def moe_swiglu(h, w_router, b_router, w_gate, w_up, w_down):
    logits = (h @ w_router).astype(jnp.float32) + b_router.astype(jnp.float32)
    top_v, top_i = lax.top_k(logits, TOP_K)
    top_w = jax.nn.softmax(top_v, axis=-1)
    combine = jnp.sum(jax.nn.one_hot(top_i, N_EXPERTS, dtype=jnp.float32) * top_w[..., None], axis=-2).astype(h.dtype)
    out = jnp.zeros_like(h)
    for e in range(N_EXPERTS):
        out = out + combine[..., e:e + 1] * swiglu(h, w_gate[e], w_up[e], w_down[e])
    return out

def setup_inputs(seed: int = 0) -> dict:
    key = jax.random.key(seed)
    ks = iter(jax.random.split(key, 40))
    D = D_MODEL

    def nrm(shape, scale):
        return jax.random.normal(next(ks), shape, jnp.float32) * scale

    def gain(n):
        return 1.0 + nrm((n,), 0.02)

    a = 5.0 + jnp.arange(RET_HEADS, dtype=jnp.float32)
    base_logit = jnp.log(2.0 ** a - 1.0)
    inp = {}
    inp['x'] = nrm((BATCH, SEQ, D), 1.0)
    inp['c'] = nrm((BATCH, D), 1.0)
    inp['l0_ada_w'] = nrm((D, 6 * D), 0.5 * D ** -0.5)
    inp['l0_ada_b'] = nrm((6 * D,), 0.01)
    inp['l0_norm1_g'] = gain(D)
    inp['l0_norm2_g'] = gain(D)
    inp['l0_ret_w_in'] = nrm((D, 2 * RET_QK + 2 * RET_V), D ** -0.5)
    inp['l0_ret_decay_logit'] = base_logit[None, :] + nrm((2, RET_HEADS), 0.01)
    inp['l0_ret_gn_g'] = gain(RET_V)
    inp['l0_ret_w_out'] = nrm((RET_V, D), RET_V ** -0.5)
    inp['l0_ffn_w_gate'] = nrm((D, D_FF), D ** -0.5)
    inp['l0_ffn_w_up'] = nrm((D, D_FF), D ** -0.5)
    inp['l0_ffn_w_down'] = nrm((D_FF, D), D_FF ** -0.5)
    inp['l1_ada_w'] = nrm((D, 6 * D), 0.5 * D ** -0.5)
    inp['l1_ada_b'] = nrm((6 * D,), 0.01)
    inp['l1_norm1_g'] = gain(D)
    inp['l1_norm2_g'] = gain(D)
    inp['l1_attn_w_qkv'] = nrm((D, ATT_Q + 2 * ATT_KV), D ** -0.5)
    inp['l1_attn_q_norm_g'] = gain(ATT_HD)
    inp['l1_attn_k_norm_g'] = gain(ATT_HD)
    inp['l1_attn_w_out'] = nrm((ATT_Q, D), ATT_Q ** -0.5)
    inp['l1_moe_w_router'] = nrm((D, N_EXPERTS), D ** -0.5)
    inp['l1_moe_b_router'] = nrm((N_EXPERTS,), 0.01)
    inp['l1_moe_w_gate'] = nrm((N_EXPERTS, D, D_FF_EXPERT), D ** -0.5)
    inp['l1_moe_w_up'] = nrm((N_EXPERTS, D, D_FF_EXPERT), D ** -0.5)
    inp['l1_moe_w_down'] = nrm((N_EXPERTS, D_FF_EXPERT, D), D_FF_EXPERT ** -0.5)
    inp['final_ada_w'] = nrm((D, 2 * D), 0.5 * D ** -0.5)
    inp['final_ada_b'] = nrm((2 * D,), 0.01)
    inp['final_norm_g'] = gain(D)
    return inp

def reference(x, c, l0_ada_w, l0_ada_b, l0_norm1_g, l0_norm2_g, l0_ret_w_in, l0_ret_decay_logit, l0_ret_gn_g, l0_ret_w_out, l0_ffn_w_gate, l0_ffn_w_up, l0_ffn_w_down, l1_ada_w, l1_ada_b, l1_norm1_g, l1_norm2_g, l1_attn_w_qkv, l1_attn_q_norm_g, l1_attn_k_norm_g, l1_attn_w_out, l1_moe_w_router, l1_moe_b_router, l1_moe_w_gate, l1_moe_w_up, l1_moe_w_down, final_ada_w, final_ada_b, final_norm_g):
    seq = x.shape[1]
    row, col = grid_positions(seq)
    c_act = jax.nn.silu(c)
    layers = [
        (l0_ada_w, l0_ada_b, l0_norm1_g, l0_norm2_g,
         (l0_ret_w_in, l0_ret_decay_logit, l0_ret_gn_g, l0_ret_w_out),
         (l0_ffn_w_gate, l0_ffn_w_up, l0_ffn_w_down)),
        (l1_ada_w, l1_ada_b, l1_norm1_g, l1_norm2_g,
         (l1_attn_w_qkv, l1_attn_q_norm_g, l1_attn_k_norm_g, l1_attn_w_out),
         (l1_moe_w_router, l1_moe_b_router, l1_moe_w_gate, l1_moe_w_up, l1_moe_w_down)),
    ]
    for i in range(DEPTH):
        ada_w, ada_b, n1, n2, mix_p, ffn_p = layers[i]
        mod = c_act @ ada_w + ada_b
        sh1, sc1, g1, sh2, sc2, g2 = jnp.split(mod, 6, axis=-1)
        h = modulate(rmsnorm(x, n1), sh1, sc1)
        if i % N_MIXERS == 0:
            m = retention_mixer(h, *mix_p, row, col)
        else:
            m = gqa_mixer(h, *mix_p, row, col)
        x = x + g1[:, None, :] * m
        h = modulate(rmsnorm(x, n2), sh2, sc2)
        if i % 2 == 0:
            f = swiglu(h, *ffn_p)
        else:
            f = moe_swiglu(h, *ffn_p)
        x = x + g2[:, None, :] * f
    fmod = c_act @ final_ada_w + final_ada_b
    fsh, fsc = jnp.split(fmod, 2, axis=-1)
    return modulate(rmsnorm(x, final_norm_g), fsh, fsc)


_drawn_inputs = setup_inputs


def setup_inputs(seed=0):
    import zlib

    import numpy as np

    out = dict(_drawn_inputs(seed))
    spreads = {}
    factors = {'l0_ada_b': 3.97,
     'l0_norm1_g': 5.802,
     'l0_norm2_g': 5.995,
     'l0_ret_gn_g': 6.686,
     'l1_ada_b': 4.733,
     'l1_norm1_g': 8.0,
     'l1_norm2_g': 18.632,
     'l1_attn_q_norm_g': 8.0,
     'l1_attn_k_norm_g': 8.0,
     'l1_moe_b_router': 29.209,
     'final_ada_b': 4.39,
     'final_norm_g': 7.756}
    for name, (base, spread) in spreads.items():
        noise = np.random.default_rng([zlib.crc32(name.encode()), seed]).standard_normal(out[name].shape)
        drawn = base * np.exp(spread * noise) if base else spread * noise
        out[name] = jnp.asarray(drawn.astype(out[name].dtype))
    for name, factor in factors.items():
        out[name] = (out[name] * factor).astype(out[name].dtype)
    return out
```

```python
from contextlib import ExitStack

import numpy as np

import concourse.bass as bass
from concourse import mybir

P = 128
D = 1024
SEQ = 256
TT = SEQ // P
KT = D // P
GRID_W = 64
RH, RDK, RDV = 4, 256, 512
RQK, RV = RH * RDK, RH * RDV
W_IN = 2 * RQK + 2 * RV
AH, AKV, AHD = 8, 2, 128
QKV = (AH + 2 * AKV) * AHD
FF = 2816
E = 8
FE = 3584
EPS = 1e-6
ROPE_THETA = 10000.0

F32 = mybir.dt.float32
F32R = mybir.dt.float32r
I32 = mybir.dt.int32
U32 = mybir.dt.uint32
ALU = mybir.AluOpType
ACT = mybir.ActivationFunctionType
AX = mybir.AxisListType

UW = 2048
RING = 6
HRING = 3
CB = 512
U_RET = 0
N_IN = W_IN // CB
U_ROUT = U_RET + 2 * N_IN
FCH = 256
N_FF = FF // FCH
U_FF = U_ROUT + 2 * (RV // CB)
U_QKV = U_FF + 3 * N_FF
U_AOUT = U_QKV + 2 * (QKV // CB)
U_MOE = U_AOUT + 2 * (D // CB)
ECH = 512
N_EC = FE // ECH
UNITS_ITEM = 6 * N_EC
SLOTS = 128
N_TAB = 16

AC = 256
ARING = 2
V_PRE = 8
V_IN = 16
V_FIN = 8
V_A = 12
V_B = 12

C_ID = 0
C_ONE = C_ID + P
C_TRI = C_ONE + P
C_IOTA = C_TRI + P
C_RC = C_IOTA + P
C_RS = C_RC + TT * 2 * 64
C_AC = C_RS + TT * 2 * 64
C_AS = C_AC + TT * 2 * 32
C_EPS = C_AS + TT * 2 * 32
C_N = C_EPS + 8


def shape_constants():
    c = np.zeros((P, C_N), np.float32)
    c[:, C_ID:C_ID + P] = np.eye(P)
    c[:, C_ONE:C_ONE + P] = 1.0
    c[:, C_TRI:C_TRI + P] = np.triu(np.ones((P, P)), 1)
    c[:, C_IOTA:C_IOTA + P] = np.arange(P)[None]
    tok = np.arange(SEQ)
    pos = [(tok // GRID_W).astype(np.float32), (tok % GRID_W).astype(np.float32)]
    for n, cc, cs in ((64, C_RC, C_RS), (32, C_AC, C_AS)):
        fr = (np.float32(ROPE_THETA) ** (-np.arange(n, dtype=np.float32) * np.float32(2.0) / np.float32(2 * n))).astype(np.float32)
        for half in range(2):
            ang = (pos[half][:, None] * fr[None]).astype(np.float32)
            for t in range(TT):
                o = (t * 2 + half) * n
                c[:, cc + o:cc + o + n] = np.cos(ang[t * P:(t + 1) * P])
                c[:, cs + o:cs + o + n] = np.sin(ang[t * P:(t + 1) * P])
    c[:, C_EPS] = EPS
    j = np.arange(P)[:, None]
    i = np.arange(SEQ)[None]
    dist = np.zeros((P, 2, TT, SEQ), np.float32)
    for jt in range(TT):
        d = i - (j + jt * P)
        dist[:, 0, jt] = np.maximum(d, 0)
        dist[:, 1, jt] = np.maximum(-d, 0)
    return c, dist.reshape(P, -1)


def encoder(nc, x, c, l0_ada_w, l0_ada_b, l0_norm1_g, l0_norm2_g, l0_ret_w_in, l0_ret_decay_logit,
            l0_ret_gn_g, l0_ret_w_out, l0_ffn_w_gate, l0_ffn_w_up, l0_ffn_w_down, l1_ada_w, l1_ada_b,
            l1_norm1_g, l1_norm2_g, l1_attn_w_qkv, l1_attn_q_norm_g, l1_attn_k_norm_g, l1_attn_w_out,
            l1_moe_w_router, l1_moe_b_router, l1_moe_w_gate, l1_moe_w_up, l1_moe_w_down,
            final_ada_w, final_ada_b, final_norm_g, consts, dist, out):
    ctx = ExitStack()
    with ctx:
        base = (nc.sbuf_base + 31) // 32 * 32
        top = [0]

        def at(name, shape, offset, dt=F32):
            return nc.alloc_sbuf_tensor_at(name, [P] + shape, dt, offset=base + 4 * offset)

        def sb(name, shape, dt=F32):
            o = top[0]
            n = int(np.prod(shape))
            top[0] = o + (n + 7) // 8 * 8
            return at(name, shape, o, dt)

        def sem(name):
            return ctx.enter_context(nc.semaphore(name))

        stage = sb("stage", [RING, UW])
        lo = at("lo", [RING, UW], 0, F32R)
        hi = sb("hi", [HRING, UW], F32R)
        ada_w = sb("ada_w", [ARING, KT, AC])
        ada_b = sb("ada_b", [ARING, AC])
        ada_acc = sb("ada_acc", [ARING, AC])
        mods = sb("mods", [2, 3, D])
        xs = sb("xs", [TT, D])
        h_at = top[0]
        hs = sb("hs", [TT, D])
        gn = at("gn", [RV], h_at)
        g_at = top[0]
        normg = sb("normg", [D])
        ropet = at("ropet", [3, 256], g_at)
        cst = sb("cst", [C_N])
        ccol = sb("ccol", [KT])
        cact = sb("cact", [KT])
        ssq = sb("ssq", [TT])
        root = sb("root", [TT])
        rstd = sb("rstd", [TT])
        declog = sb("declog", [2 * RH])
        decexp = sb("decexp", [2 * RH])
        decln = sb("decln", [2 * RH])
        gstat = sb("gstat", [8, 6])
        gmv = sb("gmv", [8, 2])
        groot = sb("groot", [8])
        grstd = sb("grstd", [8])
        pos = sb("pos", [TT, 2 * E])
        comb = sb("comb", [TT, E])
        meta = sb("meta", [2 * N_TAB + 8], I32)
        R = top[0]
        KW = 256
        hT_hi = at("hT_hi", [KT, SEQ], R, F32R)
        hT_lo = at("hT_lo", [KT, SEQ], R + 8 * KW, F32R)
        proj = at("proj", [N_IN, TT, CB], R + 16 * KW)
        dst = at("dst", [2, TT * SEQ], R)
        dec = at("dec", [2, TT * SEQ], R + 4 * KW)
        rqT = at("rqT", [2, 2, SEQ], R + 8 * KW)
        rkT = at("rkT", [2, 2, SEQ], R + 12 * KW)
        yT_hi = at("yT_hi", [2 * KT, SEQ], R + 16 * KW, F32R)
        yT_lo = at("yT_lo", [2 * KT, SEQ], R + 32 * KW, F32R)
        finrow = at("finrow", [ARING, AC], R)
        fsil = at("fsil", [TT, FCH], R + 16 * KW)
        fact = at("fact", [TT, FCH], R + 18 * KW)
        faT_hi = at("faT_hi", [2, SEQ], R + 20 * KW, F32R)
        faT_lo = at("faT_lo", [2, SEQ], R + 22 * KW, F32R)
        oT_hi = at("oT_hi", [AH, SEQ], R, F32R)
        oT_lo = at("oT_lo", [AH, SEQ], R + 8 * KW, F32R)
        qkv = at("qkv", [TT, QKV], R + 16 * KW)
        apt = at("apt", [3, TT, 320], R + 28 * KW)
        aqT = at("aqT", [AH, SEQ], R + 36 * KW)
        akT = at("akT", [AKV, SEQ], R + 44 * KW)
        prob = at("prob", [2, TT, SEQ], R + 46 * KW)
        probT = at("probT", [2, TT, SEQ], R + 50 * KW)
        asq = at("asq", [10 * AHD], R + 54 * KW)
        again = at("again", [2, AHD], R + 59 * KW)
        ahs = at("ahs", [TT, 4, 10], R + 60 * KW)
        asm = at("asm", [AH, 4, TT], R + 61 * KW)
        hg_hi = at("hg_hi", [KT, SLOTS], R, F32R)
        hg_lo = at("hg_lo", [KT, SLOTS], R + 4 * KW, F32R)
        moe = at("moe", [TT, D], R + 8 * KW)
        hh = at("hh", [TT, D], R + 16 * KW, F32R)
        hl = at("hl", [TT, D], R + 24 * KW, F32R)
        pick = at("pick", [TT, SLOTS], R + 32 * KW, F32R)
        put = at("put", [SEQ], R + 33 * KW, F32R)
        esil = at("esil", [ECH], R + 34 * KW)
        eact = at("eact", [ECH], R + 36 * KW)
        eaT_hi = at("eaT_hi", [4, SLOTS], R + 38 * KW, F32R)
        eaT_lo = at("eaT_lo", [4, SLOTS], R + 40 * KW, F32R)
        dn_hi = at("dn_hi", [D], R + 42 * KW, F32R)
        dn_lo = at("dn_lo", [D], R + 46 * KW, F32R)
        wr = at("wr", [KT, E], R + 50 * KW)
        wr_hi = at("wr_hi", [KT, E], R + 51 * KW, F32R)
        wr_lo = at("wr_lo", [KT, E], R + 52 * KW, F32R)
        rsm = at("rsm", [TT, 10, 8], R + 53 * KW)
        ridx = at("ridx", [TT, 8], R + 54 * KW, U32)
        rtab = at("rtab", [2 * N_TAB + 8], R + 55 * KW)
        rflag = at("rflag", [4, 8], R + 56 * KW)
        brt = at("brt", [E], R + 57 * KW)
        assert base + 4 * (R + 64 * KW) <= nc.sbuf_usable_end, (base + 4 * (R + 64 * KW), nc.sbuf_usable_end)

        bank = ctx.enter_context(nc.psum_tensor("bank", [P, 8, 512], F32))
        fin_dram = nc.dram_tensor("fin_rows", [1, 2 * D], F32, kind="Internal").ap()

        ident = cst[:, C_ID:C_ID + P]
        ones = cst[:, C_ONE:C_ONE + P]
        tri = cst[:, C_TRI:C_TRI + P]
        iota = cst[:, C_IOTA:C_IOTA + P]
        eps = cst[:, C_EPS:C_EPS + 1]

        w_load = [sem(f"w_load{i}") for i in range(RING)]
        hi_done = sem("hi_done")
        lo_done = sem("lo_done")
        w_used = sem("w_used")
        a_load = [sem(f"a_load{i}") for i in range(ARING)]
        a_acc = sem("a_acc")
        a_step = sem("a_step")
        a_sum = sem("a_sum")
        a_out = sem("a_out")
        const_in = sem("const_in")
        x_in = sem("x_in")
        c_in = sem("c_in")
        g_in = sem("g_in")
        aux_in = sem("aux_in")
        c_act = sem("c_act")
        v_link = sem("v_link")
        s_link = sem("s_link")
        p_link = sem("p_link")
        b_zero = sem("b_zero")
        root_done = sem("root_done")
        scale_done = sem("scale_done")
        h_ready = sem("h_ready")
        tr_done = sem("tr_done")
        hT_hi_done = sem("hT_hi_done")
        hT_done = sem("hT_done")
        proj_out = sem("proj_out")
        rope_done = sem("rope_done")
        sg_done = sem("sg_done")
        gate_done = sem("gate_done")
        ln_done = sem("ln_done")
        arg_done = sem("arg_done")
        dec_done = sem("dec_done")
        qk_tr = sem("qk_tr")
        qT_done = sem("qT_done")
        kT_done = sem("kT_done")
        sc_done = sem("sc_done")
        s_done = sem("s_done")
        y_done = sem("y_done")
        st_done = sem("st_done")
        yraw_done = sem("yraw_done")
        mv_done = sem("mv_done")
        groot_done = sem("groot_done")
        gated = sem("gated")
        y_tr = sem("y_tr")
        yT_hi_done = sem("yT_hi_done")
        yT_done = sem("yT_done")
        resid = sem("resid")
        row_out = [sem(f"row_out{i}") for i in range(ARING)]
        row_in = sem("row_in")
        f_silu = sem("f_silu")
        f_act = sem("f_act")
        f_tr = sem("f_tr")
        f_hi = sem("f_hi")
        f_lo = sem("f_lo")
        qkv_out = sem("qkv_out")
        hsum = sem("hsum")
        hroot = sem("hroot")
        qn_done = sem("qn_done")
        arope = sem("arope")
        aq_tr = sem("aq_tr")
        aq_out = sem("aq_out")
        at_sc = sem("at_sc")
        at_max = sem("at_max")
        at_exp = sem("at_exp")
        at_norm = sem("at_norm")
        at_tr = sem("at_tr")
        at_pT = sem("at_pT")
        at_o = sem("at_o")
        o_hi = sem("o_hi")
        o_lo = sem("o_lo")
        r_in = sem("r_in")
        r_w = sem("r_w")
        r_mm = sem("r_mm")
        r_d = sem("r_d")
        r_e = sem("r_e")
        r_sel = sem("r_sel")
        r_rank = sem("r_rank")
        r_meta = sem("r_meta")
        hh_done = sem("hh_done")
        hl_done = sem("hl_done")
        m_zero = sem("m_zero")
        pick_done = sem("pick_done")
        gath = sem("gath")
        hg_hi_done = sem("hg_hi_done")
        hg_lo_done = sem("hg_lo_done")
        put_tr = sem("put_tr")
        put_done = sem("put_done")
        e_silu = sem("e_silu")
        e_act = sem("e_act")
        e_tr = sem("e_tr")
        e_hi = sem("e_hi")
        e_lo = sem("e_lo")
        dn_hi_done = sem("dn_hi_done")
        dn_done = sem("dn_done")
        scat = sem("scat")
        moe_add = sem("moe_add")
        stored = sem("stored")

        def rows(w):
            return w.rearrange("(k p) n -> p k n", p=P)

        def bcast(v, n):
            return v.partition_broadcast(P)

        w_in_v, w_out_v = rows(l0_ret_w_in), rows(l0_ret_w_out)
        fg_v, fu_v, fd_v = rows(l0_ffn_w_gate), rows(l0_ffn_w_up), rows(l0_ffn_w_down)
        qkv_v, ao_v = rows(l1_attn_w_qkv), rows(l1_attn_w_out)
        mg_v = l1_moe_w_gate.rearrange("e (k p) n -> e p k n", p=P)
        mu_v = l1_moe_w_up.rearrange("e (k p) n -> e p k n", p=P)
        md_v = l1_moe_w_down.rearrange("e (k p) n -> e p k n", p=P)

        block = ctx.enter_context(nc.Block())

        @block.sync
        def _(sp):
            sp.sem_inc(w_used, RING)
            sp.sem_inc(a_acc, ARING)
            sp.sem_inc(a_sum, ARING)
            sp.sem_inc(a_out, ARING)
            sp.sem_inc(proj_out, 3)

            def load(b, src, more=0, occ=0):
                sp.wait_ge(w_used, b + more + 1)
                dst_ap = stage[:, b % RING, :]
                dims = src.shape
                dst_ap = dst_ap.rearrange("p (k n) -> p k n", k=dims[1])
                sp.dma_start(dst_ap, src).then_inc(w_load[b % RING], 16)

            def load_ada(b, w, bias, col, more=0):
                sp.wait_ge(a_acc, b + more + 1)
                sp.dma_start(ada_w[:, b % ARING], rows(w)[:, :, bass.ds(col, AC)]).then_inc(a_load[b % ARING], 16)
                sp.dma_start(ada_b[0:1, b % ARING, :], bias.unsqueeze(0)[:, bass.ds(col, AC)]).then_inc(a_load[b % ARING], 16)

            sp.dma_start(ccol[:, :], c.rearrange("a (k p) -> p (a k)", p=P), allow_slow_non_contiguous=True).then_inc(c_in, 16)
            sp.dma_start(cst[:, :], consts).then_inc(const_in, 16)
            xv = x.rearrange("a (t p) d -> p (a t) d", p=P)
            sp.dma_start(xs[:, :, :], xv).then_inc(x_in, 16)
            sp.wait_ge(b_zero, 1)
            for v in range(V_PRE):
                load_ada(v, l0_ada_w, l0_ada_b, v * AC)
            with sp.Fori(0, N_IN // 3) as it:
                a = 0
                for k in range(6):
                    load(U_RET + k, w_in_v[:, (k % 2) * 4:(k % 2) * 4 + 4, bass.ds(it * (3 * CB) + (k // 2) * CB, CB)], it * 6)
                    if k in (0, 1, 3, 4):
                        load_ada(V_PRE + a, l0_ada_w, l0_ada_b, it * (4 * AC) + (V_PRE + a) * AC, it * 4)
                        a += 1
            v = V_PRE + V_IN
            for k in range(8):
                n, kg = k // 4, k % 4
                load(U_ROUT + k, w_out_v[:, 4 * kg:4 * kg + 4, n * CB:(n + 1) * CB])
                load_ada(v + k, final_ada_w, final_ada_b, k * AC)
            v += V_FIN
            load(U_FF, fg_v[:, :, 0:FCH])
            load_ada(v, l1_ada_w, l1_ada_b, 0)
            load(U_FF + 1, fu_v[:, :, 0:FCH])
            load_ada(v + 1, l1_ada_w, l1_ada_b, AC)
            with sp.Fori(0, (N_FF - 1) // 2) as it:
                for q in range(2):
                    b = U_FF + 2 + 3 * q
                    load(b, fg_v[:, :, bass.ds(it * (2 * FCH) + (q + 1) * FCH, FCH)], it * 6)
                    load_ada(v + 2 + q, l1_ada_w, l1_ada_b, it * (2 * AC) + (2 + q) * AC, it * 2)
                    load(b + 1, fu_v[:, :, bass.ds(it * (2 * FCH) + (q + 1) * FCH, FCH)], it * 6)
                    load(b + 2, fd_v[:, bass.ds(it * 4 + 2 * q, 2), :], it * 6)
            load(U_QKV - 1, fd_v[:, 2 * (N_FF - 1):2 * N_FF, :])
            v += V_A
            a = 0
            for k in range(6):
                n, kg = k // 2, k % 2
                load(U_QKV + k, qkv_v[:, 4 * kg:4 * kg + 4, n * CB:(n + 1) * CB])
                for _ in range(2 if k < 2 else 1):
                    load_ada(v + a, l1_ada_w, l1_ada_b, (V_A + a) * AC)
                    a += 1
            for k in range(4):
                n, kg = k // 2, k % 2
                load(U_AOUT + k, ao_v[:, 4 * kg:4 * kg + 4, n * CB:(n + 1) * CB])
            for k in range(4):
                load_ada(v + a, l1_ada_w, l1_ada_b, (V_A + a) * AC)
                a += 1

            def load_gate_up(e, b, col, more):
                for m, wv in ((0, mg_v), (2, mu_v)):
                    for g in range(2):
                        load(b + m + g, wv[e, :, 4 * g:4 * g + 4, col] if isinstance(e, int) else
                             wv[bass.ds(e, 1), :, 4 * g:4 * g + 4, col].rearrange("a p k n -> p (a k) n"), more)

            def load_down(e, b, kt, more):
                for g in range(2):
                    ks = bass.ds(kt + 2 * g, 2)
                    load(b + g, md_v[e, :, ks, :] if isinstance(e, int) else
                         md_v[bass.ds(e, 1), :, ks, :].rearrange("a p k n -> p (a k) n"), more)

            def item(e, more):
                load_gate_up(e, U_MOE, slice(0, ECH), more)
                with sp.Fori(1, N_EC) as j:
                    jm = j * 6 - 6
                    load_gate_up(e, U_MOE + 4, bass.ds(j * ECH, ECH), more + jm)
                    load_down(e, U_MOE + 8, j * 4 - 4, more + jm)
                load_down(e, U_MOE + UNITS_ITEM - 2, 4 * (N_EC - 1), more)

            item(0, 0)
            sp.wait_ge(r_meta, 1)
            passes = sp.value_load(meta[0:1, 2 * N_TAB:2 * N_TAB + 1], min_val=E, max_val=E + 3)
            with sp.Fori(1, passes) as w:
                e = sp.value_load(meta[0:1, bass.ds(w, 1)], min_val=0, max_val=E - 1)
                item(e, w * UNITS_ITEM)
            sp.wait_ge(stored, 32)

        @block.gpsimd
        def _(pool):
            nc.gpsimd.memset(ada_b[:, :, :], 0.0).then_inc(b_zero, 1)
            n_link = [0]

            def link(ins):
                n_link[0] += 1
                ins.then_inc(p_link, 1)
                pool.wait_ge(p_link, n_link[0])

            pool.dma_start(normg[:, :], l0_norm1_g.partition_broadcast(P)).then_inc(g_in, 16)
            pool.dma_start(declog[:, :], l0_ret_decay_logit.rearrange("a b -> (a b)").partition_broadcast(P)).then_inc(aux_in, 16)
            pool.wait_ge(tr_done, 4)
            pool.dma_start(gn[:, :], l0_ret_gn_g.partition_broadcast(P)).then_inc(aux_in, 16)

            def rotate(x1, x2, co, si, shape, tmp, last):
                ta, tb, tc = (t.rearrange(shape[0], **shape[1]) for t in tmp)
                nc.gpsimd.tensor_tensor(ta, x1, co, ALU.mult)
                nc.gpsimd.tensor_tensor(tb, x2, si, ALU.mult)
                nc.gpsimd.tensor_tensor(tc, x1, si, ALU.mult)
                link(nc.gpsimd.tensor_tensor(x2, x2, co, ALU.mult))
                nc.gpsimd.tensor_tensor(x1, ta, tb, ALU.subtract)
                ins = nc.gpsimd.tensor_tensor(x2, x2, tc, ALU.add)
                link(ins)

            pool.wait_ge(const_in, 16)
            pool.wait_ge(scale_done, 1)
            for q in range(4):
                pool.wait_ge(proj_out, 3 + q + 1)
                for t in range(TT):
                    v = proj[:, q, t, :].rearrange("p (h f s i) -> p h f s i", h=2, f=2, s=2)
                    for f in range(2):
                        co = cst[:, C_RC + (t * 2 + f) * 64:C_RC + (t * 2 + f + 1) * 64].unsqueeze(1).to_broadcast([P, 2, 64])
                        si = cst[:, C_RS + (t * 2 + f) * 64:C_RS + (t * 2 + f + 1) * 64].unsqueeze(1).to_broadcast([P, 2, 64])
                        rotate(v[:, :, f, 0, :], v[:, :, f, 1, :], co, si, ("p (h i) -> p h i", dict(h=2)),
                               [ropet[:, i, 0:128] for i in range(3)], False)
            pool.nop().then_inc(rope_done, 1)
            pool.dma_start(normg[:, :], l0_norm2_g.partition_broadcast(P)).then_inc(g_in, 16)
            pool.wait_ge(w_used, RING + U_ROUT)
            pool.dma_start(dst[:, :, :], dist.rearrange("p (s n) -> p s n", s=2)).then_inc(aux_in, 16)
            pool.wait_ge(aux_in, 48)
            for h in range(RH):
                pool.wait_ge(sg_done, h + 1)
                for t in range(TT):
                    g = proj[:, 8 + h, t, :]
                    nc.gpsimd.tensor_tensor(g, g, gn[:, h * RDV:(h + 1) * RDV], ALU.mult).then_inc(gate_done, 1)
            pool.wait_ge(scale_done, 2)
            pool.dma_start(normg[:, :], l1_norm1_g.partition_broadcast(P)).then_inc(g_in, 16)
            pool.wait_ge(scale_done, 3)
            pool.dma_start(again[:, 0, :], l1_attn_q_norm_g.partition_broadcast(P)).then_inc(aux_in, 16)
            pool.dma_start(again[:, 1, :], l1_attn_k_norm_g.partition_broadcast(P)).then_inc(aux_in, 16)
            pool.dma_start(normg[:, :], l1_norm2_g.partition_broadcast(P)).then_inc(g_in, 16)
            for t in range(TT):
                pool.wait_ge(qn_done, t + 1)
                v = qkv[:, t, 0:10 * AHD].rearrange("p (h f s i) -> p h f s i", h=10, f=2, s=2)
                for f in range(2):
                    co = cst[:, C_AC + (t * 2 + f) * 32:C_AC + (t * 2 + f + 1) * 32].unsqueeze(1).to_broadcast([P, 10, 32])
                    si = cst[:, C_AS + (t * 2 + f) * 32:C_AS + (t * 2 + f + 1) * 32].unsqueeze(1).to_broadcast([P, 10, 32])
                    rotate(v[:, :, f, 0, :], v[:, :, f, 1, :], co, si, ("p (h i) -> p h i", dict(h=10)),
                           [apt[:, i, t, :] for i in range(3)], False)
                pool.nop().then_inc(arope, 1)
            pool.wait_ge(resid, 3 * 4)
            pool.dma_start(wr[:, :, :], l1_moe_w_router.rearrange("(k p) e -> p k e", p=P)).then_inc(r_in, 16)
            pool.dma_start(brt[:, :], l1_moe_b_router.partition_broadcast(P)).then_inc(r_in, 16)
            for r in row_out:
                pool.wait_ge(r, 16 * V_FIN // ARING)
            pool.dma_start(mods[:, 0, 0, :], fin_dram[0, 0:D].partition_broadcast(P)).then_inc(row_in, 16)
            pool.dma_start(mods[:, 0, 1, :], fin_dram[0, D:2 * D].partition_broadcast(P)).then_inc(row_in, 16)
            pool.wait_ge(scale_done, 4)
            pool.dma_start(normg[:, :], final_norm_g.partition_broadcast(P)).then_inc(g_in, 16)

        @block.scalar
        def _(act):
            n_link = [0]

            def link(ins):
                n_link[0] += 1
                ins.then_inc(s_link, 1)
                act.wait_ge(s_link, n_link[0])

            def high(b, more=0, occ=0):
                act.wait_ge(w_load[b % RING], 16 * (b // RING + 1) + occ * 16)
                act.wait_ge(w_used, RING + b - HRING + 1 + more)
                nc.scalar.copy(hi[:, b % HRING, :], stage[:, b % RING, :]).then_inc(hi_done, 1)

            def ada_take(b, dst_ap, more=0):
                act.wait_ge(a_sum, ARING + b + 1 + more)
                nc.scalar.copy(dst_ap, bank[:, 3, (b % ARING) * AC:(b % ARING + 1) * AC]).then_inc(a_out, 1)

            def mod_at(col):
                return mods[:, :, :, :].rearrange("p a b d -> p (a b d)")[:, bass.ds(col, AC)]

            def norm(s, h_free):
                h_free()
                for t in range(TT):
                    nc.scalar.activation(hs[:, t, :], xs[:, t, :], ACT.Square, accum_out=ssq[:, t:t + 1]).then_inc(s_link, 1)
                n_link[0] += TT
                act.wait_ge(s_link, n_link[0])
                nc.scalar.activation(root[:, :], ssq[:, :], ACT.Sqrt, scale=1.0 / D, bias=eps).then_inc(root_done, 1)

            def high_T(s):
                for i in range(4):
                    act.wait_ge(tr_done, 4 * s + i + 1)
                    t, g = i // 2, i % 2
                    nc.scalar.copy(hT_hi[:, 4 * g:4 * g + 4, t * P:(t + 1) * P],
                                   bank[:, 4 + i, :].rearrange("p (k n) -> p k n", k=4)).then_inc(hT_hi_done, 1)

            act.wait_ge(c_in, 16)
            nc.scalar.activation(cact[:, :], ccol[:, :], ACT.Silu).then_inc(c_act, 1)
            for v in range(V_PRE):
                ada_take(v, mod_at(v * AC))
            act.wait_ge(x_in, 16)
            act.wait_ge(const_in, 16)
            norm(0, lambda: None)
            for k in range(3):
                high(U_RET + k)
            high_T(0)

            PAIRS = [(0, 1), (2, 4), (5, 6)]

            def take_chunk(i, cc):
                act.wait_ge(w_used, RING + U_RET + 2 + cc * 2)
                for t in range(TT):
                    ins = nc.scalar.copy(
                        proj[:, :, :, :].rearrange("p c t n -> p (c t n)")[:, bass.ds(cc * (TT * CB) + t * CB, CB)],
                        bank[:, PAIRS[i][t], :])
                ins.then_inc(proj_out, 1)

            def in_body(it, first, skip=0):
                for k in range(skip, 6):
                    high(U_RET + k, it * 6, it)
                    in_after(it, k, first)

            def in_after(it, k, first):
                if k == 0 and not first:
                    ada_take(V_PRE + 2, mod_at(it * (4 * AC) - 4 * AC + (V_PRE + 2) * AC), it * 4 - 4)
                    take_chunk(1, it * 3 - 2)
                if k == 1 and not first:
                    ada_take(V_PRE + 3, mod_at(it * (4 * AC) - 4 * AC + (V_PRE + 3) * AC), it * 4 - 4)
                if k == 2 and not first:
                    take_chunk(2, it * 3 - 1)
                if k == 3:
                    ada_take(V_PRE, mod_at(it * (4 * AC) + V_PRE * AC), it * 4)
                if k == 4:
                    ada_take(V_PRE + 1, mod_at(it * (4 * AC) + (V_PRE + 1) * AC), it * 4)
                    take_chunk(0, it * 3)

            in_body(0, True, 3)
            with act.Fori(1, N_IN // 3) as it:
                in_body(it, False)
            last = N_IN // 3
            for k in range(3):
                high(U_ROUT + k)
                in_after(last, k, False)

            act.wait_ge(aux_in, 48)
            link(nc.scalar.activation(decexp[:, :], declog[:, :], ACT.Exp, scale=-1.0))
            nc.scalar.activation(decln[:, :], decexp[:, :], ACT.Ln, bias=1.0).then_inc(ln_done, 1)

            def q_take(h):
                act.wait_ge(qk_tr, 2 * h + 1)
                if h >= 2:
                    act.wait_ge(sc_done, h - 1)
                nc.scalar.copy(rqT[:, h % 2], bank[:, 4, :].rearrange("p (k n) -> p k n", k=2)).then_inc(qT_done, 1)

            def decay(h):
                act.wait_ge(arg_done, h + 1)
                nc.scalar.activation(dec[:, h % 2], dec[:, h % 2], ACT.Exp, scale=-1.0).then_inc(dec_done, 1)

            decay(0)
            decay(1)
            for h in range(RH):
                g = proj[:, 8 + h, :, :]
                if h == 0:
                    act.wait_ge(proj_out, 3 + N_IN)
                nc.scalar.activation(g, g, ACT.Silu).then_inc(sg_done, 1)
            q_take(0)
            q_take(1)

            def y_take(h):
                act.wait_ge(y_done, 2 * h + 2)
                act.wait_ge(st_done, 2 * h + 2)
                for t in range(TT):
                    nc.scalar.copy(proj[:, 4 + h, t, :], bank[:, (7, 2)[t], :]).then_inc(yraw_done, 1)

            for h in range(RH):
                y_take(h)
                if h + 2 < RH:
                    decay(h + 2)
                    q_take(h + 2)
            act.wait_ge(mv_done, 1)
            nc.scalar.activation(groot[:, :], gmv[:, :, 1], ACT.Sqrt, bias=eps).then_inc(groot_done, 1)
            for i in range(8):
                act.wait_ge(y_tr, i + 1)
                h, t = i // 2, i % 2
                nc.scalar.copy(yT_hi[:, 4 * h:4 * h + 4, t * P:(t + 1) * P],
                               bank[:, 4 + i % 4, :].rearrange("p (k n) -> p k n", k=4)).then_inc(yT_hi_done, 1)
            def fin_take(a):
                v = V_PRE + V_IN + a
                if a >= ARING:
                    act.wait_ge(row_out[a % ARING], 16 * (a // ARING))
                ada_take(v, finrow[:, v % ARING, :])
                act.wait_ge(a_out, ARING + v + 1)
                act.dma_start(fin_dram[0:1, a * AC:(a + 1) * AC], finrow[0:1, v % ARING, :]).then_inc(row_out[a % ARING], 16)

            for k in range(3, 8):
                high(U_ROUT + k)
                fin_take(k - 3)
            for a in range(5, 8):
                fin_take(a)
            for r in row_out:
                act.wait_ge(r, 16 * V_FIN // ARING)

            act.wait_ge(resid, 4)
            norm(1, lambda: None)
            high(U_FF)
            high(U_FF + 1)
            high_T(1)
            V0 = V_PRE + V_IN + V_FIN

            def f_silu_step(cc):
                act.wait_ge(w_used, RING + U_FF + 1 if isinstance(cc, int) and cc == 0 else cc * 3 + (RING + U_FF))
                act.wait_ge(f_act, cc)
                nc.scalar.activation(fsil[:, :, :].rearrange("p t n -> p (t n)"), bank[:, 0, :], ACT.Silu).then_inc(f_silu, 1)

            def f_high_act(cc):
                act.wait_ge(f_tr, cc + 1)
                nc.scalar.copy(faT_hi[:, :, :], bank[:, 2, :].rearrange("p (k n) -> p k n", k=2)).then_inc(f_hi, 1)

            f_silu_step(0)
            ada_take(V0, mod_at(0))
            ada_take(V0 + 1, mod_at(AC))
            with act.Fori(0, (N_FF - 1) // 2) as it:
                for q in range(2):
                    b = U_FF + 2 + 3 * q
                    cc = it * 2 + 1 + q
                    high(b, it * 6, it)
                    high(b + 1, it * 6, it)
                    f_high_act(cc - 1)
                    high(b + 2, it * 6, it)
                    f_silu_step(cc)
                    ada_take(V0 + 2 + q, mod_at(it * (2 * AC) + (2 + q) * AC), it * 2)
            high(U_QKV - 1)
            f_high_act(N_FF - 1)

            act.wait_ge(resid, 8)
            norm(2, lambda: None)
            high(U_QKV)
            high(U_QKV + 1)
            high_T(2)
            high(U_QKV + 2)
            V1 = V0 + V_A
            M1 = 3 * D

            def qkv_take(n):
                act.wait_ge(w_used, RING + U_QKV + 2 * n + 2)
                for t in range(TT):
                    ins = nc.scalar.copy(qkv[:, t, n * CB:(n + 1) * CB], bank[:, PAIRS[n][t], :])
                ins.then_inc(qkv_out, 1)

            a = 0
            for k in range(3, 6):
                for _ in range(2 if k < 5 else 1):
                    ada_take(V1 + a, mod_at(M1 + a * AC))
                    a += 1
                high(U_QKV + k)
                if k == 4:
                    qkv_take(0)
            for _ in range(3):
                ada_take(V1 + a, mod_at(M1 + a * AC))
                a += 1
            qkv_take(1)
            qkv_take(2)
            for k in range(3):
                high(U_AOUT + k)
            for t in range(TT):
                act.wait_ge(hsum, t + 1)
                nc.scalar.activation(ahs[:, t, 1, :], ahs[:, t, 0, :], ACT.Sqrt, scale=1.0 / AHD, bias=eps).then_inc(hroot, 1)
            for i in range(5):
                act.wait_ge(aq_tr, i + 1)
                dst_ap = (aqT[:, 2 * i:2 * i + 2, :] if i < 4 else akT[:, :, :])
                nc.scalar.copy(dst_ap, bank[:, (4, 5)[i % 2], :].rearrange("p (k n) -> p k n", k=2)).then_inc(aq_out, 1)

            def soft(h):
                act.wait_ge(at_max, h + 1)
                if h >= 2:
                    act.wait_ge(at_tr, h - 1)
                for t in range(TT):
                    ins = nc.scalar.activation(prob[:, h % 2, t, :], bank[:, 4 + h % 2, t * SEQ:(t + 1) * SEQ], ACT.Exp,
                                               bias=asm[:, h, 1, t:t + 1], scale=float(AHD) ** -0.5,
                                               accum_out=asm[:, h, 2, t:t + 1])
                    ins.then_inc(at_exp, 1)

            def pT_take(h):
                act.wait_ge(at_tr, h + 1)
                if h >= 2:
                    act.wait_ge(at_o, h - 1)
                nc.scalar.copy(probT[:, h % 2], bank[:, 6 + h % 2, :].rearrange("p (k n) -> p k n", k=2)).then_inc(at_pT, 1)

            def o_take(h):
                act.wait_ge(at_o, h + 1)
                nc.scalar.copy(oT_hi[:, h, :], bank[:, h % 2, 0:SEQ]).then_inc(o_hi, 1)

            for h in range(AH + 2):
                if h < AH:
                    soft(h)
                if 1 <= h <= AH:
                    pT_take(h - 1)
                if h >= 2:
                    o_take(h - 2)
            for k in range(3, 4):
                high(U_AOUT + k)
            for k in range(4):
                ada_take(V1 + a, mod_at(M1 + a * AC))
                a += 1

            act.wait_ge(resid, 12)
            norm(3, lambda: None)
            for k in range(3):
                high(U_MOE + k)
            high_T(3)
            act.wait_ge(r_in, 32)
            nc.scalar.copy(wr_hi[:, :, :], wr[:, :, :]).then_inc(r_w, 1)
            for t in range(TT):
                nc.scalar.copy(hh[:, t, :], hs[:, t, :]).then_inc(hh_done, 1)
            act.wait_ge(r_d, 1)
            nc.scalar.activation(rsm[:, :, 5, 0:1], rsm[:, :, 4, 0:1], ACT.Exp).then_inc(r_e, 1)

            def take_gathered(w):
                act.wait_ge(gath, w * 2 + 1)
                nc.scalar.copy(hg_hi[:, :, :], bank[:, 6:8, :].rearrange("p b (k n) -> p (b k) n", k=4)).then_inc(hg_hi_done, 1)

            def take_put(w):
                act.wait_ge(put_tr, w + 1)
                nc.scalar.copy(put[:, :], bank[:, 6, 0:SEQ]).then_inc(put_done, 1)

            def e_silu_step(n, used):
                act.wait_ge(w_used, used)
                act.wait_ge(e_act, n)
                nc.scalar.activation(esil[:, :], bank[:, 0, :], ACT.Silu).then_inc(e_silu, 1)

            def e_high_act(n):
                act.wait_ge(e_tr, n + 1)
                nc.scalar.copy(eaT_hi[:, :, :], bank[:, 2, :].rearrange("p (k n) -> p k n", k=4)).then_inc(e_hi, 1)

            take_gathered(0)
            take_put(0)

            def item(w, skip):
                m, o = w * UNITS_ITEM, w * N_EC
                for k in range(skip, 4):
                    high(U_MOE + k, m, o)
                e_silu_step(w * N_EC, m + (RING + U_MOE + 2))
                with act.Fori(1, N_EC) as j:
                    jm, jo = m + j * 6 - 6, o + j - 1
                    b = U_MOE + 4
                    n = w * N_EC + j
                    high(b, jm, jo)
                    high(b + 1, jm, jo)
                    high(b + 2, jm, jo)
                    e_high_act(n - 1)
                    high(b + 3, jm, jo)
                    high(b + 4, jm, jo)
                    e_silu_step(n, jm + (RING + U_MOE + 6))
                    high(b + 5, jm, jo)
                high(U_MOE + UNITS_ITEM - 2, m, o)
                high(U_MOE + UNITS_ITEM - 1, m, o)
                e_high_act(w * N_EC + N_EC - 1)
                act.wait_ge(w_used, m + (RING + U_MOE + UNITS_ITEM))
                nc.scalar.copy(dn_hi[:, :], bank[:, 4:6, :].rearrange("p b n -> p (b n)")).then_inc(dn_hi_done, 1)
                take_gathered(w + 1)
                take_put(w + 1)

            item(0, 3)
            passes = act.value_load(meta[0:1, 2 * N_TAB:2 * N_TAB + 1], min_val=E, max_val=E + 3)
            with act.Fori(1, passes) as w:
                item(w, 0)
            act.wait_ge(resid, 16)
            norm(4, lambda: None)
            ov = out.rearrange("a (t p) d -> p (a t) d", p=P)
            for t in range(TT):
                act.wait_ge(h_ready, 2 * 4 + t + 1)
                act.dma_start(ov[:, t, :], hs[:, t, :]).then_inc(stored, 16)
            act.wait_ge(stored, 32)

        @block.vector
        def _(dve):
            n_link = [0]

            def link(ins):
                n_link[0] += 1
                ins.then_inc(v_link, 1)
                dve.wait_ge(v_link, n_link[0])

            def low(b, more=0):
                dve.wait_ge(hi_done, b + 1 + more)
                nc.vector.tensor_tensor(lo[:, b % RING, :], stage[:, b % RING, :],
                                        hi[:, b % HRING, :].bitcast(F32), ALU.subtract).then_inc(lo_done, 1)

            def ada(b, more=0, half=0):
                s = b % ARING
                dve.wait_ge(a_load[s], 32 * (b // ARING + 1) + half * 32)
                dve.wait_ge(a_sum, b + 1 + more)
                for k in range(KT):
                    prev = ada_b[:, s, :] if k == 0 else ada_acc[:, s, :]
                    ins = nc.vector.scalar_tensor_tensor(out=ada_acc[:, s, :], in0=ada_w[:, s, k, :],
                                                         scalar=cact[:, k:k + 1], in1=prev,
                                                         op0=ALU.mult, op1=ALU.add)
                    if k < KT - 1:
                        ins.then_inc(a_step, 1)
                        dve.wait_ge(a_step, (KT - 1) * b + k + 1 + more * (KT - 1))
                ins.then_inc(a_acc, 1)

            def norm(s, took):
                m = mods[:, s % 2]
                dve.wait_ge(g_in, 16 * (s + 1))
                if took:
                    dve.wait_ge(a_out, ARING + took)
                nc.vector.scalar_tensor_tensor(out=m[:, 1, :], in0=m[:, 1, :], scalar=1.0, in1=normg[:, :],
                                               op0=ALU.add, op1=ALU.mult).then_inc(scale_done, 1)
                dve.wait_ge(scale_done, s + 1)
                dve.wait_ge(root_done, s + 1)
                link(nc.vector.reciprocal(rstd[:, :], root[:, :]))
                for t in range(TT):
                    nc.vector.scalar_tensor_tensor(out=hs[:, t, :], in0=xs[:, t, :], scalar=rstd[:, t:t + 1],
                                                   in1=m[:, 1, :], op0=ALU.mult, op1=ALU.mult).then_inc(v_link, 1)
                    n_link[0] += 1
                for t in range(TT):
                    dve.wait_ge(v_link, n_link[0] - TT + 1 + t)
                    nc.vector.tensor_tensor(hs[:, t, :], hs[:, t, :], m[:, 0, :], ALU.add).then_inc(h_ready, 1)

            def low_T(s):
                for i in range(4):
                    dve.wait_ge(hT_hi_done, 4 * s + i + 1)
                    t, g = i // 2, i % 2
                    nc.vector.tensor_tensor(hT_lo[:, 4 * g:4 * g + 4, t * P:(t + 1) * P],
                                            bank[:, 4 + i, :].rearrange("p (k n) -> p k n", k=4),
                                            hT_hi[:, 4 * g:4 * g + 4, t * P:(t + 1) * P].bitcast(F32),
                                            ALU.subtract).then_inc(hT_done, 1)

            def residual(s, order, used):
                m = mods[:, s % 2, 2]
                for (n, t, src), u in zip(order, used):
                    cols = slice(n * CB, (n + 1) * CB)
                    dve.wait_ge(w_used, RING + u)
                    link(nc.vector.tensor_tensor(hs[:, t, cols], src, m[:, cols], ALU.mult))
                    nc.vector.tensor_tensor(xs[:, t, cols], xs[:, t, cols], hs[:, t, cols], ALU.add).then_inc(resid, 1)

            dve.wait_ge(c_act, 1)
            for v in range(V_PRE):
                ada(v)
            dve.wait_ge(x_in, 16)
            norm(0, V_PRE)
            low(U_RET)
            low_T(0)
            def in_step(it, k):
                if k:
                    low(U_RET + k, it * 6)
                if k in (0, 1, 3, 4):
                    a = (0, 1, None, 2, 3)[k]
                    ada(V_PRE + a, it * 4, it * 2)

            for k in range(6):
                in_step(0, k)
            with dve.Fori(1, N_IN // 3) as it:
                low(U_RET, it * 6)
                for k in range(6):
                    in_step(it, k)
            for k in range(3):
                low(U_ROUT + k)

            def decay_arg(h):
                b = h % 2
                link(nc.vector.tensor_scalar(dec[:, b], dst[:, 0], decln[:, h:h + 1], None, ALU.mult))
                nc.vector.scalar_tensor_tensor(out=dec[:, b], in0=dst[:, 1], scalar=decln[:, RH + h:RH + h + 1],
                                               in1=dec[:, b], op0=ALU.mult, op1=ALU.add).then_inc(arg_done, 1)

            def k_take(h):
                dve.wait_ge(qk_tr, 2 * h + 2)
                if h >= 2:
                    dve.wait_ge(sc_done, h - 1)
                nc.vector.tensor_copy(rkT[:, h % 2], bank[:, 5, :].rearrange("p (k n) -> p k n", k=2)).then_inc(kT_done, 1)

            dve.wait_ge(ln_done, 1)
            dve.wait_ge(aux_in, 48)
            decay_arg(0)
            decay_arg(1)
            k_take(0)
            k_take(1)
            for h in range(RH):
                dve.wait_ge(sc_done, h + 1)
                dve.wait_ge(dec_done, h + 1)
                nc.vector.scalar_tensor_tensor(out=dec[:, h % 2], in0=bank[:, 6, :], scalar=float(RDK) ** -0.5,
                                               in1=dec[:, h % 2], op0=ALU.mult, op1=ALU.mult).then_inc(s_done, 1)
                for t in range(TT):
                    dve.wait_ge(y_done, 2 * h + t + 1)
                    nc.vector.bn_stats(gstat[:, 2 * h + t, :], bank[:, (7, 2)[t], :]).then_inc(st_done, 1)
                if h + 2 < RH:
                    decay_arg(h + 2)
                    k_take(h + 2)
            dve.wait_ge(st_done, 2 * RH)
            for i in range(8):
                ins = nc.vector.bn_aggr(gmv[:, i, :], gstat[:, i, :])
            ins.then_inc(mv_done, 1)
            dve.wait_ge(groot_done, 1)
            link(nc.vector.reciprocal(grstd[:, :], groot[:, :]))
            dve.wait_ge(yraw_done, 2 * RH)
            dve.wait_ge(gate_done, 2 * RH)

            def gate(i):
                h, t = i // 2, i % 2
                y, g = proj[:, 4 + h, t, :], proj[:, 8 + h, t, :]
                link(nc.vector.tensor_scalar(y, y, gmv[:, i, 0:1], grstd[:, i:i + 1], ALU.subtract, ALU.mult))
                nc.vector.tensor_tensor(g, y, g, ALU.mult).then_inc(gated, 1)

            def low_y(i):
                dve.wait_ge(yT_hi_done, i + 1)
                dve.wait_ge(gated, 2 * (i // 2) + 2)
                h, t = i // 2, i % 2
                nc.vector.tensor_tensor(yT_lo[:, 4 * h:4 * h + 4, t * P:(t + 1) * P],
                                        bank[:, 4 + i % 4, :].rearrange("p (k n) -> p k n", k=4),
                                        yT_hi[:, 4 * h:4 * h + 4, t * P:(t + 1) * P].bitcast(F32),
                                        ALU.subtract).then_inc(yT_done, 1)

            gate(0)
            gate(1)
            for i in range(8):
                if i + 2 < 8:
                    gate(i + 2)
                low_y(i)
            v = V_PRE + V_IN
            for k in range(8):
                if k >= 3:
                    low(U_ROUT + k)
                ada(v + k)
            residual(0, [(0, 0, bank[:, 0, :]), (0, 1, bank[:, 1, :]), (1, 0, bank[:, 6, :]), (1, 1, bank[:, 7, :])],
                     [U_FF - 4] * 2 + [U_FF] * 2)

            V0 = V_PRE + V_IN + V_FIN
            norm(1, V_PRE + V_IN)
            low(U_FF)
            low_T(1)

            def f_mul(cc):
                dve.wait_ge(w_used, RING + U_FF + 2 if isinstance(cc, int) and cc == 0 else cc * 3 + (RING + U_FF + 1))
                dve.wait_ge(f_silu, cc + 1)
                dve.wait_ge(f_tr, cc)
                nc.vector.tensor_tensor(fact[:, :, :].rearrange("p t n -> p (t n)"), bank[:, 1, :],
                                        fsil[:, :, :].rearrange("p t n -> p (t n)"), ALU.mult).then_inc(f_act, 1)

            def f_low_act(cc):
                dve.wait_ge(f_hi, cc + 1)
                nc.vector.tensor_tensor(faT_lo[:, :, :], bank[:, 2, :].rearrange("p (k n) -> p k n", k=2),
                                        faT_hi[:, :, :].bitcast(F32), ALU.subtract).then_inc(f_lo, 1)

            ada(V0)
            low(U_FF + 1)
            ada(V0 + 1)

            def f_pair(it):
                for q in range(2):
                    b = U_FF + 2 + 3 * q
                    cc = it * 2 + 1 + q
                    low(b, it * 6)
                    f_mul(cc - 1)
                    low(b + 1, it * 6)
                    f_low_act(cc - 1)
                    low(b + 2, it * 6)
                    ada(V0 + 2 + q, it * 2, it)

            f_pair(0)
            with dve.Fori(1, (N_FF - 1) // 2) as it:
                f_pair(it)
            f_mul(N_FF - 1)
            low(U_QKV - 1)
            f_low_act(N_FF - 1)
            residual(1, [(0, 0, bank[:, 4, :]), (1, 0, bank[:, 5, :]), (0, 1, bank[:, 6, :]), (1, 1, bank[:, 7, :])],
                     [U_QKV] * 4)

            V1 = V0 + V_A
            norm(2, V1)
            low(U_QKV)
            low_T(2)
            a = 0
            for k in range(6):
                if k:
                    low(U_QKV + k)
                for _ in range(2 if k < 2 else 1):
                    ada(V1 + a)
                    a += 1
            for k in range(3):
                low(U_AOUT + k)
            dve.wait_ge(qkv_out, 3)
            dve.wait_ge(aux_in, 80)
            for t in range(TT):
                qk = qkv[:, t, 0:10 * AHD]
                qh = qk.rearrange("p (h d) -> p h d", h=10)
                link(nc.vector.tensor_tensor(asq[:, :], qk, qk, ALU.mult))
                nc.vector.tensor_reduce(ahs[:, t, 0, :], asq[:, :].rearrange("p (h d) -> p h d", h=10), AX.X,
                                        ALU.add).then_inc(hsum, 1)
                for n, o, m in ((0, 0, AH), (1, AH, AKV)):
                    ins = nc.vector.tensor_tensor(qh[:, o:o + m, :], qh[:, o:o + m, :],
                                                  again[:, n, :].unsqueeze(1).to_broadcast([P, m, AHD]), ALU.mult)
                    ins.then_inc(v_link, 1)
                    n_link[0] += 1
                dve.wait_ge(hroot, t + 1)
                link(nc.vector.reciprocal(ahs[:, t, 2, :], ahs[:, t, 1, :]))
                nc.vector.tensor_tensor(qh, qh, ahs[:, t, 2, :].unsqueeze(2).to_broadcast([P, 10, AHD]),
                                        ALU.mult).then_inc(qn_done, 1)

            def row_max(h):
                dve.wait_ge(at_sc, h + 1)
                link(nc.vector.tensor_reduce(asm[:, h, 0, :], bank[:, 4 + h % 2, :].rearrange("p (t n) -> p t n", t=TT),
                                             AX.X, ALU.max))
                nc.vector.tensor_scalar(asm[:, h, 1, :], asm[:, h, 0, :], -float(AHD) ** -0.5, None,
                                        ALU.mult).then_inc(at_max, 1)

            def row_norm(h):
                dve.wait_ge(at_exp, 2 * h + 2)
                link(nc.vector.reciprocal(asm[:, h, 3, :], asm[:, h, 2, :]))
                for t in range(TT):
                    p = prob[:, h % 2, t, :]
                    nc.vector.tensor_scalar(p, p, asm[:, h, 3, t:t + 1], None, ALU.mult).then_inc(at_norm, 1)

            def o_low(h):
                dve.wait_ge(o_hi, h + 1)
                nc.vector.tensor_tensor(oT_lo[:, h, :], bank[:, h % 2, 0:SEQ], oT_hi[:, h, :].bitcast(F32),
                                        ALU.subtract).then_inc(o_lo, 1)

            for h in range(AH + 2):
                if h < AH:
                    row_max(h)
                    row_norm(h)
                if h >= 2:
                    o_low(h - 2)
            low(U_AOUT + 3)
            for k in range(4):
                ada(V1 + a)
                a += 1
            residual(2, [(0, 0, bank[:, 0, :]), (0, 1, bank[:, 1, :]), (1, 0, bank[:, 6, :]), (1, 1, bank[:, 7, :])],
                     [U_MOE - 2] * 2 + [U_MOE] * 2)

            norm(3, V1 + V_B)
            low(U_MOE)
            low_T(3)
            dve.wait_ge(r_w, 1)
            nc.vector.tensor_tensor(wr_lo[:, :, :], wr[:, :, :], wr_hi[:, :, :].bitcast(F32), ALU.subtract).then_inc(r_w, 1)
            for k in range(1, 3):
                low(U_MOE + k)
            for t in range(TT):
                dve.wait_ge(hh_done, t + 1)
                nc.vector.tensor_tensor(hl[:, t, :], hs[:, t, :], hh[:, t, :].bitcast(F32), ALU.subtract).then_inc(hl_done, 1)
            io8 = iota[:, 0:8]
            dve.wait_ge(r_mm, 1)
            for t in range(TT):
                r = rsm[:, t]
                link(nc.vector.tensor_tensor(r[:, 0, :], bank[:, t, 0:E], brt[:, :], ALU.add))
                link(nc.vector.max(r[:, 1, :], r[:, 0, :]))
                link(nc.vector.max_index(ridx[:, t, :], r[:, 1, :], r[:, 0, :]))
                link(nc.vector.tensor_copy(r[:, 2, :], ridx[:, t, :]))
                nc.vector.tensor_scalar(r[:, 6, :], io8, r[:, 2, 0:1], None, ALU.is_equal)
                nc.vector.tensor_scalar(r[:, 7, :], io8, r[:, 2, 1:2], None, ALU.is_equal)
                link(nc.vector.tensor_tensor(r[:, 4, 0:1], r[:, 1, 1:2], r[:, 1, 0:1], ALU.subtract))
            nc.vector.nop().then_inc(r_d, 1)
            for t in range(TT):
                link(nc.vector.tensor_tensor(rsm[:, t, 8, :], rsm[:, t, 6, :], rsm[:, t, 7, :], ALU.add))
            dve.nop().then_inc(r_sel, 1)
            dve.wait_ge(r_e, 1)
            for t in range(TT):
                r = rsm[:, t]
                link(nc.vector.tensor_scalar(r[:, 5, 1:2], r[:, 5, 0:1], 1.0, None, ALU.add))
                link(nc.vector.reciprocal(r[:, 5, 2:3], r[:, 5, 1:2]))
                link(nc.vector.tensor_tensor(r[:, 5, 3:4], r[:, 5, 0:1], r[:, 5, 2:3], ALU.mult))
                link(nc.vector.tensor_scalar(r[:, 9, :], r[:, 7, :], r[:, 5, 3:4], None, ALU.mult))
                link(nc.vector.scalar_tensor_tensor(out=comb[:, t, :], in0=r[:, 6, :], scalar=r[:, 5, 2:3],
                                                    in1=r[:, 9, :], op0=ALU.mult, op1=ALU.add))
            dve.wait_ge(r_rank, 1)
            for t in range(TT):
                r = rsm[:, t]
                link(nc.vector.scalar_tensor_tensor(out=r[:, 3, :], in0=bank[:, 2, t * 8:t * 8 + 8], scalar=1000.0,
                                                    in1=r[:, 8, :], op0=ALU.add, op1=ALU.mult))
                link(nc.vector.tensor_scalar(pos[:, t, 0:E], r[:, 3, :], -1000.0, None, ALU.add))
                link(nc.vector.tensor_scalar(pos[:, t, E:2 * E], r[:, 3, :], -1000.0 - SLOTS, None, ALU.add))
            q0 = slice(0, 1)
            link(nc.vector.tensor_scalar(rflag[q0, 0, :], bank[q0, 2, 16:24], float(SLOTS), None, ALU.is_gt))
            link(nc.vector.tensor_scalar(rflag[q0, 1, :], cst[q0, C_IOTA:C_IOTA + 8], -1.0, float(N_TAB), ALU.mult, ALU.add))
            link(nc.vector.tensor_tensor(rflag[q0, 2, :], rflag[q0, 0, :], rflag[q0, 1, :], ALU.mult))
            link(nc.vector.max(rflag[q0, 3, :], rflag[q0, 2, :]))
            link(nc.vector.tensor_copy(rtab[q0, 0:E], cst[q0, C_IOTA:C_IOTA + E]))
            link(nc.vector.tensor_copy(rtab[q0, N_TAB:N_TAB + E], cst[q0, C_IOTA:C_IOTA + E]))
            link(nc.vector.tensor_scalar(rtab[q0, E:N_TAB], rflag[q0, 3, :], -1.0, float(N_TAB), ALU.mult, ALU.add))
            link(nc.vector.tensor_scalar(rtab[q0, E:N_TAB], rtab[q0, E:N_TAB], float(E - 1), None, ALU.min))
            link(nc.vector.tensor_scalar(rtab[q0, N_TAB + E:2 * N_TAB], rtab[q0, E:N_TAB], float(E), None, ALU.add))
            link(nc.vector.tensor_reduce(rtab[q0, 2 * N_TAB:2 * N_TAB + 1], rflag[q0, 0, :], AX.X, ALU.add))
            link(nc.vector.tensor_scalar(rtab[q0, 2 * N_TAB:2 * N_TAB + 1], rtab[q0, 2 * N_TAB:2 * N_TAB + 1], float(E), None, ALU.add))
            nc.vector.tensor_copy(meta[q0, 0:2 * N_TAB + 1], rtab[q0, 0:2 * N_TAB + 1]).then_inc(r_meta, 1)

            def choose(w, col):
                dve.wait_ge(put_tr, w)
                for t in range(TT):
                    ins = nc.vector.tensor_scalar(pick[:, t, :], iota, pos[:, t, col], None, ALU.is_equal)
                ins.then_inc(pick_done, 1)

            def low_gathered(w):
                dve.wait_ge(gath, w * 2 + 2)
                nc.vector.tensor_copy(hg_lo[:, :, :], bank[:, 0:2, :].rearrange("p b (k n) -> p (b k) n", k=4)).then_inc(hg_lo_done, 1)

            def e_mul(n, used):
                dve.wait_ge(w_used, used)
                dve.wait_ge(e_silu, n + 1)
                dve.wait_ge(e_tr, n)
                nc.vector.tensor_tensor(eact[:, :], bank[:, 1, :], esil[:, :], ALU.mult).then_inc(e_act, 1)

            def e_low_act(n):
                dve.wait_ge(e_hi, n + 1)
                nc.vector.tensor_tensor(eaT_lo[:, :, :], bank[:, 2, :].rearrange("p (k n) -> p k n", k=4),
                                        eaT_hi[:, :, :].bitcast(F32), ALU.subtract).then_inc(e_lo, 1)

            choose(0, slice(0, 1))
            nc.vector.memset(moe[:, :, :], 0.0).then_inc(m_zero, 1)
            low_gathered(0)
            dve.wait_ge(r_meta, 1)

            def item(w, skip, e, col):
                m = w * UNITS_ITEM
                for k in range(skip, 4):
                    low(U_MOE + k, m)
                choose(w + 1, col)

                def chunk(j, up):
                    jm = m + j * 6 - 6
                    b = U_MOE + 4
                    n = w * N_EC + j
                    low(b, jm)
                    e_mul(n - 1, jm + (RING + U_MOE + up))
                    low(b + 1, jm)
                    low(b + 2, jm)
                    e_low_act(n - 1)
                    low(b + 3, jm)
                    low(b + 4, jm)
                    low(b + 5, jm)

                chunk(1, 4)
                with dve.Fori(2, N_EC) as j:
                    chunk(j, 2)
                e_mul(w * N_EC + N_EC - 1, m + (RING + U_MOE + 4 + 6 * (N_EC - 2) + 4))
                low(U_MOE + UNITS_ITEM - 2, m)
                low(U_MOE + UNITS_ITEM - 1, m)
                e_low_act(w * N_EC + N_EC - 1)
                dve.wait_ge(dn_hi_done, w + 1)
                nc.vector.tensor_tensor(dn_lo[:, :], bank[:, 4:6, :].rearrange("p b n -> p (b n)"),
                                        dn_hi[:, :].bitcast(F32), ALU.subtract).then_inc(dn_done, 1)
                low_gathered(w + 1)
                for t in range(TT):
                    dve.wait_ge(scat, w * 2 + t + 1)
                    dve.wait_ge(moe_add, w * 2 + t)
                    if t == 0 and isinstance(w, int):
                        dve.wait_ge(m_zero, 1)
                    nc.vector.scalar_tensor_tensor(out=moe[:, t, :],
                                                   in0=bank[:, (2, 4)[t]:(4, 6)[t], :].rearrange("p b n -> p (b n)"),
                                                   scalar=comb[:, t, e], in1=moe[:, t, :],
                                                   op0=ALU.mult, op1=ALU.add).then_inc(moe_add, 1)

            item(0, 3, slice(0, 1), slice(1, 2))
            passes = dve.value_load(meta[0:1, 2 * N_TAB:2 * N_TAB + 1], min_val=E, max_val=E + 3)
            with dve.Fori(1, passes) as w:
                e = dve.value_load(meta[0:1, bass.ds(w, 1)], min_val=0, max_val=E - 1)
                col = dve.value_load(meta[0:1, bass.ds(w + N_TAB + 1, 1)], min_val=0, max_val=2 * E - 1)
                item(w, 0, bass.ds(e, 1), bass.ds(col, 1))
            dve.wait_ge(moe_add, passes * 2)
            m = mods[:, 1, 2]
            for t in range(TT):
                link(nc.vector.tensor_tensor(hs[:, t, :], moe[:, t, :], m, ALU.mult))
                nc.vector.tensor_tensor(xs[:, t, :], xs[:, t, :], hs[:, t, :], ALU.add).then_inc(resid, 2)
            dve.wait_ge(row_in, 32)
            dve.wait_ge(resid, 16)
            norm(4, 0)

        @block.tensor
        def _(pe):
            mm = nc.tensor.matmul

            def ada_sum(b, more=0):
                pe.wait_ge(a_acc, ARING + b + 1 + more)
                pe.wait_ge(a_out, ARING + b + more)
                mm(bank[:, 3, (b % ARING) * AC:(b % ARING + 1) * AC], ones, ada_acc[:, b % ARING, :],
                   start=True, stop=True).then_inc(a_sum, 1)

            def turn(s):
                for i in range(4):
                    t, g = i // 2, i % 2
                    pe.wait_ge(h_ready, 2 * s + t + 1)
                    for k in range(4):
                        kt = 4 * g + k
                        ins = nc.tensor.transpose(bank[:, 4 + i, k * P:(k + 1) * P], hs[:, t, kt * P:(kt + 1) * P], ident)
                    ins.then_inc(tr_done, 1)

            def three(dst_ap, a_hi, a_lo, w_hi, w_lo, first, last):
                mm(dst_ap, a_hi, w_hi, start=first, stop=False)
                mm(dst_ap, a_hi, w_lo, start=False, stop=False)
                return mm(dst_ap, a_lo, w_hi, start=False, stop=last)

            def unit(b, nk, more=0):
                pe.wait_ge(lo_done, b + 1 + more)
                h = hi[:, b % HRING, :].rearrange("p (k n) -> p k n", k=nk)
                l = lo[:, b % RING, :].rearrange("p (k n) -> p k n", k=nk)
                return h, l

            def product(b, more, nk, k0, lhs_hi, lhs_lo, dsts, first, last):
                h, l = unit(b, nk, more)
                for t, dst_ap in enumerate(dsts):
                    for k in range(nk):
                        tok = slice(t * P, (t + 1) * P)
                        ins = three(dst_ap, lhs_hi[:, k0 + k, tok], lhs_lo[:, k0 + k, tok], h[:, k, :], l[:, k, :],
                                    first and k == 0, last and k == nk - 1)
                ins.then_inc(w_used, 1)
                return ins

            pe.wait_ge(const_in, 16)
            for v in range(V_PRE):
                ada_sum(v)
            turn(0)
            pe.wait_ge(hT_done, 4)
            PAIRS = [(0, 1), (2, 4), (5, 6)]
            with pe.Fori(0, N_IN // 3) as it:
                for k in range(6):
                    i = k // 2
                    if k % 2 == 0:
                        pe.wait_ge(proj_out, it * 3 + i + 1)
                    product(U_RET + k, it * 6, 4, 4 * (k % 2), hT_hi, hT_lo, [bank[:, PAIRS[i][t], :] for t in range(TT)],
                            k % 2 == 0, k % 2 == 1)
                    if k in (0, 1, 3, 4):
                        a = (0, 1, None, 2, 3)[k]
                        ada_sum(V_PRE + a, it * 4)

            def turn_qk(h):
                for n, bk in ((0, 4), (2, 5)):
                    if h:
                        pe.wait_ge(qT_done if n == 0 else kT_done, h)
                    for k in range(2):
                        for t in range(TT):
                            o = (h % 2) * RDK + k * P
                            ins = nc.tensor.transpose(bank[:, bk, k * SEQ + t * P:k * SEQ + (t + 1) * P],
                                                      proj[:, n + h // 2, t, o:o + P], ident)
                    ins.then_inc(qk_tr, 1)

            def scores(h):
                pe.wait_ge(qT_done, h + 1)
                pe.wait_ge(kT_done, h + 1)
                if h:
                    pe.wait_ge(s_done, h)
                for jt in range(TT):
                    for k in range(2):
                        ins = mm(bank[:, 6, jt * SEQ:(jt + 1) * SEQ], rkT[:, h % 2, k, jt * P:(jt + 1) * P],
                                 rqT[:, h % 2, k, :], start=(k == 0), stop=(k == 1))
                ins.then_inc(sc_done, 1)

            def values(h):
                pe.wait_ge(s_done, h + 1)
                if h:
                    pe.wait_ge(st_done, 2 * h)
                    pe.wait_ge(yraw_done, 2 * h)
                for t in range(TT):
                    for jt in range(TT):
                        ins = mm(bank[:, (7, 2)[t], :], dec[:, h % 2, jt * SEQ + t * P:jt * SEQ + (t + 1) * P],
                                 proj[:, 4 + h, jt, :], start=(jt == 0), stop=(jt == TT - 1))
                    ins.then_inc(y_done, 1)

            pe.wait_ge(rope_done, 1)
            pe.wait_ge(proj_out, 3 + N_IN)
            turn_qk(0)
            for h in range(RH):
                scores(h)
                if h + 1 < RH:
                    turn_qk(h + 1)
                values(h)
            for i in range(8):
                h, t = i // 2, i % 2
                pe.wait_ge(gated, i + 1)
                if i >= 4:
                    pe.wait_ge(yT_done, i - 3)
                for k in range(4):
                    ins = nc.tensor.transpose(bank[:, 4 + i % 4, k * P:(k + 1) * P], proj[:, 8 + h, t, k * P:(k + 1) * P], ident)
                ins.then_inc(y_tr, 1)
            pe.wait_ge(yT_done, 8)
            v = V_PRE + V_IN
            OUT = [(0, 1), (6, 7)]
            for k in range(8):
                n, kg = k // 4, k % 4
                ins = product(U_ROUT + k, 0, 4, 4 * kg, yT_hi, yT_lo, [bank[:, OUT[n][t], :] for t in range(TT)],
                              kg == 0, kg == 3)
                ada_sum(v + k)

            V0 = V_PRE + V_IN + V_FIN
            turn(1)
            pe.wait_ge(hT_done, 8)

            def f_gate_up(b, more, cc):
                pe.wait_ge(f_act, cc)
                for j in range(2):
                    product(b + j, more, 8, 0, hT_hi, hT_lo, [bank[:, j, t * FCH:(t + 1) * FCH] for t in range(TT)], True, True)

            def f_turn(cc):
                pe.wait_ge(f_act, cc + 1)
                for k in range(2):
                    for t in range(TT):
                        ins = nc.tensor.transpose(bank[:, 2, k * SEQ + t * P:k * SEQ + (t + 1) * P],
                                                  fact[:, t, k * P:(k + 1) * P], ident)
                ins.then_inc(f_tr, 1)

            def f_down(b, more, cc, first, last):
                pe.wait_ge(f_lo, cc + 1)
                h, l = unit(b, 2, more)
                for t in range(TT):
                    for n in range(2):
                        for k in range(2):
                            tok, cols = slice(t * P, (t + 1) * P), slice(n * CB, (n + 1) * CB)
                            ins = three(bank[:, 4 + 2 * t + n, :], faT_hi[:, k, tok], faT_lo[:, k, tok],
                                        h[:, k, cols], l[:, k, cols], first and k == 0, last and k == 1)
                ins.then_inc(w_used, 1)

            f_gate_up(U_FF, 0, 0)
            ada_sum(V0)
            ada_sum(V0 + 1)
            f_turn(0)
            def f_chunk(b, more, cc, first, a, am):
                f_gate_up(b, more, cc)
                f_down(b + 2, more, cc - 1, first, False)
                ada_sum(a, am)
                f_turn(cc)

            f_chunk(U_FF + 2, 0, 1, True, V0 + 2, 0)
            f_chunk(U_FF + 5, 0, 2, False, V0 + 3, 0)
            with pe.Fori(1, (N_FF - 1) // 2) as it:
                for q in range(2):
                    f_chunk(U_FF + 2 + 3 * q, it * 6, it * 2 + 1 + q, False, V0 + 2 + q, it * 2)
            f_down(U_QKV - 1, 0, N_FF - 1, False, True)

            V1 = V0 + V_A
            turn(2)
            pe.wait_ge(hT_done, 12)
            a = 0
            for k in range(6):
                n, kg = k // 2, k % 2
                product(U_QKV + k, 0, 4, 4 * kg, hT_hi, hT_lo, [bank[:, PAIRS[n][t], :] for t in range(TT)],
                        kg == 0, kg == 1)
                for _ in range(2 if k < 2 else 1):
                    ada_sum(V1 + a)
                    a += 1
            for i in range(5):
                if i == 0:
                    pe.wait_ge(arope, 2)
                    pe.wait_ge(qkv_out, 3)
                if i >= 2:
                    pe.wait_ge(aq_out, i - 1)
                for k in range(2):
                    for t in range(TT):
                        hd = 2 * i + k
                        ins = nc.tensor.transpose(bank[:, (4, 5)[i % 2], k * SEQ + t * P:k * SEQ + (t + 1) * P],
                                                  qkv[:, t, hd * AHD:(hd + 1) * AHD], ident)
                ins.then_inc(aq_tr, 1)
            pe.wait_ge(aq_out, 5)

            def a_scores(h):
                if h >= 2:
                    pe.wait_ge(at_exp, 2 * h - 2)
                for t in range(TT):
                    ins = mm(bank[:, 4 + h % 2, t * SEQ:(t + 1) * SEQ], aqT[:, h, t * P:(t + 1) * P],
                             akT[:, h // (AH // AKV), :], start=True, stop=True)
                ins.then_inc(at_sc, 1)

            def a_turn(h):
                pe.wait_ge(at_norm, 2 * h + 2)
                if h >= 2:
                    pe.wait_ge(at_pT, h - 1)
                for k in range(TT):
                    for t in range(TT):
                        ins = nc.tensor.transpose(bank[:, 6 + h % 2, k * SEQ + t * P:k * SEQ + (t + 1) * P],
                                                  prob[:, h % 2, t, k * P:(k + 1) * P], ident)
                ins.then_inc(at_tr, 1)

            def a_values(h):
                pe.wait_ge(at_pT, h + 1)
                if h >= 2:
                    pe.wait_ge(o_lo, h - 1)
                vo = (AH + AKV + h // (AH // AKV)) * AHD
                for k in range(TT):
                    ins = mm(bank[:, h % 2, 0:SEQ], qkv[:, k, vo:vo + AHD], probT[:, h % 2, k, :],
                             start=(k == 0), stop=(k == TT - 1))
                ins.then_inc(at_o, 1)

            for h in range(AH + 2):
                if h < AH:
                    a_scores(h)
                if 1 <= h <= AH:
                    a_turn(h - 1)
                if h >= 2:
                    a_values(h - 2)
            pe.wait_ge(o_lo, AH)
            for k in range(4):
                n, kg = k // 2, k % 2
                product(U_AOUT + k, 0, 4, 4 * kg, oT_hi, oT_lo, [bank[:, OUT[n][t], :] for t in range(TT)],
                        kg == 0, kg == 1)
            for k in range(4):
                ada_sum(V1 + a)
                a += 1

            turn(3)
            pe.wait_ge(hT_done, 16)
            pe.wait_ge(r_w, 2)
            for t in range(TT):
                tok = slice(t * P, (t + 1) * P)
                for k in range(KT):
                    three(bank[:, t, 0:E], hT_hi[:, k, tok], hT_lo[:, k, tok], wr_hi[:, k, :], wr_lo[:, k, :], k == 0, False)
                    ins = mm(bank[:, t, 0:E], hT_lo[:, k, tok], wr_lo[:, k, :], start=False, stop=(k == KT - 1))
            ins.then_inc(r_mm, 1)
            pe.wait_ge(r_sel, 1)
            mm(bank[:, 2, 0:8], tri, rsm[:, 0, 8, :], start=True, stop=True)
            mm(bank[:, 2, 8:16], tri, rsm[:, 1, 8, :], start=True, stop=False)
            mm(bank[:, 2, 8:16], ones, rsm[:, 0, 8, :], start=False, stop=True)
            mm(bank[:, 2, 16:24], ones, rsm[:, 0, 8, :], start=True, stop=False)
            mm(bank[:, 2, 16:24], ones, rsm[:, 1, 8, :], start=False, stop=True).then_inc(r_rank, 1)

            def gather(w):
                pe.wait_ge(pick_done, w + 1)
                pe.wait_ge(put_done, w)
                for part, b0 in ((hh, 6), (hl, 0)):
                    for k in range(KT):
                        for t in range(TT):
                            ins = mm(bank[:, b0 + k // 4, (k % 4) * P:(k % 4 + 1) * P], part[:, t, k * P:(k + 1) * P],
                                     pick[:, t, :], start=(t == 0), stop=(t == TT - 1))
                    ins.then_inc(gath, 1)

            def turn_pick(w):
                pe.wait_ge(hg_hi_done, w + 1)
                for t in range(TT):
                    ins = nc.tensor.transpose(bank[:, 6, t * P:(t + 1) * P], pick[:, t, :].bitcast(F32), ident)
                ins.then_inc(put_tr, 1)

            def e_gate_up(b, more, n):
                pe.wait_ge(e_act, n)
                for j in range(2):
                    for g in range(2):
                        h, l = unit(b + 2 * j + g, 4, more)
                        for k in range(4):
                            ins = three(bank[:, j, :], hg_hi[:, 4 * g + k, :], hg_lo[:, 4 * g + k, :], h[:, k, :], l[:, k, :],
                                        g == 0 and k == 0, g == 1 and k == 3)
                        ins.then_inc(w_used, 1)

            def e_turn(n):
                pe.wait_ge(e_act, n + 1)
                for k in range(4):
                    ins = nc.tensor.transpose(bank[:, 2, k * P:(k + 1) * P], eact[:, k * P:(k + 1) * P], ident)
                ins.then_inc(e_tr, 1)

            def e_down_step(b, more, n, first, last):
                pe.wait_ge(e_lo, n + 1)
                for g in range(2):
                    h, l = unit(b + g, 2, more)
                    for c2 in range(2):
                        for k in range(2):
                            cols = slice(c2 * CB, (c2 + 1) * CB)
                            ins = three(bank[:, 4 + c2, :], eaT_hi[:, 2 * g + k, :], eaT_lo[:, 2 * g + k, :], h[:, k, cols],
                                        l[:, k, cols], first and g == 0 and k == 0, last and g == 1 and k == 1)
                    ins.then_inc(w_used, 1)

            def item(w):
                m = w * UNITS_ITEM
                pe.wait_ge(hg_hi_done, w + 1)
                pe.wait_ge(hg_lo_done, w + 1)
                e_gate_up(U_MOE, m, w * N_EC)
                pe.wait_ge(moe_add, w * 2)
                e_turn(w * N_EC)
                e_gate_up(U_MOE + 4, m, w * N_EC + 1)
                e_down_step(U_MOE + 8, m, w * N_EC, True, False)
                e_turn(w * N_EC + 1)
                with pe.Fori(2, N_EC) as j:
                    jm = m + j * 6 - 6
                    e_gate_up(U_MOE + 4, jm, w * N_EC + j)
                    e_down_step(U_MOE + 8, jm, w * N_EC + j - 1, False, False)
                    e_turn(w * N_EC + j)
                e_down_step(U_MOE + UNITS_ITEM - 2, m, w * N_EC + N_EC - 1, False, True)
                gather(w + 1)
                pe.wait_ge(dn_done, w + 1)
                pe.wait_ge(put_done, w + 1)
                for t in range(TT):
                    for n in range(2):
                        cols = slice(n * CB, (n + 1) * CB)
                        mm(bank[:, (2, 4)[t] + n, :], put[:, t * P:(t + 1) * P], dn_hi[:, cols], start=True, stop=False)
                        ins = mm(bank[:, (2, 4)[t] + n, :], put[:, t * P:(t + 1) * P], dn_lo[:, cols], start=False, stop=True)
                    ins.then_inc(scat, 1)
                turn_pick(w + 1)

            pe.wait_ge(hl_done, 2)
            gather(0)
            turn_pick(0)
            item(0)
            pe.wait_ge(r_meta, 1)
            passes = pe.value_load(meta[0:1, 2 * N_TAB:2 * N_TAB + 1], min_val=E, max_val=E + 3)
            with pe.Fori(1, passes) as w:
                item(w)


_INS = ['x', 'c', 'l0_ada_w', 'l0_ada_b', 'l0_norm1_g', 'l0_norm2_g', 'l0_ret_w_in', 'l0_ret_decay_logit',
        'l0_ret_gn_g', 'l0_ret_w_out', 'l0_ffn_w_gate', 'l0_ffn_w_up', 'l0_ffn_w_down', 'l1_ada_w', 'l1_ada_b',
        'l1_norm1_g', 'l1_norm2_g', 'l1_attn_w_qkv', 'l1_attn_q_norm_g', 'l1_attn_k_norm_g', 'l1_attn_w_out',
        'l1_moe_w_router', 'l1_moe_b_router', 'l1_moe_w_gate', 'l1_moe_w_up', 'l1_moe_w_down',
        'final_ada_w', 'final_ada_b', 'final_norm_g']


def kernel(**inputs):
    import concourse.bacc as _bacc
    from concourse.bass_utils import run_bass_kernel_spmd as _run

    nc = _bacc.Bacc("TRN2", target_bir_lowering=False, num_devices=1)
    given = {name: np.ascontiguousarray(inputs[name]) for name in _INS}
    given["consts"], given["dist"] = shape_constants()
    arrays, args = {}, []
    for name, a in given.items():
        arrays[f"in_{name}"] = a
        args.append(nc.dram_tensor(f"in_{name}", a.shape, mybir.dt.from_np(a.dtype), kind="ExternalInput").ap())
    out = nc.dram_tensor("out_0", (1, SEQ, D), F32, kind="ExternalOutput").ap()
    encoder(nc, *args, out)
    r = _run(nc, [arrays], core_ids=[0])
    return r.results[0]["out_0"]
```

```python
from contextlib import ExitStack

import numpy as np

import concourse.bass as bass
from concourse import mybir

P = 128
D = 1024
SEQ = 256
TT = SEQ // P
KT = D // P
GRID_W = 64
RH, RDK, RDV = 4, 256, 512
RQK, RV = RH * RDK, RH * RDV
W_IN = 2 * RQK + 2 * RV
AH, AKV, AHD = 8, 2, 128
QKV = (AH + 2 * AKV) * AHD
FF = 2816
E = 8
FE = 3584
EPS = 1e-6
ROPE_THETA = 10000.0

F32 = mybir.dt.float32
F32R = mybir.dt.float32r
I32 = mybir.dt.int32
U32 = mybir.dt.uint32
ALU = mybir.AluOpType
ACT = mybir.ActivationFunctionType
AX = mybir.AxisListType

UW = 2048
RING = 6
HRING = 3
CB = 512
U_RET = 0
N_IN = W_IN // CB
U_ROUT = U_RET + 2 * N_IN
FCH = 256
N_FF = FF // FCH
U_FF = U_ROUT + 2 * (RV // CB)
U_QKV = U_FF + 3 * N_FF
U_AOUT = U_QKV + 2 * (QKV // CB)
U_MOE = U_AOUT + 2 * (D // CB)
ECH = 512
N_EC = FE // ECH
UNITS_ITEM = 6 * N_EC
SLOTS = 128
N_TAB = 16

AC = 256
ARING = 2
V_PRE = 8
V_IN = 16
V_FIN = 8
V_FF = 20
V_AT = 4

C_ID = 0
C_ONE = C_ID + P
C_TRI = C_ONE + P
C_IOTA = C_TRI + P
C_RC = C_IOTA + P
C_RS = C_RC + TT * 2 * 64
C_AC = C_RS + TT * 2 * 64
C_AS = C_AC + TT * 2 * 32
C_EPS = C_AS + TT * 2 * 32
C_N = C_EPS + 8


def shape_constants():
    c = np.zeros((P, C_N), np.float32)
    c[:, C_ID:C_ID + P] = np.eye(P)
    c[:, C_ONE:C_ONE + P] = 1.0
    c[:, C_TRI:C_TRI + P] = np.triu(np.ones((P, P)), 1)
    c[:, C_IOTA:C_IOTA + P] = np.arange(P)[None]
    tok = np.arange(SEQ)
    pos = [(tok // GRID_W).astype(np.float32), (tok % GRID_W).astype(np.float32)]
    for n, cc, cs in ((64, C_RC, C_RS), (32, C_AC, C_AS)):
        fr = (np.float32(ROPE_THETA) ** (-np.arange(n, dtype=np.float32) * np.float32(2.0) / np.float32(2 * n))).astype(np.float32)
        for half in range(2):
            ang = (pos[half][:, None] * fr[None]).astype(np.float32)
            for t in range(TT):
                o = (t * 2 + half) * n
                c[:, cc + o:cc + o + n] = np.cos(ang[t * P:(t + 1) * P])
                c[:, cs + o:cs + o + n] = np.sin(ang[t * P:(t + 1) * P])
    c[:, C_EPS] = EPS
    j = np.arange(P)[:, None]
    i = np.arange(SEQ)[None]
    dist = np.zeros((P, 2, TT, SEQ), np.float32)
    for jt in range(TT):
        d = i - (j + jt * P)
        dist[:, 0, jt] = np.maximum(d, 0)
        dist[:, 1, jt] = np.maximum(-d, 0)
    return c, dist.reshape(P, -1)


def encoder(nc, x, c, l0_ada_w, l0_ada_b, l0_norm1_g, l0_norm2_g, l0_ret_w_in, l0_ret_decay_logit,
            l0_ret_gn_g, l0_ret_w_out, l0_ffn_w_gate, l0_ffn_w_up, l0_ffn_w_down, l1_ada_w, l1_ada_b,
            l1_norm1_g, l1_norm2_g, l1_attn_w_qkv, l1_attn_q_norm_g, l1_attn_k_norm_g, l1_attn_w_out,
            l1_moe_w_router, l1_moe_b_router, l1_moe_w_gate, l1_moe_w_up, l1_moe_w_down,
            final_ada_w, final_ada_b, final_norm_g, consts, dist, out):
    ctx = ExitStack()
    with ctx:
        base = (nc.sbuf_base + 31) // 32 * 32
        top = [0]

        def at(name, shape, offset, dt=F32):
            return nc.alloc_sbuf_tensor_at(name, [P] + shape, dt, offset=base + 4 * offset)

        def sb(name, shape, dt=F32):
            o = top[0]
            n = int(np.prod(shape))
            top[0] = o + (n + 7) // 8 * 8
            return at(name, shape, o, dt)

        def sem(name):
            return ctx.enter_context(nc.semaphore(name))

        stage = sb("stage", [RING, UW])
        lo = at("lo", [RING, UW], 0, F32R)
        hi = sb("hi", [HRING, UW], F32R)
        ada_w = sb("ada_w", [ARING, KT, AC])
        ada_b = sb("ada_b", [ARING, AC])
        ada_acc = sb("ada_acc", [ARING, AC])
        mods = sb("mods", [2, 3, D])
        xs = sb("xs", [TT, D])
        h_at = top[0]
        hs = sb("hs", [TT, D])
        gn = at("gn", [RV], h_at)
        g_at = top[0]
        normg = sb("normg", [D])
        ropet = at("ropet", [3, 256], g_at)
        dst = at("dst", [2, TT * SEQ], g_at)
        cb1 = at("cb1", [KT, P], g_at)
        cst = sb("cst", [C_N])
        ccol = sb("ccol", [KT])
        cact = sb("cact", [KT])
        ssq = sb("ssq", [TT])
        root = sb("root", [TT])
        rstd = sb("rstd", [TT])
        declog = sb("declog", [2 * RH])
        decexp = sb("decexp", [2 * RH])
        decln = sb("decln", [2 * RH])
        gstat = sb("gstat", [8, 6])
        gmv = sb("gmv", [8, 2])
        groot = sb("groot", [8])
        grstd = sb("grstd", [8])
        pos = sb("pos", [TT, 2 * E])
        comb = sb("comb", [TT, E])
        meta = sb("meta", [2 * N_TAB + 8], I32)
        R = top[0]
        KW = 256
        hT_hi = at("hT_hi", [KT, SEQ], R, F32R)
        hT_lo = at("hT_lo", [KT, SEQ], R + 8 * KW, F32R)
        proj = at("proj", [N_IN, TT, CB], R + 16 * KW)
        dec = at("dec", [2, TT * SEQ], R + 4 * KW)
        rqT = at("rqT", [2, 2, SEQ], R + 8 * KW)
        rkT = at("rkT", [2, 2, SEQ], R + 12 * KW)
        yT_hi = at("yT_hi", [2 * KT, SEQ], R + 16 * KW, F32R)
        yT_lo = at("yT_lo", [2 * KT, SEQ], R + 32 * KW, F32R)
        cb0 = at("cb0", [KT, P], R + 60 * KW)
        finrow = at("finrow", [ARING, AC], R)
        fsil = at("fsil", [TT, FCH], R + 16 * KW)
        fact = at("fact", [TT, FCH], R + 18 * KW)
        faT_hi = at("faT_hi", [2, SEQ], R + 20 * KW, F32R)
        faT_lo = at("faT_lo", [2, SEQ], R + 22 * KW, F32R)
        oT_hi = at("oT_hi", [AH, SEQ], R, F32R)
        oT_lo = at("oT_lo", [AH, SEQ], R + 8 * KW, F32R)
        qkv = at("qkv", [TT, QKV], R + 16 * KW)
        apt = at("apt", [3, TT, 320], R + 28 * KW)
        aqT = at("aqT", [AH, SEQ], R + 36 * KW)
        akT = at("akT", [AKV, SEQ], R + 44 * KW)
        prob = at("prob", [2, TT, SEQ], R + 46 * KW)
        probT = at("probT", [2, TT, SEQ], R + 50 * KW)
        asq = at("asq", [10 * AHD], R + 54 * KW)
        again = at("again", [2, AHD], R + 59 * KW)
        ahs = at("ahs", [TT, 4, 10], R + 60 * KW)
        asm = at("asm", [AH, 4, TT], R + 61 * KW)
        hg_hi = at("hg_hi", [KT, SLOTS], R, F32R)
        hg_lo = at("hg_lo", [KT, SLOTS], R + 4 * KW, F32R)
        moe = at("moe", [TT, D], R + 8 * KW)
        hh = at("hh", [TT, D], R + 16 * KW, F32R)
        hl = at("hl", [TT, D], R + 24 * KW, F32R)
        pick = at("pick", [TT, SLOTS], R + 32 * KW, F32R)
        put = at("put", [SEQ], R + 33 * KW, F32R)
        esil = at("esil", [ECH], R + 34 * KW)
        eact = at("eact", [ECH], R + 36 * KW)
        eaT_hi = at("eaT_hi", [4, SLOTS], R + 38 * KW, F32R)
        eaT_lo = at("eaT_lo", [4, SLOTS], R + 40 * KW, F32R)
        dn_hi = at("dn_hi", [D], R + 42 * KW, F32R)
        dn_lo = at("dn_lo", [D], R + 46 * KW, F32R)
        wr = at("wr", [KT, E], R + 50 * KW)
        wr_hi = at("wr_hi", [KT, E], R + 51 * KW, F32R)
        wr_lo = at("wr_lo", [KT, E], R + 52 * KW, F32R)
        rsm = at("rsm", [TT, 10, 8], R + 53 * KW)
        ridx = at("ridx", [TT, 8], R + 54 * KW, U32)
        rtab = at("rtab", [2 * N_TAB + 8], R + 55 * KW)
        rflag = at("rflag", [4, 8], R + 56 * KW)
        brt = at("brt", [E], R + 57 * KW)
        assert base + 4 * (R + 64 * KW) <= nc.sbuf_usable_end, (base + 4 * (R + 64 * KW), nc.sbuf_usable_end)

        bank = ctx.enter_context(nc.psum_tensor("bank", [P, 8, 512], F32))
        fin_dram = nc.dram_tensor("fin_rows", [1, 2 * D], F32, kind="Internal").ap()

        ident = cst[:, C_ID:C_ID + P]
        ones = cst[:, C_ONE:C_ONE + P]
        tri = cst[:, C_TRI:C_TRI + P]
        iota = cst[:, C_IOTA:C_IOTA + P]
        eps = cst[:, C_EPS:C_EPS + 1]

        w_load = [sem(f"w_load{i}") for i in range(RING)]
        hi_done = sem("hi_done")
        lo_done = sem("lo_done")
        w_used = sem("w_used")
        a_load = [sem(f"a_load{i}") for i in range(ARING)]
        a_free = [sem(f"a_free{i}") for i in range(ARING)]
        a_acc = sem("a_acc")
        cb_done = sem("cb_done")
        a_step = sem("a_step")
        a_sum = sem("a_sum")
        a_out = sem("a_out")
        const_in = sem("const_in")
        x_in = sem("x_in")
        c_in = sem("c_in")
        g_in = sem("g_in")
        aux_in = sem("aux_in")
        c_act = sem("c_act")
        v_link = sem("v_link")
        s_link = sem("s_link")
        p_link = sem("p_link")
        b_zero = sem("b_zero")
        root_done = sem("root_done")
        scale_done = sem("scale_done")
        h_ready = sem("h_ready")
        tr_done = sem("tr_done")
        hT_hi_done = sem("hT_hi_done")
        hT_done = sem("hT_done")
        proj_out = sem("proj_out")
        rope_done = sem("rope_done")
        sg_done = sem("sg_done")
        gate_done = sem("gate_done")
        ln_done = sem("ln_done")
        arg_done = sem("arg_done")
        dec_done = sem("dec_done")
        qk_tr = sem("qk_tr")
        qT_done = sem("qT_done")
        kT_done = sem("kT_done")
        sc_done = sem("sc_done")
        s_done = sem("s_done")
        y_done = sem("y_done")
        st_done = sem("st_done")
        yraw_done = sem("yraw_done")
        mv_done = sem("mv_done")
        groot_done = sem("groot_done")
        gated = sem("gated")
        y_tr = sem("y_tr")
        yT_hi_done = sem("yT_hi_done")
        yT_done = sem("yT_done")
        resid = sem("resid")
        row_out = [sem(f"row_out{i}") for i in range(ARING)]
        row_in = sem("row_in")
        f_silu = sem("f_silu")
        f_act = sem("f_act")
        f_tr = sem("f_tr")
        f_hi = sem("f_hi")
        f_lo = sem("f_lo")
        qkv_out = sem("qkv_out")
        hsum = sem("hsum")
        hroot = sem("hroot")
        qn_done = sem("qn_done")
        arope = sem("arope")
        aq_tr = sem("aq_tr")
        aq_out = sem("aq_out")
        at_sc = sem("at_sc")
        at_max = sem("at_max")
        at_exp = sem("at_exp")
        at_norm = sem("at_norm")
        at_tr = sem("at_tr")
        at_pT = sem("at_pT")
        at_o = sem("at_o")
        o_hi = sem("o_hi")
        o_lo = sem("o_lo")
        r_in = sem("r_in")
        r_w = sem("r_w")
        r_mm = sem("r_mm")
        r_d = sem("r_d")
        r_e = sem("r_e")
        r_sel = sem("r_sel")
        r_rank = sem("r_rank")
        r_meta = sem("r_meta")
        hh_done = sem("hh_done")
        hl_done = sem("hl_done")
        m_zero = sem("m_zero")
        pick_done = sem("pick_done")
        gath = sem("gath")
        hg_hi_done = sem("hg_hi_done")
        hg_lo_done = sem("hg_lo_done")
        put_tr = sem("put_tr")
        put_done = sem("put_done")
        e_silu = sem("e_silu")
        e_act = sem("e_act")
        e_tr = sem("e_tr")
        e_hi = sem("e_hi")
        e_lo = sem("e_lo")
        dn_hi_done = sem("dn_hi_done")
        dn_done = sem("dn_done")
        scat = sem("scat")
        moe_add = sem("moe_add")
        stored = sem("stored")

        def rows(w):
            return w.rearrange("(k p) n -> p k n", p=P)

        def bcast(v, n):
            return v.partition_broadcast(P)

        w_in_v, w_out_v = rows(l0_ret_w_in), rows(l0_ret_w_out)
        fg_v, fu_v, fd_v = rows(l0_ffn_w_gate), rows(l0_ffn_w_up), rows(l0_ffn_w_down)
        qkv_v, ao_v = rows(l1_attn_w_qkv), rows(l1_attn_w_out)
        mg_v = l1_moe_w_gate.rearrange("e (k p) n -> e p k n", p=P)
        mu_v = l1_moe_w_up.rearrange("e (k p) n -> e p k n", p=P)
        md_v = l1_moe_w_down.rearrange("e (k p) n -> e p k n", p=P)

        block = ctx.enter_context(nc.Block())

        @block.sync
        def _(sp):
            sp.sem_inc(w_used, RING)
            sp.sem_inc(a_free[0], 1)
            sp.sem_inc(a_free[1], 1)
            sp.sem_inc(a_sum, ARING)
            sp.sem_inc(a_out, ARING)
            sp.sem_inc(proj_out, 3)

            def load(b, src, more=0):
                sp.wait_ge(w_used, b + more + 1)
                nk = src.shape[1]
                dst_ap = stage[:, b % RING, :].rearrange("p (k n) -> p k n", k=nk)
                for ks in (slice(0, nk // 2), slice(nk // 2, nk)):
                    sp.dma_start(dst_ap[:, ks, :], src[:, ks, :]).then_inc(w_load[b % RING], 16)

            def load_pair(b, k0, cols, more=0):
                sp.wait_ge(w_used, b + more + 1)
                dst_ap = stage[:, b % RING, :].rearrange("p (k g n) -> p k g n", k=4, g=2)
                for g, wv in enumerate((fg_v, fu_v)):
                    sp.dma_start(dst_ap[:, :, g, :], wv[:, k0:k0 + 4, cols]).then_inc(w_load[b % RING], 16)

            def load_ada(b, w, bias, col, half=0):
                sp.wait_ge(a_free[b % ARING], b // ARING + 1 + half)
                sp.dma_start(ada_w[:, b % ARING], rows(w)[:, :, bass.ds(col, AC)]).then_inc(a_load[b % ARING], 16)
                sp.dma_start(ada_b[0:1, b % ARING, :], bias.unsqueeze(0)[:, bass.ds(col, AC)]).then_inc(a_load[b % ARING], 16)

            sp.dma_start(ccol[:, :], c.rearrange("a (k p) -> p (a k)", p=P), allow_slow_non_contiguous=True).then_inc(c_in, 16)
            sp.wait_ge(b_zero, 1)
            sp.dma_start(cst[:, :], consts).then_inc(const_in, 16)
            xv = x.rearrange("a (t p) d -> p (a t) d", p=P)
            for v in range(V_PRE):
                load_ada(v, l0_ada_w, l0_ada_b, v * AC)
                if v == 3:
                    sp.dma_start(xs[:, :, :], xv).then_inc(x_in, 16)
            with sp.Fori(0, N_IN // 3) as it:
                a = 0
                for k in range(6):
                    load(U_RET + k, w_in_v[:, (k % 2) * 4:(k % 2) * 4 + 4, bass.ds(it * (3 * CB) + (k // 2) * CB, CB)], it * 6)
                    if k in (0, 1, 3, 4):
                        load_ada(V_PRE + a, l0_ada_w, l0_ada_b, it * (4 * AC) + (V_PRE + a) * AC, it * 2)
                        a += 1
            v = V_PRE + V_IN
            for k in range(8):
                n, kg = k // 4, k % 4
                load(U_ROUT + k, w_out_v[:, 4 * kg:4 * kg + 4, n * CB:(n + 1) * CB])
                load_ada(v + k, final_ada_w, final_ada_b, k * AC)
            v += V_FIN
            load_pair(U_FF, 0, slice(0, FCH))
            load_pair(U_FF + 1, 4, slice(0, FCH))
            with sp.Fori(0, (N_FF - 1) // 2) as it:
                for q in range(2):
                    b = U_FF + 2 + 3 * q
                    cols = bass.ds(it * (2 * FCH) + (q + 1) * FCH, FCH)
                    load_pair(b, 0, cols, it * 6)
                    load_pair(b + 1, 4, cols, it * 6)
                    load(b + 2, fd_v[:, bass.ds(it * 4 + 2 * q, 2), :], it * 6)
                    for a in range(2 * q, 2 * q + 2):
                        load_ada(v + a, l1_ada_w, l1_ada_b, it * (4 * AC) + a * AC, it * 2)
            load(U_QKV - 1, fd_v[:, 2 * (N_FF - 1):2 * N_FF, :])
            v += V_FF
            for k in range(6):
                n, kg = k // 2, k % 2
                load(U_QKV + k, qkv_v[:, 4 * kg:4 * kg + 4, n * CB:(n + 1) * CB])
            for a in range(2):
                load_ada(v + a, l1_ada_w, l1_ada_b, (V_FF + a) * AC)
            for k in range(4):
                n, kg = k // 2, k % 2
                load(U_AOUT + k, ao_v[:, 4 * kg:4 * kg + 4, n * CB:(n + 1) * CB])
            for a in range(2, 4):
                load_ada(v + a, l1_ada_w, l1_ada_b, (V_FF + a) * AC)

            def load_gate_up(e, b, col, more):
                for m, wv in ((0, mg_v), (2, mu_v)):
                    for g in range(2):
                        load(b + m + g, wv[e, :, 4 * g:4 * g + 4, col] if isinstance(e, int) else
                             wv[bass.ds(e, 1), :, 4 * g:4 * g + 4, col].rearrange("a p k n -> p (a k) n"), more)

            def load_down(e, b, kt, more):
                for g in range(2):
                    ks = bass.ds(kt + 2 * g, 2)
                    load(b + g, md_v[e, :, ks, :] if isinstance(e, int) else
                         md_v[bass.ds(e, 1), :, ks, :].rearrange("a p k n -> p (a k) n"), more)

            def item(e, more):
                load_gate_up(e, U_MOE, slice(0, ECH), more)
                with sp.Fori(1, N_EC) as j:
                    jm = j * 6 - 6
                    load_gate_up(e, U_MOE + 4, bass.ds(j * ECH, ECH), more + jm)
                    load_down(e, U_MOE + 8, j * 4 - 4, more + jm)
                load_down(e, U_MOE + UNITS_ITEM - 2, 4 * (N_EC - 1), more)

            item(0, 0)
            sp.wait_ge(r_meta, 1)
            passes = sp.value_load(meta[0:1, 2 * N_TAB:2 * N_TAB + 1], min_val=E, max_val=E + 3)
            with sp.Fori(1, passes) as w:
                e = sp.value_load(meta[0:1, bass.ds(w, 1)], min_val=0, max_val=E - 1)
                item(e, w * UNITS_ITEM)
            sp.wait_ge(stored, 32)

        @block.gpsimd
        def _(pool):
            nc.gpsimd.memset(ada_b[:, :, :], 0.0).then_inc(b_zero, 1)
            n_link = [0]

            def link(ins):
                n_link[0] += 1
                ins.then_inc(p_link, 1)
                pool.wait_ge(p_link, n_link[0])

            def repeat_c(dst_ap):
                for k in range(KT):
                    ins = nc.gpsimd.tensor_scalar(dst_ap[:, k, :], ones, cact[:, k:k + 1], None, ALU.mult)
                ins.then_inc(cb_done, 1)

            pool.dma_start(normg[:, :], l0_norm1_g.partition_broadcast(P)).then_inc(g_in, 16)
            pool.wait_ge(const_in, 16)
            pool.wait_ge(c_act, 1)
            repeat_c(cb0)
            pool.dma_start(declog[:, :], l0_ret_decay_logit.rearrange("a b -> (a b)").partition_broadcast(P)).then_inc(aux_in, 16)
            pool.wait_ge(tr_done, 4)
            pool.dma_start(gn[:, :], l0_ret_gn_g.partition_broadcast(P)).then_inc(aux_in, 16)

            def rotate(x1, x2, co, si, shape, tmp, last):
                ta, tb, tc = (t.rearrange(shape[0], **shape[1]) for t in tmp)
                nc.gpsimd.tensor_tensor(ta, x1, co, ALU.mult)
                nc.gpsimd.tensor_tensor(tb, x2, si, ALU.mult)
                nc.gpsimd.tensor_tensor(tc, x1, si, ALU.mult)
                link(nc.gpsimd.tensor_tensor(x2, x2, co, ALU.mult))
                nc.gpsimd.tensor_tensor(x1, ta, tb, ALU.subtract)
                ins = nc.gpsimd.tensor_tensor(x2, x2, tc, ALU.add)
                link(ins)

            pool.wait_ge(scale_done, 1)
            for q in range(4):
                pool.wait_ge(proj_out, 3 + q + 1)
                for t in range(TT):
                    v = proj[:, q, t, :].rearrange("p (h f s i) -> p h f s i", h=2, f=2, s=2)
                    for f in range(2):
                        co = cst[:, C_RC + (t * 2 + f) * 64:C_RC + (t * 2 + f + 1) * 64].unsqueeze(1).to_broadcast([P, 2, 64])
                        si = cst[:, C_RS + (t * 2 + f) * 64:C_RS + (t * 2 + f + 1) * 64].unsqueeze(1).to_broadcast([P, 2, 64])
                        rotate(v[:, :, f, 0, :], v[:, :, f, 1, :], co, si, ("p (h i) -> p h i", dict(h=2)),
                               [ropet[:, i, 0:128] for i in range(3)], False)
            pool.nop().then_inc(rope_done, 1)
            pool.dma_start(dst[:, :, :], dist.rearrange("p (s n) -> p s n", s=2)).then_inc(aux_in, 16)
            pool.wait_ge(aux_in, 48)
            for h in range(RH):
                pool.wait_ge(sg_done, h + 1)
                for t in range(TT):
                    g = proj[:, 8 + h, t, :]
                    nc.gpsimd.tensor_tensor(g, g, gn[:, h * RDV:(h + 1) * RDV], ALU.mult).then_inc(gate_done, 1)
            pool.wait_ge(arg_done, RH)
            pool.dma_start(normg[:, :], l0_norm2_g.partition_broadcast(P)).then_inc(g_in, 16)
            pool.wait_ge(scale_done, 2)
            pool.dma_start(normg[:, :], l1_norm1_g.partition_broadcast(P)).then_inc(g_in, 16)
            pool.wait_ge(scale_done, 3)
            pool.dma_start(again[:, 0, :], l1_attn_q_norm_g.partition_broadcast(P)).then_inc(aux_in, 16)
            pool.dma_start(again[:, 1, :], l1_attn_k_norm_g.partition_broadcast(P)).then_inc(aux_in, 16)
            repeat_c(cb1)
            for t in range(TT):
                pool.wait_ge(qn_done, t + 1)
                v = qkv[:, t, 0:10 * AHD].rearrange("p (h f s i) -> p h f s i", h=10, f=2, s=2)
                for f in range(2):
                    co = cst[:, C_AC + (t * 2 + f) * 32:C_AC + (t * 2 + f + 1) * 32].unsqueeze(1).to_broadcast([P, 10, 32])
                    si = cst[:, C_AS + (t * 2 + f) * 32:C_AS + (t * 2 + f + 1) * 32].unsqueeze(1).to_broadcast([P, 10, 32])
                    rotate(v[:, :, f, 0, :], v[:, :, f, 1, :], co, si, ("p (h i) -> p h i", dict(h=10)),
                           [apt[:, i, t, :] for i in range(3)], False)
                pool.nop().then_inc(arope, 1)
            pool.wait_ge(a_sum, ARING + V_PRE + V_IN + V_FIN + V_FF + V_AT)
            pool.dma_start(normg[:, :], l1_norm2_g.partition_broadcast(P)).then_inc(g_in, 16)
            pool.wait_ge(resid, 3 * 4)
            pool.dma_start(wr[:, :, :], l1_moe_w_router.rearrange("(k p) e -> p k e", p=P)).then_inc(r_in, 16)
            pool.dma_start(brt[:, :], l1_moe_b_router.partition_broadcast(P)).then_inc(r_in, 16)
            for r in row_out:
                pool.wait_ge(r, 16 * V_FIN // ARING)
            pool.dma_start(mods[:, 0, 0, :], fin_dram[0, 0:D].partition_broadcast(P)).then_inc(row_in, 16)
            pool.dma_start(mods[:, 0, 1, :], fin_dram[0, D:2 * D].partition_broadcast(P)).then_inc(row_in, 16)
            pool.wait_ge(scale_done, 4)
            pool.dma_start(normg[:, :], final_norm_g.partition_broadcast(P)).then_inc(g_in, 16)

        @block.scalar
        def _(act):
            n_link = [0]

            def link(ins):
                n_link[0] += 1
                ins.then_inc(s_link, 1)
                act.wait_ge(s_link, n_link[0])

            def high(b, more=0, occ=0):
                act.wait_ge(w_load[b % RING], 32 * (b // RING + 1) + occ * 32)
                act.wait_ge(w_used, RING + b - HRING + 1 + more)
                nc.scalar.copy(hi[:, b % HRING, :], stage[:, b % RING, :]).then_inc(hi_done, 1)

            def ada_take(b, dst_ap, more=0):
                act.wait_ge(a_sum, ARING + b + 1 + more)
                nc.scalar.copy(dst_ap, bank[:, 3, (b % ARING) * AC:(b % ARING + 1) * AC]).then_inc(a_out, 1)

            def mod_at(col):
                return mods[:, :, :, :].rearrange("p a b d -> p (a b d)")[:, bass.ds(col, AC)]

            def norm(s, after=(0, 0)):
                for t in range(TT):
                    if after[t]:
                        act.wait_ge(resid, after[t])
                    nc.scalar.activation(hs[:, t, :], xs[:, t, :], ACT.Square, accum_out=ssq[:, t:t + 1]).then_inc(s_link, 1)
                n_link[0] += TT
                for t in range(TT):
                    act.wait_ge(s_link, n_link[0] - TT + 1 + t)
                    nc.scalar.activation(root[:, t:t + 1], ssq[:, t:t + 1], ACT.Sqrt, scale=1.0 / D, bias=eps).then_inc(root_done, 1)

            def high_T(s):
                for i in range(4):
                    act.wait_ge(tr_done, 4 * s + i + 1)
                    t, g = i // 2, i % 2
                    nc.scalar.copy(hT_hi[:, 4 * g:4 * g + 4, t * P:(t + 1) * P],
                                   bank[:, 4 + i, :].rearrange("p (k n) -> p k n", k=4)).then_inc(hT_hi_done, 1)

            act.wait_ge(c_in, 16)
            nc.scalar.activation(cact[:, :], ccol[:, :], ACT.Silu).then_inc(c_act, 1)
            for v in range(V_PRE):
                ada_take(v, mod_at(v * AC))
            act.wait_ge(x_in, 16)
            act.wait_ge(const_in, 16)
            norm(0)
            for k in range(3):
                high(U_RET + k)
            high_T(0)

            PAIRS = [(0, 1), (2, 4), (5, 6)]

            def take_chunk(i, cc):
                act.wait_ge(w_used, RING + U_RET + 2 + cc * 2)
                for t in range(TT):
                    ins = nc.scalar.copy(
                        proj[:, :, :, :].rearrange("p c t n -> p (c t n)")[:, bass.ds(cc * (TT * CB) + t * CB, CB)],
                        bank[:, PAIRS[i][t], :])
                ins.then_inc(proj_out, 1)

            def in_body(it, first, skip=0):
                for k in range(skip, 6):
                    high(U_RET + k, it * 6, it)
                    in_after(it, k, first)

            def in_after(it, k, first):
                if k == 0 and not first:
                    ada_take(V_PRE + 2, mod_at(it * (4 * AC) - 4 * AC + (V_PRE + 2) * AC), it * 4 - 4)
                    take_chunk(1, it * 3 - 2)
                if k == 1 and not first:
                    ada_take(V_PRE + 3, mod_at(it * (4 * AC) - 4 * AC + (V_PRE + 3) * AC), it * 4 - 4)
                if k == 2 and not first:
                    take_chunk(2, it * 3 - 1)
                if k == 3:
                    ada_take(V_PRE, mod_at(it * (4 * AC) + V_PRE * AC), it * 4)
                if k == 4:
                    ada_take(V_PRE + 1, mod_at(it * (4 * AC) + (V_PRE + 1) * AC), it * 4)
                    take_chunk(0, it * 3)

            act.wait_ge(aux_in, 32)
            link(nc.scalar.activation(decexp[:, :], declog[:, :], ACT.Exp, scale=-1.0))
            nc.scalar.activation(decln[:, :], decexp[:, :], ACT.Ln, bias=1.0).then_inc(ln_done, 1)
            in_body(0, True, 3)
            with act.Fori(1, N_IN // 3) as it:
                in_body(it, False)
            last = N_IN // 3
            for k in range(3):
                high(U_ROUT + k)
                in_after(last, k, False)


            def q_take(h):
                act.wait_ge(qk_tr, 2 * h + 1)
                if h >= 2:
                    act.wait_ge(sc_done, h - 1)
                nc.scalar.copy(rqT[:, h % 2], bank[:, 4, :].rearrange("p (k n) -> p k n", k=2)).then_inc(qT_done, 1)

            def decay(h):
                act.wait_ge(arg_done, h + 1)
                nc.scalar.activation(dec[:, h % 2], dec[:, h % 2], ACT.Exp, scale=-1.0).then_inc(dec_done, 1)

            q_take(0)
            decay(0)
            decay(1)
            for h in range(RH):
                g = proj[:, 8 + h, :, :]
                if h == 0:
                    act.wait_ge(proj_out, 3 + N_IN)
                nc.scalar.activation(g, g, ACT.Silu).then_inc(sg_done, 1)
            q_take(1)

            def y_take(h):
                act.wait_ge(y_done, 2 * h + 2)
                act.wait_ge(st_done, 2 * h + 2)
                for t in range(TT):
                    nc.scalar.copy(proj[:, 4 + h, t, :], bank[:, (7, 2)[t], :]).then_inc(yraw_done, 1)

            for h in range(RH):
                y_take(h)
                if h + 2 < RH:
                    decay(h + 2)
                    q_take(h + 2)
            act.wait_ge(mv_done, 1)
            nc.scalar.activation(groot[:, :], gmv[:, :, 1], ACT.Sqrt, bias=eps).then_inc(groot_done, 1)
            for i in range(8):
                act.wait_ge(y_tr, i + 1)
                h, t = i // 2, i % 2
                nc.scalar.copy(yT_hi[:, 4 * h:4 * h + 4, t * P:(t + 1) * P],
                               bank[:, 4 + i % 4, :].rearrange("p (k n) -> p k n", k=4)).then_inc(yT_hi_done, 1)
            def fin_take(a):
                v = V_PRE + V_IN + a
                if a >= ARING:
                    act.wait_ge(row_out[a % ARING], 16 * (a // ARING))
                ada_take(v, finrow[:, v % ARING, :])
                act.wait_ge(a_out, ARING + v + 1)
                act.dma_start(fin_dram[0:1, a * AC:(a + 1) * AC], finrow[0:1, v % ARING, :]).then_inc(row_out[a % ARING], 16)

            for k in range(3, 8):
                high(U_ROUT + k)
                fin_take(k - 3)
            for a in range(5, 8):
                fin_take(a)
            for r in row_out:
                act.wait_ge(r, 16 * V_FIN // ARING)

            norm(1, (3, 4))
            high(U_FF)
            high(U_FF + 1)
            high_T(1)
            V0 = V_PRE + V_IN + V_FIN

            def f_silu_step(cc):
                act.wait_ge(w_used, RING + U_FF + 2 if isinstance(cc, int) and cc == 0 else cc * 3 + (RING + U_FF + 1))
                act.wait_ge(f_act, cc)
                nc.scalar.activation(fsil[:, :, :], bank[:, 0:2, 0:FCH], ACT.Silu).then_inc(f_silu, 1)

            def f_high_act(cc):
                act.wait_ge(f_tr, cc + 1)
                nc.scalar.copy(faT_hi[:, :, :], bank[:, 2, :].rearrange("p (k n) -> p k n", k=2)).then_inc(f_hi, 1)

            def take_pair(col, more):
                act.wait_ge(a_sum, ARING + V0 + 2 + more)
                nc.scalar.copy(mods[:, :, :, :].rearrange("p a b d -> p (a b d)")[:, bass.ds(col, 2 * AC)],
                               bank[:, 3, :]).then_inc(a_out, 2)

            def f_chunk(it, q, pair):
                b = U_FF + 2 + 3 * q
                cc = it * 2 + 1 + q
                high(b, it * 6, it)
                f_silu_step(cc - 1)
                high(b + 1, it * 6, it)
                if pair:
                    take_pair(it * (4 * AC) + (2 * q - 2) * AC, it * 4 + (2 * q - 2))
                f_high_act(cc - 1)
                high(b + 2, it * 6, it)

            f_chunk(0, 0, False)
            f_chunk(0, 1, True)
            with act.Fori(1, (N_FF - 1) // 2) as it:
                f_chunk(it, 0, True)
                f_chunk(it, 1, True)
            f_silu_step(N_FF - 1)
            high(U_QKV - 1)
            take_pair((V_FF - 2) * AC, V_FF - 2)
            f_high_act(N_FF - 1)

            norm(2, (6, 8))
            high(U_QKV)
            high(U_QKV + 1)
            high_T(2)
            high(U_QKV + 2)
            V1 = V0 + V_FF

            def qkv_take(n):
                act.wait_ge(w_used, RING + U_QKV + 2 * n + 2)
                for t in range(TT):
                    ins = nc.scalar.copy(qkv[:, t, n * CB:(n + 1) * CB], bank[:, PAIRS[n][t], :])
                ins.then_inc(qkv_out, 1)

            for k in range(3, 6):
                high(U_QKV + k)
                if k == 4:
                    qkv_take(0)
            high(U_AOUT)
            qkv_take(1)
            high(U_AOUT + 1)
            qkv_take(2)
            for t in range(TT):
                act.wait_ge(hsum, t + 1)
                nc.scalar.activation(ahs[:, t, 1, :], ahs[:, t, 0, :], ACT.Sqrt, scale=1.0 / AHD, bias=eps).then_inc(hroot, 1)
            high(U_AOUT + 2)
            for a in range(V_AT):
                ada_take(V1 + a, mod_at((V_FF + a) * AC))
            for i in range(5):
                act.wait_ge(aq_tr, i + 1)
                dst_ap = (aqT[:, 2 * i:2 * i + 2, :] if i < 4 else akT[:, :, :])
                nc.scalar.copy(dst_ap, bank[:, (4, 5)[i % 2], :].rearrange("p (k n) -> p k n", k=2)).then_inc(aq_out, 1)

            def soft(h):
                act.wait_ge(at_max, h + 1)
                if h >= 2:
                    act.wait_ge(at_tr, h - 1)
                for t in range(TT):
                    ins = nc.scalar.activation(prob[:, h % 2, t, :], bank[:, 4 + h % 2, t * SEQ:(t + 1) * SEQ], ACT.Exp,
                                               bias=asm[:, h, 1, t:t + 1], scale=float(AHD) ** -0.5,
                                               accum_out=asm[:, h, 2, t:t + 1])
                    ins.then_inc(at_exp, 1)

            def pT_take(h):
                act.wait_ge(at_tr, h + 1)
                if h >= 2:
                    act.wait_ge(at_o, h - 1)
                nc.scalar.copy(probT[:, h % 2], bank[:, 6 + h % 2, :].rearrange("p (k n) -> p k n", k=2)).then_inc(at_pT, 1)

            def o_take(h):
                act.wait_ge(at_o, h + 1)
                nc.scalar.copy(oT_hi[:, h, :], bank[:, h % 2, 0:SEQ]).then_inc(o_hi, 1)

            for h in range(AH + 2):
                if h < AH:
                    soft(h)
                if 1 <= h <= AH:
                    pT_take(h - 1)
                if h >= 2:
                    o_take(h - 2)
            high(U_AOUT + 3)

            norm(3, (11, 12))
            for k in range(3):
                high(U_MOE + k)
            high_T(3)
            act.wait_ge(r_in, 32)
            nc.scalar.copy(wr_hi[:, :, :], wr[:, :, :]).then_inc(r_w, 1)
            for t in range(TT):
                nc.scalar.copy(hh[:, t, :], hs[:, t, :]).then_inc(hh_done, 1)
            act.wait_ge(r_d, 1)
            nc.scalar.activation(rsm[:, :, 5, 0:1], rsm[:, :, 4, 0:1], ACT.Exp).then_inc(r_e, 1)

            def take_gathered(w):
                act.wait_ge(gath, w * 2 + 1)
                nc.scalar.copy(hg_hi[:, :, :], bank[:, 6:8, :].rearrange("p b (k n) -> p (b k) n", k=4)).then_inc(hg_hi_done, 1)

            def take_put(w):
                act.wait_ge(put_tr, w + 1)
                nc.scalar.copy(put[:, :], bank[:, 6, 0:SEQ]).then_inc(put_done, 1)

            def e_silu_step(n, used):
                act.wait_ge(w_used, used)
                act.wait_ge(e_act, n)
                nc.scalar.activation(esil[:, :], bank[:, 0, :], ACT.Silu).then_inc(e_silu, 1)

            def e_high_act(n):
                act.wait_ge(e_tr, n + 1)
                nc.scalar.copy(eaT_hi[:, :, :], bank[:, 2, :].rearrange("p (k n) -> p k n", k=4)).then_inc(e_hi, 1)

            def take_down(n):
                act.wait_ge(w_used, n * UNITS_ITEM + (RING + U_MOE))
                nc.scalar.copy(dn_hi[:, :], bank[:, 4:6, :].rearrange("p b n -> p (b n)")).then_inc(dn_hi_done, 1)

            def item(w, first):
                m, o = w * UNITS_ITEM, w * N_EC
                if first:
                    take_gathered(0)
                else:
                    high(U_MOE, m, o)
                    high(U_MOE + 1, m, o)
                    take_down(w)
                    high(U_MOE + 2, m, o)
                high(U_MOE + 3, m, o)
                take_put(w)
                e_silu_step(w * N_EC, m + (RING + U_MOE + 2))
                with act.Fori(1, N_EC) as j:
                    jm, jo = m + j * 6 - 6, o + j - 1
                    b = U_MOE + 4
                    n = w * N_EC + j
                    high(b, jm, jo)
                    high(b + 1, jm, jo)
                    high(b + 2, jm, jo)
                    e_high_act(n - 1)
                    high(b + 3, jm, jo)
                    high(b + 4, jm, jo)
                    e_silu_step(n, jm + (RING + U_MOE + 6))
                    high(b + 5, jm, jo)
                high(U_MOE + UNITS_ITEM - 2, m, o)
                e_high_act(w * N_EC + N_EC - 1)
                high(U_MOE + UNITS_ITEM - 1, m, o)
                take_gathered(w + 1)

            item(0, True)
            passes = act.value_load(meta[0:1, 2 * N_TAB:2 * N_TAB + 1], min_val=E, max_val=E + 3)
            with act.Fori(1, passes) as w:
                item(w, False)
            take_down(passes)
            norm(4, (14, 16))
            ov = out.rearrange("a (t p) d -> p (a t) d", p=P)
            for t in range(TT):
                act.wait_ge(h_ready, 2 * 4 + t + 1)
                act.dma_start(ov[:, t, :], hs[:, t, :]).then_inc(stored, 16)
            act.wait_ge(stored, 32)

        @block.vector
        def _(dve):
            n_link = [0]

            def link(ins):
                n_link[0] += 1
                ins.then_inc(v_link, 1)
                dve.wait_ge(v_link, n_link[0])

            def low(b, more=0):
                dve.wait_ge(hi_done, b + 1 + more)
                nc.vector.tensor_tensor(lo[:, b % RING, :], stage[:, b % RING, :],
                                        hi[:, b % HRING, :].bitcast(F32), ALU.subtract).then_inc(lo_done, 1)

            def ada(b, n, half=0):
                more = half * ARING
                s = b % ARING
                dve.wait_ge(a_load[s], 32 * (b // ARING + 1) + half * 32)
                dve.wait_ge(a_sum, b + 1 + more)
                for k in range(KT):
                    prev = ada_b[:, s, :] if k == 0 else ada_acc[:, s, :]
                    ins = nc.vector.scalar_tensor_tensor(out=ada_acc[:, s, :], in0=ada_w[:, s, k, :],
                                                         scalar=cact[:, k:k + 1], in1=prev,
                                                         op0=ALU.mult, op1=ALU.add)
                    if k < KT - 1:
                        ins.then_inc(a_step, 1)
                        dve.wait_ge(a_step, (KT - 1) * n + k + 1 + more * (KT - 1))
                    else:
                        ins.then_inc(a_acc, 1)
                dve.wait_ge(a_acc, n + 1 + more)
                dve.sem_inc(a_free[s], 1)

            def norm(s, took):
                m = mods[:, s % 2]
                dve.wait_ge(g_in, 16 * (s + 1))
                if took:
                    dve.wait_ge(a_out, ARING + took)
                nc.vector.scalar_tensor_tensor(out=m[:, 1, :], in0=m[:, 1, :], scalar=1.0, in1=normg[:, :],
                                               op0=ALU.add, op1=ALU.mult).then_inc(scale_done, 1)
                dve.wait_ge(scale_done, s + 1)
                for t in range(TT):
                    dve.wait_ge(root_done, 2 * s + t + 1)
                    link(nc.vector.reciprocal(rstd[:, t:t + 1], root[:, t:t + 1]))
                    link(nc.vector.scalar_tensor_tensor(out=hs[:, t, :], in0=xs[:, t, :], scalar=rstd[:, t:t + 1],
                                                        in1=m[:, 1, :], op0=ALU.mult, op1=ALU.mult))
                    nc.vector.tensor_tensor(hs[:, t, :], hs[:, t, :], m[:, 0, :], ALU.add).then_inc(h_ready, 1)

            def low_T(s):
                for i in range(4):
                    dve.wait_ge(hT_hi_done, 4 * s + i + 1)
                    t, g = i // 2, i % 2
                    nc.vector.tensor_tensor(hT_lo[:, 4 * g:4 * g + 4, t * P:(t + 1) * P],
                                            bank[:, 4 + i, :].rearrange("p (k n) -> p k n", k=4),
                                            hT_hi[:, 4 * g:4 * g + 4, t * P:(t + 1) * P].bitcast(F32),
                                            ALU.subtract).then_inc(hT_done, 1)

            def residual(s, order, used):
                m = mods[:, s % 2, 2]
                for (n, t, src), u in zip(order, used):
                    cols = slice(n * CB, (n + 1) * CB)
                    dve.wait_ge(w_used, RING + u)
                    link(nc.vector.tensor_tensor(hs[:, t, cols], src, m[:, cols], ALU.mult))
                    nc.vector.tensor_tensor(xs[:, t, cols], xs[:, t, cols], hs[:, t, cols], ALU.add).then_inc(resid, 1)

            dve.wait_ge(c_act, 1)
            for v in range(0, V_PRE, 2):
                ada(v, v // 2)
            dve.wait_ge(x_in, 16)
            norm(0, V_PRE)
            low(U_RET)
            low_T(0)
            def in_step(it, k):
                if k:
                    low(U_RET + k, it * 6)
                if k in (0, 1, 3, 4):
                    a = (0, 1, None, 2, 3)[k]
                    ada(V_PRE + a, V_PRE // 2 + a, it * 2)

            for k in range(6):
                in_step(0, k)
            with dve.Fori(1, N_IN // 3) as it:
                low(U_RET, it * 6)
                for k in range(6):
                    in_step(it, k)

            def decay_arg(h):
                b = h % 2
                link(nc.vector.tensor_scalar(dec[:, b], dst[:, 0], decln[:, h:h + 1], None, ALU.mult))
                nc.vector.scalar_tensor_tensor(out=dec[:, b], in0=dst[:, 1], scalar=decln[:, RH + h:RH + h + 1],
                                               in1=dec[:, b], op0=ALU.mult, op1=ALU.add).then_inc(arg_done, 1)

            def k_take(h):
                dve.wait_ge(qk_tr, 2 * h + 2)
                if h >= 2:
                    dve.wait_ge(sc_done, h - 1)
                nc.vector.tensor_copy(rkT[:, h % 2], bank[:, 5, :].rearrange("p (k n) -> p k n", k=2)).then_inc(kT_done, 1)

            dve.wait_ge(ln_done, 1)
            dve.wait_ge(aux_in, 48)
            dve.wait_ge(w_used, RING + U_ROUT)
            decay_arg(0)
            k_take(0)
            decay_arg(1)
            low(U_ROUT)
            k_take(1)
            for h in range(RH):
                dve.wait_ge(sc_done, h + 1)
                dve.wait_ge(dec_done, h + 1)
                nc.vector.scalar_tensor_tensor(out=dec[:, h % 2], in0=bank[:, 6, :], scalar=float(RDK) ** -0.5,
                                               in1=dec[:, h % 2], op0=ALU.mult, op1=ALU.mult).then_inc(s_done, 1)
                for t in range(TT):
                    dve.wait_ge(y_done, 2 * h + t + 1)
                    nc.vector.bn_stats(gstat[:, 2 * h + t, :], bank[:, (7, 2)[t], :]).then_inc(st_done, 1)
                if h + 2 < RH:
                    decay_arg(h + 2)
                    low(U_ROUT + 1 + h)
                    k_take(h + 2)
            dve.wait_ge(st_done, 2 * RH)
            for i in range(8):
                ins = nc.vector.bn_aggr(gmv[:, i, :], gstat[:, i, :])
            ins.then_inc(mv_done, 1)
            dve.wait_ge(groot_done, 1)
            link(nc.vector.reciprocal(grstd[:, :], groot[:, :]))
            dve.wait_ge(yraw_done, 2 * RH)
            dve.wait_ge(gate_done, 2 * RH)

            def gate(i):
                h, t = i // 2, i % 2
                y, g = proj[:, 4 + h, t, :], proj[:, 8 + h, t, :]
                link(nc.vector.tensor_scalar(y, y, gmv[:, i, 0:1], grstd[:, i:i + 1], ALU.subtract, ALU.mult))
                nc.vector.tensor_tensor(g, y, g, ALU.mult).then_inc(gated, 1)

            def low_y(i):
                dve.wait_ge(yT_hi_done, i + 1)
                dve.wait_ge(gated, 2 * (i // 2) + 2)
                h, t = i // 2, i % 2
                nc.vector.tensor_tensor(yT_lo[:, 4 * h:4 * h + 4, t * P:(t + 1) * P],
                                        bank[:, 4 + i % 4, :].rearrange("p (k n) -> p k n", k=4),
                                        yT_hi[:, 4 * h:4 * h + 4, t * P:(t + 1) * P].bitcast(F32),
                                        ALU.subtract).then_inc(yT_done, 1)

            gate(0)
            gate(1)
            for i in range(8):
                if i + 2 < 8:
                    gate(i + 2)
                low_y(i)
            v = V_PRE + V_IN
            for k in range(8):
                if k >= 3:
                    low(U_ROUT + k)
                ada(v + k, V_PRE // 2 + V_IN + k)
            residual(0, [(0, 0, bank[:, 0, :]), (0, 1, bank[:, 1, :]), (1, 0, bank[:, 6, :]), (1, 1, bank[:, 7, :])],
                     [U_FF - 4] * 2 + [U_FF] * 2)

            V0 = V_PRE + V_IN + V_FIN
            norm(1, V_PRE + V_IN)
            low(U_FF)
            low_T(1)

            def f_mul(cc):
                dve.wait_ge(f_silu, cc + 1)
                dve.wait_ge(f_tr, cc)
                nc.vector.tensor_tensor(fact[:, :, :], bank[:, 0:2, FCH:2 * FCH], fsil[:, :, :], ALU.mult).then_inc(f_act, 1)

            def f_low_act(cc):
                dve.wait_ge(f_hi, cc + 1)
                nc.vector.tensor_tensor(faT_lo[:, :, :], bank[:, 2, :].rearrange("p (k n) -> p k n", k=2),
                                        faT_hi[:, :, :].bitcast(F32), ALU.subtract).then_inc(f_lo, 1)

            low(U_FF + 1)
            N0 = V_PRE // 2 + V_IN + V_FIN

            def f_pair(it):
                for q in range(2):
                    b = U_FF + 2 + 3 * q
                    cc = it * 2 + 1 + q
                    low(b, it * 6)
                    f_mul(cc - 1)
                    low(b + 1, it * 6)
                    f_low_act(cc - 1)
                    low(b + 2, it * 6)
                    for a in range(2 * q, 2 * q + 2):
                        ada(V0 + a, N0 + a, it * 2)

            f_pair(0)
            with dve.Fori(1, (N_FF - 1) // 2) as it:
                f_pair(it)
            f_mul(N_FF - 1)
            low(U_QKV - 1)
            f_low_act(N_FF - 1)
            residual(1, [(0, 0, bank[:, 4, :]), (1, 0, bank[:, 5, :]), (0, 1, bank[:, 6, :]), (1, 1, bank[:, 7, :])],
                     [U_QKV] * 4)

            V1 = V0 + V_FF
            norm(2, V1)
            low(U_QKV)
            low_T(2)
            for k in range(1, 6):
                low(U_QKV + k)
            low(U_AOUT)
            dve.wait_ge(qkv_out, 3)
            dve.wait_ge(aux_in, 80)
            for t in range(TT):
                qk = qkv[:, t, 0:10 * AHD]
                qh = qk.rearrange("p (h d) -> p h d", h=10)
                link(nc.vector.tensor_tensor(asq[:, :], qk, qk, ALU.mult))
                nc.vector.tensor_reduce(ahs[:, t, 0, :], asq[:, :].rearrange("p (h d) -> p h d", h=10), AX.X,
                                        ALU.add).then_inc(hsum, 1)
                for n, o, m in ((0, 0, AH), (1, AH, AKV)):
                    ins = nc.vector.tensor_tensor(qh[:, o:o + m, :], qh[:, o:o + m, :],
                                                  again[:, n, :].unsqueeze(1).to_broadcast([P, m, AHD]), ALU.mult)
                    ins.then_inc(v_link, 1)
                    n_link[0] += 1
                dve.wait_ge(hroot, t + 1)
                link(nc.vector.reciprocal(ahs[:, t, 2, :], ahs[:, t, 1, :]))
                nc.vector.tensor_tensor(qh, qh, ahs[:, t, 2, :].unsqueeze(2).to_broadcast([P, 10, AHD]),
                                        ALU.mult).then_inc(qn_done, 1)
            low(U_AOUT + 1)
            low(U_AOUT + 2)

            def row_max(h):
                dve.wait_ge(at_sc, h + 1)
                link(nc.vector.tensor_reduce(asm[:, h, 0, :], bank[:, 4 + h % 2, :].rearrange("p (t n) -> p t n", t=TT),
                                             AX.X, ALU.max))
                nc.vector.tensor_scalar(asm[:, h, 1, :], asm[:, h, 0, :], -float(AHD) ** -0.5, None,
                                        ALU.mult).then_inc(at_max, 1)

            def row_norm(h):
                dve.wait_ge(at_exp, 2 * h + 2)
                link(nc.vector.reciprocal(asm[:, h, 3, :], asm[:, h, 2, :]))
                for t in range(TT):
                    p = prob[:, h % 2, t, :]
                    nc.vector.tensor_scalar(p, p, asm[:, h, 3, t:t + 1], None, ALU.mult).then_inc(at_norm, 1)

            def o_low(h):
                dve.wait_ge(o_hi, h + 1)
                nc.vector.tensor_tensor(oT_lo[:, h, :], bank[:, h % 2, 0:SEQ], oT_hi[:, h, :].bitcast(F32),
                                        ALU.subtract).then_inc(o_lo, 1)

            for h in range(AH + 2):
                if h < AH:
                    row_max(h)
                    row_norm(h)
                if h >= 2:
                    o_low(h - 2)
            low(U_AOUT + 3)
            residual(2, [(0, 0, bank[:, 0, :]), (0, 1, bank[:, 1, :]), (1, 0, bank[:, 6, :]), (1, 1, bank[:, 7, :])],
                     [U_MOE - 2] * 2 + [U_MOE] * 2)

            norm(3, V1 + V_AT)
            low(U_MOE)
            low_T(3)
            dve.wait_ge(r_w, 1)
            nc.vector.tensor_tensor(wr_lo[:, :, :], wr[:, :, :], wr_hi[:, :, :].bitcast(F32), ALU.subtract).then_inc(r_w, 1)
            for k in range(1, 3):
                low(U_MOE + k)
            for t in range(TT):
                dve.wait_ge(hh_done, t + 1)
                nc.vector.tensor_tensor(hl[:, t, :], hs[:, t, :], hh[:, t, :].bitcast(F32), ALU.subtract).then_inc(hl_done, 1)
            io8 = iota[:, 0:8]
            dve.wait_ge(r_mm, 1)
            for t in range(TT):
                r = rsm[:, t]
                link(nc.vector.tensor_tensor(r[:, 0, :], bank[:, t, 0:E], brt[:, :], ALU.add))
                link(nc.vector.max(r[:, 1, :], r[:, 0, :]))
                link(nc.vector.max_index(ridx[:, t, :], r[:, 1, :], r[:, 0, :]))
                link(nc.vector.tensor_copy(r[:, 2, :], ridx[:, t, :]))
                nc.vector.tensor_scalar(r[:, 6, :], io8, r[:, 2, 0:1], None, ALU.is_equal)
                nc.vector.tensor_scalar(r[:, 7, :], io8, r[:, 2, 1:2], None, ALU.is_equal)
                link(nc.vector.tensor_tensor(r[:, 4, 0:1], r[:, 1, 1:2], r[:, 1, 0:1], ALU.subtract))
            nc.vector.nop().then_inc(r_d, 1)
            for t in range(TT):
                link(nc.vector.tensor_tensor(rsm[:, t, 8, :], rsm[:, t, 6, :], rsm[:, t, 7, :], ALU.add))
            dve.nop().then_inc(r_sel, 1)
            dve.wait_ge(r_e, 1)
            for t in range(TT):
                r = rsm[:, t]
                link(nc.vector.tensor_scalar(r[:, 5, 1:2], r[:, 5, 0:1], 1.0, None, ALU.add))
                link(nc.vector.reciprocal(r[:, 5, 2:3], r[:, 5, 1:2]))
                link(nc.vector.tensor_tensor(r[:, 5, 3:4], r[:, 5, 0:1], r[:, 5, 2:3], ALU.mult))
                link(nc.vector.tensor_scalar(r[:, 9, :], r[:, 7, :], r[:, 5, 3:4], None, ALU.mult))
                link(nc.vector.scalar_tensor_tensor(out=comb[:, t, :], in0=r[:, 6, :], scalar=r[:, 5, 2:3],
                                                    in1=r[:, 9, :], op0=ALU.mult, op1=ALU.add))
            dve.wait_ge(r_rank, 1)
            for t in range(TT):
                r = rsm[:, t]
                link(nc.vector.scalar_tensor_tensor(out=r[:, 3, :], in0=bank[:, 2, t * 8:t * 8 + 8], scalar=1000.0,
                                                    in1=r[:, 8, :], op0=ALU.add, op1=ALU.mult))
                link(nc.vector.tensor_scalar(pos[:, t, 0:E], r[:, 3, :], -1000.0, None, ALU.add))
                link(nc.vector.tensor_scalar(pos[:, t, E:2 * E], r[:, 3, :], -1000.0 - SLOTS, None, ALU.add))
            q0 = slice(0, 1)
            link(nc.vector.tensor_scalar(rflag[q0, 0, :], bank[q0, 2, 16:24], float(SLOTS), None, ALU.is_gt))
            link(nc.vector.tensor_scalar(rflag[q0, 1, :], cst[q0, C_IOTA:C_IOTA + 8], -1.0, float(N_TAB), ALU.mult, ALU.add))
            link(nc.vector.tensor_tensor(rflag[q0, 2, :], rflag[q0, 0, :], rflag[q0, 1, :], ALU.mult))
            link(nc.vector.max(rflag[q0, 3, :], rflag[q0, 2, :]))
            link(nc.vector.tensor_copy(rtab[q0, 0:E], cst[q0, C_IOTA:C_IOTA + E]))
            link(nc.vector.tensor_copy(rtab[q0, N_TAB:N_TAB + E], cst[q0, C_IOTA:C_IOTA + E]))
            link(nc.vector.tensor_scalar(rtab[q0, E:N_TAB], rflag[q0, 3, :], -1.0, float(N_TAB), ALU.mult, ALU.add))
            link(nc.vector.tensor_scalar(rtab[q0, E:N_TAB], rtab[q0, E:N_TAB], float(E - 1), None, ALU.min))
            link(nc.vector.tensor_scalar(rtab[q0, N_TAB + E:2 * N_TAB], rtab[q0, E:N_TAB], float(E), None, ALU.add))
            link(nc.vector.tensor_reduce(rtab[q0, 2 * N_TAB:2 * N_TAB + 1], rflag[q0, 0, :], AX.X, ALU.add))
            link(nc.vector.tensor_scalar(rtab[q0, 2 * N_TAB:2 * N_TAB + 1], rtab[q0, 2 * N_TAB:2 * N_TAB + 1], float(E), None, ALU.add))
            nc.vector.tensor_copy(meta[q0, 0:2 * N_TAB + 1], rtab[q0, 0:2 * N_TAB + 1]).then_inc(r_meta, 1)

            def choose(w, col):
                dve.wait_ge(put_tr, w)
                for t in range(TT):
                    ins = nc.vector.tensor_scalar(pick[:, t, :], iota, pos[:, t, col], None, ALU.is_equal)
                ins.then_inc(pick_done, 1)

            def low_gathered(w):
                dve.wait_ge(gath, w * 2 + 2)
                nc.vector.tensor_copy(hg_lo[:, :, :], bank[:, 0:2, :].rearrange("p b (k n) -> p (b k) n", k=4)).then_inc(hg_lo_done, 1)

            def e_mul(n, used):
                dve.wait_ge(w_used, used)
                dve.wait_ge(e_silu, n + 1)
                dve.wait_ge(e_tr, n)
                nc.vector.tensor_tensor(eact[:, :], bank[:, 1, :], esil[:, :], ALU.mult).then_inc(e_act, 1)

            def e_low_act(n):
                dve.wait_ge(e_hi, n + 1)
                nc.vector.tensor_tensor(eaT_lo[:, :, :], bank[:, 2, :].rearrange("p (k n) -> p k n", k=4),
                                        eaT_hi[:, :, :].bitcast(F32), ALU.subtract).then_inc(e_lo, 1)

            choose(0, slice(0, 1))
            nc.vector.memset(moe[:, :, :], 0.0).then_inc(m_zero, 1)
            low_gathered(0)
            dve.wait_ge(r_meta, 1)

            def low_down(n):
                dve.wait_ge(dn_hi_done, n)
                nc.vector.tensor_tensor(dn_lo[:, :], bank[:, 4:6, :].rearrange("p b n -> p (b n)"),
                                        dn_hi[:, :].bitcast(F32), ALU.subtract).then_inc(dn_done, 1)

            def add(scats, e):
                dve.wait_ge(m_zero, 1)
                for t in range(TT):
                    dve.wait_ge(scat, scats[t])
                    nc.vector.scalar_tensor_tensor(out=moe[:, t, :],
                                                   in0=bank[:, (2, 4)[t]:(4, 6)[t], :].rearrange("p b n -> p (b n)"),
                                                   scalar=comb[:, t, e], in1=moe[:, t, :],
                                                   op0=ALU.mult, op1=ALU.add).then_inc(moe_add, 1)

            def item(w, first, before, col):
                m = w * UNITS_ITEM
                if not first:
                    low(U_MOE, m)
                    low(U_MOE + 1, m)
                    low_down(w)
                    low(U_MOE + 2, m)
                low(U_MOE + 3, m)
                if not first:
                    add((w * 2 - 1, w * 2), before)
                choose(w + 1, col)

                def chunk(j, up):
                    jm = m + j * 6 - 6
                    b = U_MOE + 4
                    n = w * N_EC + j
                    low(b, jm)
                    e_mul(n - 1, jm + (RING + U_MOE + up))
                    low(b + 1, jm)
                    low(b + 2, jm)
                    e_low_act(n - 1)
                    low(b + 3, jm)
                    low(b + 4, jm)
                    low(b + 5, jm)

                chunk(1, 4)
                with dve.Fori(2, N_EC) as j:
                    chunk(j, 2)
                e_mul(w * N_EC + N_EC - 1, m + (RING + U_MOE + 4 + 6 * (N_EC - 2) + 4))
                low(U_MOE + UNITS_ITEM - 2, m)
                e_low_act(w * N_EC + N_EC - 1)
                low(U_MOE + UNITS_ITEM - 1, m)
                low_gathered(w + 1)

            item(0, True, None, slice(1, 2))
            passes = dve.value_load(meta[0:1, 2 * N_TAB:2 * N_TAB + 1], min_val=E, max_val=E + 3)
            with dve.Fori(1, passes) as w:
                before = dve.value_load(meta[0:1, bass.ds(w - 1, 1)], min_val=0, max_val=E - 1)
                col = dve.value_load(meta[0:1, bass.ds(w + N_TAB + 1, 1)], min_val=0, max_val=2 * E - 1)
                item(w, False, bass.ds(before, 1), bass.ds(col, 1))
            low_down(passes)
            last = dve.value_load(meta[0:1, bass.ds(passes - 1, 1)], min_val=0, max_val=E - 1)
            add((passes * 2, passes * 2), bass.ds(last, 1))
            dve.wait_ge(moe_add, passes * 2)
            m = mods[:, 1, 2]
            for t in range(TT):
                link(nc.vector.tensor_tensor(hs[:, t, :], moe[:, t, :], m, ALU.mult))
                nc.vector.tensor_tensor(xs[:, t, :], xs[:, t, :], hs[:, t, :], ALU.add).then_inc(resid, 2)
            dve.wait_ge(row_in, 32)
            dve.wait_ge(resid, 16)
            norm(4, 0)

        @block.tensor
        def _(pe):
            mm = nc.tensor.matmul

            def ada_whole(b, cb):
                s = b % ARING
                pe.wait_ge(a_load[s], 32 * (b // ARING + 1))
                pe.wait_ge(a_out, ARING + b)
                dst_ap = bank[:, 3, s * AC:(s + 1) * AC]
                mm(dst_ap, ones, ada_b[:, s, :], start=True, stop=False)
                for k in range(KT):
                    ins = mm(dst_ap, cb[:, k, :], ada_w[:, s, k, :], start=False, stop=(k == KT - 1))
                ins.then_inc(a_sum, 1)
                pe.wait_ge(a_sum, ARING + b + 1)
                pe.sem_inc(a_free[s], 1)

            def ada_sum(b, n, more=0):
                pe.wait_ge(a_acc, n + 1 + more)
                pe.wait_ge(a_out, ARING + b + more)
                mm(bank[:, 3, (b % ARING) * AC:(b % ARING + 1) * AC], ones, ada_acc[:, b % ARING, :],
                   start=True, stop=True).then_inc(a_sum, 1)

            def turn(s):
                for i in range(4):
                    t, g = i // 2, i % 2
                    pe.wait_ge(h_ready, 2 * s + t + 1)
                    for k in range(4):
                        kt = 4 * g + k
                        ins = nc.tensor.transpose(bank[:, 4 + i, k * P:(k + 1) * P], hs[:, t, kt * P:(kt + 1) * P], ident)
                    ins.then_inc(tr_done, 1)

            def three(dst_ap, a_hi, a_lo, w_hi, w_lo, first, last):
                mm(dst_ap, a_hi, w_hi, start=first, stop=False)
                mm(dst_ap, a_hi, w_lo, start=False, stop=False)
                return mm(dst_ap, a_lo, w_hi, start=False, stop=last)

            def unit(b, nk, more=0):
                pe.wait_ge(lo_done, b + 1 + more)
                h = hi[:, b % HRING, :].rearrange("p (k n) -> p k n", k=nk)
                l = lo[:, b % RING, :].rearrange("p (k n) -> p k n", k=nk)
                return h, l

            def product(b, more, nk, k0, lhs_hi, lhs_lo, dsts, first, last):
                h, l = unit(b, nk, more)
                for t, dst_ap in enumerate(dsts):
                    for k in range(nk):
                        tok = slice(t * P, (t + 1) * P)
                        ins = three(dst_ap, lhs_hi[:, k0 + k, tok], lhs_lo[:, k0 + k, tok], h[:, k, :], l[:, k, :],
                                    first and k == 0, last and k == nk - 1)
                ins.then_inc(w_used, 1)
                return ins

            pe.wait_ge(const_in, 16)
            pe.wait_ge(cb_done, 1)
            for v in range(V_PRE):
                if v % 2:
                    ada_whole(v, cb0)
                else:
                    ada_sum(v, v // 2)
            turn(0)
            pe.wait_ge(hT_done, 4)
            PAIRS = [(0, 1), (2, 4), (5, 6)]
            with pe.Fori(0, N_IN // 3) as it:
                for k in range(6):
                    i = k // 2
                    if k % 2 == 0:
                        pe.wait_ge(proj_out, it * 3 + i + 1)
                    product(U_RET + k, it * 6, 4, 4 * (k % 2), hT_hi, hT_lo, [bank[:, PAIRS[i][t], :] for t in range(TT)],
                            k % 2 == 0, k % 2 == 1)
                    if k in (0, 1, 3, 4):
                        a = (0, 1, None, 2, 3)[k]
                        ada_sum(V_PRE + a, V_PRE // 2 + a, it * 4)

            def turn_qk(h):
                for n, bk in ((0, 4), (2, 5)):
                    if h:
                        pe.wait_ge(qT_done if n == 0 else kT_done, h)
                    for k in range(2):
                        for t in range(TT):
                            o = (h % 2) * RDK + k * P
                            ins = nc.tensor.transpose(bank[:, bk, k * SEQ + t * P:k * SEQ + (t + 1) * P],
                                                      proj[:, n + h // 2, t, o:o + P], ident)
                    ins.then_inc(qk_tr, 1)

            def scores(h):
                pe.wait_ge(qT_done, h + 1)
                pe.wait_ge(kT_done, h + 1)
                if h:
                    pe.wait_ge(s_done, h)
                for jt in range(TT):
                    for k in range(2):
                        ins = mm(bank[:, 6, jt * SEQ:(jt + 1) * SEQ], rkT[:, h % 2, k, jt * P:(jt + 1) * P],
                                 rqT[:, h % 2, k, :], start=(k == 0), stop=(k == 1))
                ins.then_inc(sc_done, 1)

            def values(h):
                pe.wait_ge(s_done, h + 1)
                if h:
                    pe.wait_ge(st_done, 2 * h)
                    pe.wait_ge(yraw_done, 2 * h)
                for t in range(TT):
                    for jt in range(TT):
                        ins = mm(bank[:, (7, 2)[t], :], dec[:, h % 2, jt * SEQ + t * P:jt * SEQ + (t + 1) * P],
                                 proj[:, 4 + h, jt, :], start=(jt == 0), stop=(jt == TT - 1))
                    ins.then_inc(y_done, 1)

            pe.wait_ge(rope_done, 1)
            pe.wait_ge(proj_out, 3 + N_IN)
            turn_qk(0)
            for h in range(RH):
                scores(h)
                if h + 1 < RH:
                    turn_qk(h + 1)
                values(h)
            for i in range(8):
                h, t = i // 2, i % 2
                pe.wait_ge(gated, i + 1)
                if i >= 4:
                    pe.wait_ge(yT_done, i - 3)
                for k in range(4):
                    ins = nc.tensor.transpose(bank[:, 4 + i % 4, k * P:(k + 1) * P], proj[:, 8 + h, t, k * P:(k + 1) * P], ident)
                ins.then_inc(y_tr, 1)
            pe.wait_ge(yT_done, 8)
            v = V_PRE + V_IN
            OUT = [(0, 1), (6, 7)]
            for k in range(8):
                n, kg = k // 4, k % 4
                ins = product(U_ROUT + k, 0, 4, 4 * kg, yT_hi, yT_lo, [bank[:, OUT[n][t], :] for t in range(TT)],
                              kg == 0, kg == 3)
                ada_sum(v + k, V_PRE // 2 + V_IN + k)

            V0 = V_PRE + V_IN + V_FIN
            turn(1)
            pe.wait_ge(hT_done, 8)

            def f_gate_up(b, more, cc):
                pe.wait_ge(f_act, cc)
                for j in range(2):
                    product(b + j, more, 4, 4 * j, hT_hi, hT_lo, [bank[:, t, :] for t in range(TT)], j == 0, j == 1)

            def f_turn(cc):
                pe.wait_ge(f_act, cc + 1)
                for k in range(2):
                    for t in range(TT):
                        ins = nc.tensor.transpose(bank[:, 2, k * SEQ + t * P:k * SEQ + (t + 1) * P],
                                                  fact[:, t, k * P:(k + 1) * P], ident)
                ins.then_inc(f_tr, 1)

            def f_down(b, more, cc, first, last):
                pe.wait_ge(f_lo, cc + 1)
                h, l = unit(b, 2, more)
                for t in range(TT):
                    for n in range(2):
                        for k in range(2):
                            tok, cols = slice(t * P, (t + 1) * P), slice(n * CB, (n + 1) * CB)
                            ins = three(bank[:, 4 + 2 * t + n, :], faT_hi[:, k, tok], faT_lo[:, k, tok],
                                        h[:, k, cols], l[:, k, cols], first and k == 0, last and k == 1)
                ins.then_inc(w_used, 1)

            def sum_pair(more):
                pe.wait_ge(a_acc, N0 + 2 + more)
                pe.wait_ge(a_out, ARING + V0 + more)
                mm(bank[:, 3, 0:AC], ones, ada_acc[:, 0, :], start=True, stop=True)
                mm(bank[:, 3, AC:2 * AC], ones, ada_acc[:, 1, :], start=True, stop=True).then_inc(a_sum, 2)

            N0 = V_PRE // 2 + V_IN + V_FIN
            f_gate_up(U_FF, 0, 0)
            f_turn(0)
            def f_chunk(b, more, cc, first, a):
                f_gate_up(b, more, cc)
                f_down(b + 2, more, cc - 1, first, False)
                sum_pair(a)
                f_turn(cc)

            f_chunk(U_FF + 2, 0, 1, True, 0)
            f_chunk(U_FF + 5, 0, 2, False, 2)
            with pe.Fori(1, (N_FF - 1) // 2) as it:
                for q in range(2):
                    f_chunk(U_FF + 2 + 3 * q, it * 6, it * 2 + 1 + q, False, it * 4 + 2 * q)
            f_down(U_QKV - 1, 0, N_FF - 1, False, True)

            V1 = V0 + V_FF
            turn(2)
            pe.wait_ge(hT_done, 12)
            for k in range(6):
                n, kg = k // 2, k % 2
                product(U_QKV + k, 0, 4, 4 * kg, hT_hi, hT_lo, [bank[:, PAIRS[n][t], :] for t in range(TT)],
                        kg == 0, kg == 1)
            pe.wait_ge(cb_done, 2)
            for a in range(V_AT):
                ada_whole(V1 + a, cb1)
            for i in range(5):
                if i == 0:
                    pe.wait_ge(arope, 2)
                    pe.wait_ge(qkv_out, 3)
                if i >= 2:
                    pe.wait_ge(aq_out, i - 1)
                for k in range(2):
                    for t in range(TT):
                        hd = 2 * i + k
                        ins = nc.tensor.transpose(bank[:, (4, 5)[i % 2], k * SEQ + t * P:k * SEQ + (t + 1) * P],
                                                  qkv[:, t, hd * AHD:(hd + 1) * AHD], ident)
                ins.then_inc(aq_tr, 1)
            pe.wait_ge(aq_out, 5)

            def a_scores(h):
                if h >= 2:
                    pe.wait_ge(at_exp, 2 * h - 2)
                for t in range(TT):
                    ins = mm(bank[:, 4 + h % 2, t * SEQ:(t + 1) * SEQ], aqT[:, h, t * P:(t + 1) * P],
                             akT[:, h // (AH // AKV), :], start=True, stop=True)
                ins.then_inc(at_sc, 1)

            def a_turn(h):
                pe.wait_ge(at_norm, 2 * h + 2)
                if h >= 2:
                    pe.wait_ge(at_pT, h - 1)
                for k in range(TT):
                    for t in range(TT):
                        ins = nc.tensor.transpose(bank[:, 6 + h % 2, k * SEQ + t * P:k * SEQ + (t + 1) * P],
                                                  prob[:, h % 2, t, k * P:(k + 1) * P], ident)
                ins.then_inc(at_tr, 1)

            def a_values(h):
                pe.wait_ge(at_pT, h + 1)
                if h >= 2:
                    pe.wait_ge(o_lo, h - 1)
                vo = (AH + AKV + h // (AH // AKV)) * AHD
                for k in range(TT):
                    ins = mm(bank[:, h % 2, 0:SEQ], qkv[:, k, vo:vo + AHD], probT[:, h % 2, k, :],
                             start=(k == 0), stop=(k == TT - 1))
                ins.then_inc(at_o, 1)

            for h in range(AH + 2):
                if h < AH:
                    a_scores(h)
                if 1 <= h <= AH:
                    a_turn(h - 1)
                if h >= 2:
                    a_values(h - 2)
            pe.wait_ge(o_lo, AH)
            for k in range(4):
                n, kg = k // 2, k % 2
                product(U_AOUT + k, 0, 4, 4 * kg, oT_hi, oT_lo, [bank[:, OUT[n][t], :] for t in range(TT)],
                        kg == 0, kg == 1)

            turn(3)
            pe.wait_ge(hT_done, 16)
            pe.wait_ge(r_w, 2)
            for t in range(TT):
                tok = slice(t * P, (t + 1) * P)
                for k in range(KT):
                    three(bank[:, t, 0:E], hT_hi[:, k, tok], hT_lo[:, k, tok], wr_hi[:, k, :], wr_lo[:, k, :], k == 0, False)
                    ins = mm(bank[:, t, 0:E], hT_lo[:, k, tok], wr_lo[:, k, :], start=False, stop=(k == KT - 1))
            ins.then_inc(r_mm, 1)
            pe.wait_ge(r_sel, 1)
            mm(bank[:, 2, 0:8], tri, rsm[:, 0, 8, :], start=True, stop=True)
            mm(bank[:, 2, 8:16], tri, rsm[:, 1, 8, :], start=True, stop=False)
            mm(bank[:, 2, 8:16], ones, rsm[:, 0, 8, :], start=False, stop=True)
            mm(bank[:, 2, 16:24], ones, rsm[:, 0, 8, :], start=True, stop=False)
            mm(bank[:, 2, 16:24], ones, rsm[:, 1, 8, :], start=False, stop=True).then_inc(r_rank, 1)

            def gather(w):
                pe.wait_ge(pick_done, w + 1)
                pe.wait_ge(put_done, w)
                for part, b0 in ((hh, 6), (hl, 0)):
                    for k in range(KT):
                        for t in range(TT):
                            ins = mm(bank[:, b0 + k // 4, (k % 4) * P:(k % 4 + 1) * P], part[:, t, k * P:(k + 1) * P],
                                     pick[:, t, :], start=(t == 0), stop=(t == TT - 1))
                    ins.then_inc(gath, 1)

            def turn_pick(w):
                pe.wait_ge(hg_hi_done, w + 1)
                for t in range(TT):
                    ins = nc.tensor.transpose(bank[:, 6, t * P:(t + 1) * P], pick[:, t, :].bitcast(F32), ident)
                ins.then_inc(put_tr, 1)

            def e_turn(n):
                pe.wait_ge(e_act, n + 1)
                for k in range(4):
                    ins = nc.tensor.transpose(bank[:, 2, k * P:(k + 1) * P], eact[:, k * P:(k + 1) * P], ident)
                ins.then_inc(e_tr, 1)

            def e_down_step(b, more, n, first, last):
                pe.wait_ge(e_lo, n + 1)
                for g in range(2):
                    h, l = unit(b + g, 2, more)
                    for c2 in range(2):
                        for k in range(2):
                            cols = slice(c2 * CB, (c2 + 1) * CB)
                            ins = three(bank[:, 4 + c2, :], eaT_hi[:, 2 * g + k, :], eaT_lo[:, 2 * g + k, :], h[:, k, cols],
                                        l[:, k, cols], first and g == 0 and k == 0, last and g == 1 and k == 1)
                    ins.then_inc(w_used, 1)

            def scatter(n):
                pe.wait_ge(dn_done, n)
                pe.wait_ge(put_done, n)
                for t in range(TT):
                    for n in range(2):
                        cols = slice(n * CB, (n + 1) * CB)
                        mm(bank[:, (2, 4)[t] + n, :], put[:, t * P:(t + 1) * P], dn_hi[:, cols], start=True, stop=False)
                        ins = mm(bank[:, (2, 4)[t] + n, :], put[:, t * P:(t + 1) * P], dn_lo[:, cols], start=False, stop=True)
                    ins.then_inc(scat, 1)

            def e_half(b, j, more):
                for g in range(2):
                    h, l = unit(b + 2 * j + g, 4, more)
                    for k in range(4):
                        ins = three(bank[:, j, :], hg_hi[:, 4 * g + k, :], hg_lo[:, 4 * g + k, :], h[:, k, :], l[:, k, :],
                                    g == 0 and k == 0, g == 1 and k == 3)
                    ins.then_inc(w_used, 1)

            def e_gate_up(b, more, n):
                pe.wait_ge(e_act, n)
                e_half(b, 0, more)
                e_half(b, 1, more)

            def item(w, first):
                m = w * UNITS_ITEM
                pe.wait_ge(hg_hi_done, w + 1)
                pe.wait_ge(hg_lo_done, w + 1)
                e_half(U_MOE, 0, m)
                if not first:
                    scatter(w)
                turn_pick(w)
                e_half(U_MOE, 1, m)
                if not first:
                    pe.wait_ge(moe_add, w * 2)
                e_turn(w * N_EC)
                e_gate_up(U_MOE + 4, m, w * N_EC + 1)
                e_down_step(U_MOE + 8, m, w * N_EC, True, False)
                e_turn(w * N_EC + 1)
                with pe.Fori(2, N_EC) as j:
                    jm = m + j * 6 - 6
                    e_gate_up(U_MOE + 4, jm, w * N_EC + j)
                    e_down_step(U_MOE + 8, jm, w * N_EC + j - 1, False, False)
                    e_turn(w * N_EC + j)
                gather(w + 1)
                e_down_step(U_MOE + UNITS_ITEM - 2, m, w * N_EC + N_EC - 1, False, True)

            pe.wait_ge(hl_done, 2)
            gather(0)
            item(0, True)
            pe.wait_ge(r_meta, 1)
            passes = pe.value_load(meta[0:1, 2 * N_TAB:2 * N_TAB + 1], min_val=E, max_val=E + 3)
            with pe.Fori(1, passes) as w:
                item(w, False)
            scatter(passes)


_INS = ['x', 'c', 'l0_ada_w', 'l0_ada_b', 'l0_norm1_g', 'l0_norm2_g', 'l0_ret_w_in', 'l0_ret_decay_logit',
        'l0_ret_gn_g', 'l0_ret_w_out', 'l0_ffn_w_gate', 'l0_ffn_w_up', 'l0_ffn_w_down', 'l1_ada_w', 'l1_ada_b',
        'l1_norm1_g', 'l1_norm2_g', 'l1_attn_w_qkv', 'l1_attn_q_norm_g', 'l1_attn_k_norm_g', 'l1_attn_w_out',
        'l1_moe_w_router', 'l1_moe_b_router', 'l1_moe_w_gate', 'l1_moe_w_up', 'l1_moe_w_down',
        'final_ada_w', 'final_ada_b', 'final_norm_g']


def kernel(**inputs):
    import concourse.bacc as _bacc
    from concourse.bass_utils import run_bass_kernel_spmd as _run

    nc = _bacc.Bacc("TRN2", target_bir_lowering=False, num_devices=1)
    given = {name: np.ascontiguousarray(inputs[name]) for name in _INS}
    given["consts"], given["dist"] = shape_constants()
    arrays, args = {}, []
    for name, a in given.items():
        arrays[f"in_{name}"] = a
        args.append(nc.dram_tensor(f"in_{name}", a.shape, mybir.dt.from_np(a.dtype), kind="ExternalInput").ap())
    out = nc.dram_tensor("out_0", (1, SEQ, D), F32, kind="ExternalOutput").ap()
    encoder(nc, *args, out)
    r = _run(nc, [arrays], core_ids=[0])
    return r.results[0]["out_0"]
```

```python
from contextlib import ExitStack

import numpy as np

import concourse.bass as bass
from concourse import mybir

P = 128
D = 1024
SEQ = 256
TT = SEQ // P
KT = D // P
GRID_W = 64
RH, RDK, RDV = 4, 256, 512
RQK, RV = RH * RDK, RH * RDV
W_IN = 2 * RQK + 2 * RV
AH, AKV, AHD = 8, 2, 128
QKV = (AH + 2 * AKV) * AHD
FF = 2816
E = 8
FE = 3584
EPS = 1e-6
ROPE_THETA = 10000.0

F32 = mybir.dt.float32
F32R = mybir.dt.float32r
I32 = mybir.dt.int32
U32 = mybir.dt.uint32
ALU = mybir.AluOpType
ACT = mybir.ActivationFunctionType
AX = mybir.AxisListType

UW = 2048
RING = 6
HRING = 3
CB = 512
U_RET = 0
N_IN = W_IN // CB
U_ROUT = U_RET + 2 * N_IN
FCH = 256
N_FF = FF // FCH
U_FF = U_ROUT + 2 * (RV // CB)
U_QKV = U_FF + 3 * N_FF
U_AOUT = U_QKV + 2 * (QKV // CB)
U_MOE = U_AOUT + 2 * (D // CB)
ECH = 512
N_EC = FE // ECH
UNITS_ITEM = 6 * N_EC
SLOTS = 128
N_TAB = 16

AC = 256
ARING = 2
V_PRE = 8
V_OWN = 6
V_IN = 16
V_FIN = 8
V_FF = 20
V_AT = 4

C_ID = 0
C_ONE = C_ID + P
C_TRI = C_ONE + P
C_IOTA = C_TRI + P
C_RC = C_IOTA + P
C_RS = C_RC + TT * 2 * 64
C_AC = C_RS + TT * 2 * 64
C_AS = C_AC + TT * 2 * 32
C_EPS = C_AS + TT * 2 * 32
C_N = C_EPS + 8


def shape_constants():
    c = np.zeros((P, C_N), np.float32)
    c[:, C_ID:C_ID + P] = np.eye(P)
    c[:, C_ONE:C_ONE + P] = 1.0
    c[:, C_TRI:C_TRI + P] = np.triu(np.ones((P, P)), 1)
    c[:, C_IOTA:C_IOTA + P] = np.arange(P)[None]
    tok = np.arange(SEQ)
    pos = [(tok // GRID_W).astype(np.float32), (tok % GRID_W).astype(np.float32)]
    for n, cc, cs in ((64, C_RC, C_RS), (32, C_AC, C_AS)):
        fr = (np.float32(ROPE_THETA) ** (-np.arange(n, dtype=np.float32) * np.float32(2.0) / np.float32(2 * n))).astype(np.float32)
        for half in range(2):
            ang = (pos[half][:, None] * fr[None]).astype(np.float32)
            for t in range(TT):
                o = (t * 2 + half) * n
                c[:, cc + o:cc + o + n] = np.cos(ang[t * P:(t + 1) * P])
                c[:, cs + o:cs + o + n] = np.sin(ang[t * P:(t + 1) * P])
    c[:, C_EPS] = EPS
    j = np.arange(P)[:, None]
    i = np.arange(SEQ)[None]
    dist = np.zeros((P, 2, TT, SEQ), np.float32)
    for jt in range(TT):
        d = i - (j + jt * P)
        dist[:, 0, jt] = np.maximum(d, 0)
        dist[:, 1, jt] = np.maximum(-d, 0)
    return c, dist.reshape(P, -1)


def encoder(nc, x, c, l0_ada_w, l0_ada_b, l0_norm1_g, l0_norm2_g, l0_ret_w_in, l0_ret_decay_logit,
            l0_ret_gn_g, l0_ret_w_out, l0_ffn_w_gate, l0_ffn_w_up, l0_ffn_w_down, l1_ada_w, l1_ada_b,
            l1_norm1_g, l1_norm2_g, l1_attn_w_qkv, l1_attn_q_norm_g, l1_attn_k_norm_g, l1_attn_w_out,
            l1_moe_w_router, l1_moe_b_router, l1_moe_w_gate, l1_moe_w_up, l1_moe_w_down,
            final_ada_w, final_ada_b, final_norm_g, consts, dist, out):
    ctx = ExitStack()
    with ctx:
        base = (nc.sbuf_base + 31) // 32 * 32
        top = [0]

        def at(name, shape, offset, dt=F32):
            return nc.alloc_sbuf_tensor_at(name, [P] + shape, dt, offset=base + 4 * offset)

        def sb(name, shape, dt=F32):
            o = top[0]
            n = int(np.prod(shape))
            top[0] = o + (n + 7) // 8 * 8
            return at(name, shape, o, dt)

        def sem(name):
            return ctx.enter_context(nc.semaphore(name))

        stage = sb("stage", [RING, UW])
        lo = at("lo", [RING, UW], 0, F32R)
        hi = sb("hi", [HRING, UW], F32R)
        ada_w = sb("ada_w", [ARING, KT, AC])
        ada_b = sb("ada_b", [ARING, AC])
        ada_acc = sb("ada_acc", [ARING, AC])
        mods = sb("mods", [2, 3, D])
        xs = sb("xs", [TT, D])
        h_at = top[0]
        hs = sb("hs", [TT, D])
        gn = at("gn", [RV], h_at)
        g_at = top[0]
        normg = sb("normg", [D])
        ropet = at("ropet", [3, 256], g_at)
        dst = at("dst", [2, TT * SEQ], g_at)
        cb1 = at("cb1", [KT, P], h_at)
        cst = sb("cst", [C_N])
        ccol = sb("ccol", [KT])
        cact = sb("cact", [KT])
        ssq = sb("ssq", [TT])
        root = sb("root", [TT])
        rstd = sb("rstd", [TT])
        warm = sb("warm", [8])
        declog = sb("declog", [2 * RH])
        decexp = sb("decexp", [2 * RH])
        decln = sb("decln", [2 * RH])
        gstat = sb("gstat", [8, 6])
        gmv = sb("gmv", [8, 2])
        groot = sb("groot", [8])
        grstd = sb("grstd", [8])
        pos = sb("pos", [TT, 2 * E])
        comb = sb("comb", [TT, E])
        meta = sb("meta", [2 * N_TAB + 8], I32)
        R = top[0]
        KW = 256
        hT_hi = at("hT_hi", [KT, SEQ], R, F32R)
        hT_lo = at("hT_lo", [KT, SEQ], R + 8 * KW, F32R)
        squares1 = at("squares1", [TT, D], R)
        squares = at("squares", [TT, D], R + 28 * KW)
        pre_w = at("pre_w", [V_OWN, KT, AC], R)
        pre_b = at("pre_b", [V_OWN, AC], R + 8 * V_OWN * KW)
        proj = at("proj", [N_IN, TT, CB], R + 16 * KW)
        dec = at("dec", [2, TT * SEQ], R + 4 * KW)
        rqT = at("rqT", [2, 2, SEQ], R + 8 * KW)
        rkT = at("rkT", [2, 2, SEQ], R + 12 * KW)
        yT_hi = at("yT_hi", [2 * KT, SEQ], R + 16 * KW, F32R)
        yT_lo = at("yT_lo", [2 * KT, SEQ], R + 32 * KW, F32R)
        cb0 = at("cb0", [KT, P], R + 60 * KW)
        finrow = at("finrow", [ARING, AC], R + 62 * KW)
        fsil = at("fsil", [TT, FCH], R + 16 * KW)
        fact = at("fact", [TT, FCH], R + 18 * KW)
        faT_hi = at("faT_hi", [2, SEQ], R + 20 * KW, F32R)
        faT_lo = at("faT_lo", [2, SEQ], R + 22 * KW, F32R)
        oT_hi = at("oT_hi", [AH, SEQ], R, F32R)
        oT_lo = at("oT_lo", [AH, SEQ], R + 8 * KW, F32R)
        qkv = at("qkv", [TT, QKV], R + 16 * KW)
        apt = at("apt", [3, TT, 320], R + 28 * KW)
        aqT = at("aqT", [AH, SEQ], R + 36 * KW)
        akT = at("akT", [AKV, SEQ], R + 44 * KW)
        prob = at("prob", [2, TT, SEQ], R + 46 * KW)
        probT = at("probT", [2, TT, SEQ], R + 50 * KW)
        asq = at("asq", [10 * AHD], R + 54 * KW)
        again = at("again", [2, AHD], R + 59 * KW)
        ahs = at("ahs", [TT, 4, 10], R + 60 * KW)
        asm = at("asm", [AH, 4, TT], R + 61 * KW)
        hg_hi = at("hg_hi", [KT, SLOTS], R, F32R)
        hg_lo = at("hg_lo", [KT, SLOTS], R + 4 * KW, F32R)
        moe = at("moe", [TT, D], R + 8 * KW)
        hh = at("hh", [TT, D], R + 16 * KW, F32R)
        hl = at("hl", [TT, D], R + 24 * KW, F32R)
        pick = at("pick", [TT, SLOTS], R + 32 * KW, F32R)
        put = at("put", [SEQ], R + 33 * KW, F32R)
        esil = at("esil", [ECH], R + 34 * KW)
        eact = at("eact", [ECH], R + 36 * KW)
        eaT_hi = at("eaT_hi", [4, SLOTS], R + 38 * KW, F32R)
        eaT_lo = at("eaT_lo", [4, SLOTS], R + 40 * KW, F32R)
        dn_hi = at("dn_hi", [D], R + 42 * KW, F32R)
        dn_lo = at("dn_lo", [D], R + 46 * KW, F32R)
        wr = at("wr", [KT, E], R + 60 * KW + 128)
        wr_hl = at("wr_hl", [KT, 2 * E], R + 51 * KW, F32R)
        rsm = at("rsm", [TT, 10, 8], R + 53 * KW)
        ridx = at("ridx", [TT, 8], R + 54 * KW, U32)
        rtab = at("rtab", [2 * N_TAB + 8], R + 55 * KW)
        rflag = at("rflag", [4, 8], R + 56 * KW)
        brt = at("brt", [E], R + 61 * KW + 128)
        assert base + 4 * (R + 64 * KW) <= nc.sbuf_usable_end, (base + 4 * (R + 64 * KW), nc.sbuf_usable_end)

        bank = ctx.enter_context(nc.psum_tensor("bank", [P, 8, 512], F32))
        fin_dram = nc.dram_tensor("fin_rows", [1, 2 * D], F32, kind="Internal").ap()

        ident = cst[:, C_ID:C_ID + P]
        ones = cst[:, C_ONE:C_ONE + P]
        tri = cst[:, C_TRI:C_TRI + P]
        iota = cst[:, C_IOTA:C_IOTA + P]
        eps = cst[:, C_EPS:C_EPS + 1]

        w_load = [sem(f"w_load{i}") for i in range(RING)]
        hi_done = sem("hi_done")
        lo_done = sem("lo_done")
        w_used = sem("w_used")
        a_load = [sem(f"a_load{i}") for i in range(ARING)]
        a_free = [sem(f"a_free{i}") for i in range(ARING)]
        pre_load = [sem(f"pre_load{i}") for i in range(V_OWN)]
        a_acc = sem("a_acc")
        cb_done = sem("cb_done")
        a_step = sem("a_step")
        a_sum = sem("a_sum")
        a_out = sem("a_out")
        const_in = sem("const_in")
        x_in = sem("x_in")
        c_in = sem("c_in")
        g_in = sem("g_in")
        aux_in = sem("aux_in")
        c_act = sem("c_act")
        v_link = sem("v_link")
        s_link = sem("s_link")
        p_link = sem("p_link")
        b_zero = sem("b_zero")
        root_done = sem("root_done")
        scale_done = sem("scale_done")
        h_ready = sem("h_ready")
        tr_done = sem("tr_done")
        hT_hi_done = sem("hT_hi_done")
        hT_done = sem("hT_done")
        proj_out = sem("proj_out")
        rope_done = sem("rope_done")
        sg_done = sem("sg_done")
        gate_done = sem("gate_done")
        ln_done = sem("ln_done")
        arg_done = sem("arg_done")
        dec_done = sem("dec_done")
        qk_tr = sem("qk_tr")
        qT_done = sem("qT_done")
        kT_done = sem("kT_done")
        sc_done = sem("sc_done")
        s_done = sem("s_done")
        y_done = sem("y_done")
        st_done = sem("st_done")
        yraw_done = sem("yraw_done")
        mv_done = sem("mv_done")
        groot_done = sem("groot_done")
        gated = sem("gated")
        y_tr = sem("y_tr")
        yT_hi_done = sem("yT_hi_done")
        yT_done = sem("yT_done")
        t0_done = sem("t0_done")
        resid = sem("resid")
        row_out = [sem(f"row_out{i}") for i in range(ARING)]
        row_in = sem("row_in")
        f_silu = sem("f_silu")
        f_act = sem("f_act")
        f_tr = sem("f_tr")
        f_hi = sem("f_hi")
        f_lo = sem("f_lo")
        qkv_out = sem("qkv_out")
        hsum = sem("hsum")
        hroot = sem("hroot")
        qn_done = sem("qn_done")
        arope = sem("arope")
        aq_tr = sem("aq_tr")
        aq_out = sem("aq_out")
        at_sc = sem("at_sc")
        at_max = sem("at_max")
        at_exp = sem("at_exp")
        at_norm = sem("at_norm")
        at_tr = sem("at_tr")
        at_pT = sem("at_pT")
        at_o = sem("at_o")
        o_hi = sem("o_hi")
        o_lo = sem("o_lo")
        r_in = sem("r_in")
        r_w = sem("r_w")
        r_mm = sem("r_mm")
        r_d = sem("r_d")
        r_e = sem("r_e")
        r_sel = sem("r_sel")
        r_rank = sem("r_rank")
        r_meta = sem("r_meta")
        hh_done = sem("hh_done")
        hl_done = sem("hl_done")
        m_zero = sem("m_zero")
        pick_done = sem("pick_done")
        gath = sem("gath")
        hg_hi_done = sem("hg_hi_done")
        hg_lo_done = sem("hg_lo_done")
        put_tr = sem("put_tr")
        put_done = sem("put_done")
        e_silu = sem("e_silu")
        e_act = sem("e_act")
        e_tr = sem("e_tr")
        e_hi = sem("e_hi")
        e_lo = sem("e_lo")
        dn_hi_done = sem("dn_hi_done")
        dn_done = sem("dn_done")
        scat = sem("scat")
        moe_add = sem("moe_add")
        stored = sem("stored")

        def rows(w):
            return w.rearrange("(k p) n -> p k n", p=P)

        w_in_v, w_out_v = rows(l0_ret_w_in), rows(l0_ret_w_out)
        fg_v, fu_v, fd_v = rows(l0_ffn_w_gate), rows(l0_ffn_w_up), rows(l0_ffn_w_down)
        qkv_v, ao_v = rows(l1_attn_w_qkv), rows(l1_attn_w_out)
        mg_v = l1_moe_w_gate.rearrange("e (k p) n -> e p k n", p=P)
        mu_v = l1_moe_w_up.rearrange("e (k p) n -> e p k n", p=P)
        md_v = l1_moe_w_down.rearrange("e (k p) n -> e p k n", p=P)

        block = ctx.enter_context(nc.Block())

        @block.sync
        def _(sp):
            sp.sem_inc(w_used, RING)
            for i in range(ARING):
                sp.sem_inc(a_free[i], 1 + V_OWN // ARING)
                sp.sem_inc(a_load[i], 32 * (V_OWN // ARING))
            sp.sem_inc(a_sum, ARING)
            sp.sem_inc(a_out, ARING)
            sp.sem_inc(proj_out, 3)
            sp.sem_inc(moe_add, TT)
            sp.sem_inc(scat, 1)

            def load(b, src, more=0):
                sp.wait_ge(w_used, b + more + 1)
                nk = src.shape[1]
                dst_ap = stage[:, b % RING, :].rearrange("p (k n) -> p k n", k=nk)
                for ks in (slice(0, nk // 2), slice(nk // 2, nk)):
                    sp.dma_start(dst_ap[:, ks, :], src[:, ks, :]).then_inc(w_load[b % RING], 16)

            def load_pair(b, k0, cols, more=0):
                sp.wait_ge(w_used, b + more + 1)
                dst_ap = stage[:, b % RING, :].rearrange("p (k g n) -> p k g n", k=4, g=2)
                for g, wv in enumerate((fg_v, fu_v)):
                    sp.dma_start(dst_ap[:, :, g, :], wv[:, k0:k0 + 4, cols]).then_inc(w_load[b % RING], 16)

            def load_ada(b, w, bias, col, half=0):
                sp.wait_ge(a_free[b % ARING], b // ARING + 1 + half)
                sp.dma_start(ada_w[:, b % ARING], rows(w)[:, :, bass.ds(col, AC)]).then_inc(a_load[b % ARING], 16)
                sp.dma_start(ada_b[0:1, b % ARING, :], bias.unsqueeze(0)[:, bass.ds(col, AC)]).then_inc(a_load[b % ARING], 16)

            sp.dma_start(ccol[:, :], c.rearrange("a (k p) -> p (a k)", p=P), allow_slow_non_contiguous=True).then_inc(c_in, 16)
            sp.dma_start(cst[:, :], consts).then_inc(const_in, 16)
            xv = x.rearrange("a (t p) d -> p (a t) d", p=P)
            for v in range(V_OWN):
                sp.dma_start(pre_w[:, v], rows(l0_ada_w)[:, :, v * AC:(v + 1) * AC]).then_inc(pre_load[v], 16)
                if v == 0:
                    sp.wait_ge(b_zero, 1)
                sp.dma_start(pre_b[0:1, v, :], l0_ada_b.unsqueeze(0)[:, v * AC:(v + 1) * AC]).then_inc(pre_load[v], 16)
            for v in range(V_OWN, V_PRE):
                load_ada(v, l0_ada_w, l0_ada_b, v * AC)
                if v == V_OWN:
                    sp.dma_start(xs[:, :, :], xv).then_inc(x_in, 16)
            with sp.Fori(0, N_IN // 3) as it:
                a = 0
                for k in range(6):
                    load(U_RET + k, w_in_v[:, (k % 2) * 4:(k % 2) * 4 + 4, bass.ds(it * (3 * CB) + (k // 2) * CB, CB)], it * 6)
                    if k in (0, 1, 3, 4):
                        load_ada(V_PRE + a, l0_ada_w, l0_ada_b, it * (4 * AC) + (V_PRE + a) * AC, it * 2)
                        a += 1
            v = V_PRE + V_IN
            for k in range(8):
                n, kg = k // 4, k % 4
                load(U_ROUT + k, w_out_v[:, 4 * kg:4 * kg + 4, n * CB:(n + 1) * CB])
                load_ada(v + k, final_ada_w, final_ada_b, k * AC)
            v += V_FIN
            load_pair(U_FF, 0, slice(0, FCH))
            load_pair(U_FF + 1, 4, slice(0, FCH))
            with sp.Fori(0, (N_FF - 1) // 2) as it:
                for q in range(2):
                    b = U_FF + 2 + 3 * q
                    cols = bass.ds(it * (2 * FCH) + (q + 1) * FCH, FCH)
                    load_pair(b, 0, cols, it * 6)
                    load_pair(b + 1, 4, cols, it * 6)
                    load(b + 2, fd_v[:, bass.ds(it * 4 + 2 * q, 2), :], it * 6)
                    for a in range(2 * q, 2 * q + 2):
                        load_ada(v + a, l1_ada_w, l1_ada_b, it * (4 * AC) + a * AC, it * 2)
            load(U_QKV - 1, fd_v[:, 2 * (N_FF - 1):2 * N_FF, :])
            v += V_FF
            for k in range(6):
                n, kg = k // 2, k % 2
                load(U_QKV + k, qkv_v[:, 4 * kg:4 * kg + 4, n * CB:(n + 1) * CB])
            for a in range(2):
                load_ada(v + a, l1_ada_w, l1_ada_b, (V_FF + a) * AC)
            for k in range(4):
                n, kg = k // 2, k % 2
                load(U_AOUT + k, ao_v[:, 4 * kg:4 * kg + 4, n * CB:(n + 1) * CB])
            for a in range(2, 4):
                load_ada(v + a, l1_ada_w, l1_ada_b, (V_FF + a) * AC)

            def load_gate_up(e, b, col, more):
                for m, wv in ((0, mg_v), (2, mu_v)):
                    for g in range(2):
                        load(b + m + g, wv[e, :, 4 * g:4 * g + 4, col] if isinstance(e, int) else
                             wv[bass.ds(e, 1), :, 4 * g:4 * g + 4, col].rearrange("a p k n -> p (a k) n"), more)

            def load_down(e, b, kt, more):
                for g in range(2):
                    ks = bass.ds(kt + 2 * g, 2)
                    load(b + g, md_v[e, :, ks, :] if isinstance(e, int) else
                         md_v[bass.ds(e, 1), :, ks, :].rearrange("a p k n -> p (a k) n"), more)

            def item(e, more):
                load_gate_up(e, U_MOE, slice(0, ECH), more)
                with sp.Fori(1, N_EC) as j:
                    jm = j * 6 - 6
                    load_gate_up(e, U_MOE + 4, bass.ds(j * ECH, ECH), more + jm)
                    load_down(e, U_MOE + 8, j * 4 - 4, more + jm)
                load_down(e, U_MOE + UNITS_ITEM - 2, 4 * (N_EC - 1), more)

            item(0, 0)
            sp.wait_ge(r_meta, 1)
            passes = sp.value_load(meta[0:1, 2 * N_TAB:2 * N_TAB + 1], min_val=E, max_val=E + 3)
            with sp.Fori(1, passes) as w:
                e = sp.value_load(meta[0:1, bass.ds(w, 1)], min_val=0, max_val=E - 1)
                item(e, w * UNITS_ITEM)
            sp.wait_ge(stored, 32)

        @block.gpsimd
        def _(pool):
            nc.gpsimd.memset(pre_b[:, :, :], 0.0)
            nc.gpsimd.memset(ada_b[:, :, :], 0.0).then_inc(b_zero, 1)
            n_link = [0]

            def link(ins):
                n_link[0] += 1
                ins.then_inc(p_link, 1)
                pool.wait_ge(p_link, n_link[0])

            def repeat_c(dst_ap):
                for k in range(KT):
                    ins = nc.gpsimd.tensor_scalar(dst_ap[:, k, :], ones, cact[:, k:k + 1], None, ALU.mult)
                ins.then_inc(cb_done, 1)

            pool.dma_start(normg[:, :], l0_norm1_g.partition_broadcast(P)).then_inc(g_in, 16)
            pool.wait_ge(const_in, 16)
            pool.wait_ge(c_act, 1)
            repeat_c(cb0)
            pool.dma_start(declog[:, :], l0_ret_decay_logit.rearrange("a b -> (a b)").partition_broadcast(P)).then_inc(aux_in, 16)
            pool.wait_ge(tr_done, 4)
            pool.dma_start(gn[:, :], l0_ret_gn_g.partition_broadcast(P)).then_inc(aux_in, 16)

            def rotate(x1, x2, co, si, shape, tmp):
                ta, tb, tc = (t.rearrange(shape[0], **shape[1]) for t in tmp)
                nc.gpsimd.tensor_tensor(ta, x1, co, ALU.mult)
                nc.gpsimd.tensor_tensor(tb, x2, si, ALU.mult)
                nc.gpsimd.tensor_tensor(tc, x1, si, ALU.mult)
                link(nc.gpsimd.tensor_tensor(x2, x2, co, ALU.mult))
                nc.gpsimd.tensor_tensor(x1, ta, tb, ALU.subtract)
                ins = nc.gpsimd.tensor_tensor(x2, x2, tc, ALU.add)
                link(ins)

            pool.wait_ge(scale_done, 1)
            for q in range(4):
                pool.wait_ge(proj_out, 3 + q + 1)
                for t in range(TT):
                    v = proj[:, q, t, :].rearrange("p (h f s i) -> p h f s i", h=2, f=2, s=2)
                    for f in range(2):
                        co = cst[:, C_RC + (t * 2 + f) * 64:C_RC + (t * 2 + f + 1) * 64].unsqueeze(1).to_broadcast([P, 2, 64])
                        si = cst[:, C_RS + (t * 2 + f) * 64:C_RS + (t * 2 + f + 1) * 64].unsqueeze(1).to_broadcast([P, 2, 64])
                        rotate(v[:, :, f, 0, :], v[:, :, f, 1, :], co, si, ("p (h i) -> p h i", dict(h=2)),
                               [ropet[:, i, 0:128] for i in range(3)])
            pool.nop().then_inc(rope_done, 1)
            pool.dma_start(dst[:, :, :], dist.rearrange("p (s n) -> p s n", s=2)).then_inc(aux_in, 16)
            pool.wait_ge(aux_in, 48)
            for h in range(RH):
                pool.wait_ge(sg_done, h + 1)
                for t in range(TT):
                    g = proj[:, 8 + h, t, :]
                    nc.gpsimd.tensor_tensor(g, g, gn[:, h * RDV:(h + 1) * RDV], ALU.mult).then_inc(gate_done, 1)
            pool.wait_ge(arg_done, RH)
            pool.dma_start(normg[:, :], l0_norm2_g.partition_broadcast(P)).then_inc(g_in, 16)
            pool.wait_ge(scale_done, 2)
            pool.dma_start(normg[:, :], l1_norm1_g.partition_broadcast(P)).then_inc(g_in, 16)
            pool.wait_ge(scale_done, 3)
            pool.dma_start(again[:, 0, :], l1_attn_q_norm_g.partition_broadcast(P)).then_inc(aux_in, 16)
            pool.dma_start(again[:, 1, :], l1_attn_k_norm_g.partition_broadcast(P)).then_inc(aux_in, 16)
            pool.dma_start(wr[:, :, :], l1_moe_w_router.rearrange("(k p) e -> p k e", p=P)).then_inc(r_in, 16)
            pool.dma_start(brt[:, :], l1_moe_b_router.partition_broadcast(P)).then_inc(r_in, 16)
            pool.wait_ge(tr_done, 12)
            repeat_c(cb1)
            pool.dma_start(normg[:, :], l1_norm2_g.partition_broadcast(P)).then_inc(g_in, 16)
            for t in range(1):
                pool.wait_ge(qn_done, t + 1)
                v = qkv[:, t, 0:10 * AHD].rearrange("p (h f s i) -> p h f s i", h=10, f=2, s=2)
                for f in range(2):
                    co = cst[:, C_AC + (t * 2 + f) * 32:C_AC + (t * 2 + f + 1) * 32].unsqueeze(1).to_broadcast([P, 10, 32])
                    si = cst[:, C_AS + (t * 2 + f) * 32:C_AS + (t * 2 + f + 1) * 32].unsqueeze(1).to_broadcast([P, 10, 32])
                    rotate(v[:, :, f, 0, :], v[:, :, f, 1, :], co, si, ("p (h i) -> p h i", dict(h=10)),
                           [apt[:, i, t, :] for i in range(3)])
                pool.nop().then_inc(arope, 1)
            pool.wait_ge(resid, 3 * 4)
            for r in row_out:
                pool.wait_ge(r, 16 * V_FIN // ARING)
            pool.dma_start(mods[:, 0, 0, :], fin_dram[0, 0:D].partition_broadcast(P)).then_inc(row_in, 16)
            pool.dma_start(mods[:, 0, 1, :], fin_dram[0, D:2 * D].partition_broadcast(P)).then_inc(row_in, 16)
            pool.wait_ge(scale_done, 4)
            pool.dma_start(normg[:, :], final_norm_g.partition_broadcast(P)).then_inc(g_in, 16)

        @block.scalar
        def _(act):
            n_link = [0]

            def link(ins):
                n_link[0] += 1
                ins.then_inc(s_link, 1)
                act.wait_ge(s_link, n_link[0])

            def high(b, more=0, occ=0):
                act.wait_ge(w_load[b % RING], 32 * (b // RING + 1) + occ * 32)
                act.wait_ge(w_used, RING + b - HRING + 1 + more)
                nc.scalar.copy(hi[:, b % HRING, :], stage[:, b % RING, :]).then_inc(hi_done, 1)

            def ada_take(b, dst_ap, more=0):
                act.wait_ge(a_sum, ARING + b + 1 + more)
                nc.scalar.copy(dst_ap, bank[:, 3, (b % ARING) * AC:(b % ARING + 1) * AC]).then_inc(a_out, 1)

            def mod_at(col):
                return mods[:, :, :, :].rearrange("p a b d -> p (a b d)")[:, bass.ds(col, AC)]

            def norm(s, after=(0, 0)):
                nc.scalar.activation(warm[:, s:s + 1], eps, ACT.Sqrt)
                for t in range(TT):
                    if after[t]:
                        act.wait_ge(resid, after[t])
                    nc.scalar.activation((squares1 if s == 1 else squares)[:, t, :], xs[:, t, :], ACT.Square,
                                         accum_out=ssq[:, t:t + 1]).then_inc(s_link, 1)
                n_link[0] += TT
                for t in range(TT):
                    act.wait_ge(s_link, n_link[0] - TT + 1 + t)
                    nc.scalar.activation(root[:, t:t + 1], ssq[:, t:t + 1], ACT.Sqrt, scale=1.0 / D, bias=eps).then_inc(root_done, 1)

            def high_T(s):
                for i in range(4):
                    act.wait_ge(tr_done, 4 * s + i + 1)
                    t, g = i // 2, i % 2
                    nc.scalar.copy(hT_hi[:, 4 * g:4 * g + 4, t * P:(t + 1) * P],
                                   bank[:, 4 + i, :].rearrange("p (k n) -> p k n", k=4)).then_inc(hT_hi_done, 1)

            act.wait_ge(c_in, 16)
            nc.scalar.activation(cact[:, :], ccol[:, :], ACT.Silu).then_inc(c_act, 1)
            act.wait_ge(const_in, 16)
            for v in range(V_PRE):
                if v == V_OWN:
                    act.wait_ge(x_in, 16)
                    norm(0)
                if v == V_PRE - 1:
                    high(U_RET)
                ada_take(v, mod_at(v * AC))
            high_T(0)
            for k in range(1, 3):
                high(U_RET + k)

            PAIRS = [(0, 1), (2, 4), (5, 6)]

            def take_chunk(i, cc):
                act.wait_ge(w_used, RING + U_RET + 2 + cc * 2)
                for t in range(TT):
                    ins = nc.scalar.copy(
                        proj[:, :, :, :].rearrange("p c t n -> p (c t n)")[:, bass.ds(cc * (TT * CB) + t * CB, CB)],
                        bank[:, PAIRS[i][t], :])
                ins.then_inc(proj_out, 1)

            def in_body(it, first, skip=0):
                for k in range(skip, 6):
                    high(U_RET + k, it * 6, it)
                    in_after(it, k, first)

            def in_after(it, k, first):
                if k == 0 and not first:
                    ada_take(V_PRE + 2, mod_at(it * (4 * AC) - 4 * AC + (V_PRE + 2) * AC), it * 4 - 4)
                    take_chunk(1, it * 3 - 2)
                if k == 1 and not first:
                    ada_take(V_PRE + 3, mod_at(it * (4 * AC) - 4 * AC + (V_PRE + 3) * AC), it * 4 - 4)
                if k == 2 and not first:
                    take_chunk(2, it * 3 - 1)
                if k == 3:
                    ada_take(V_PRE, mod_at(it * (4 * AC) + V_PRE * AC), it * 4)
                if k == 4:
                    ada_take(V_PRE + 1, mod_at(it * (4 * AC) + (V_PRE + 1) * AC), it * 4)
                    take_chunk(0, it * 3)

            act.wait_ge(aux_in, 32)
            link(nc.scalar.activation(decexp[:, :], declog[:, :], ACT.Exp, scale=-1.0))
            nc.scalar.activation(decln[:, :], decexp[:, :], ACT.Ln, bias=1.0).then_inc(ln_done, 1)
            in_body(0, True, 3)
            with act.Fori(1, N_IN // 3) as it:
                in_body(it, False)
            last = N_IN // 3
            for k in range(3):
                if k == 2:
                    in_after(last, k, False)
                high(U_ROUT + k)
                if k < 2:
                    in_after(last, k, False)

            def q_take(h):
                act.wait_ge(qk_tr, 2 * h + 1)
                if h >= 2:
                    act.wait_ge(sc_done, h - 1)
                nc.scalar.copy(rqT[:, h % 2], bank[:, 4, :].rearrange("p (k n) -> p k n", k=2)).then_inc(qT_done, 1)

            def decay(h):
                act.wait_ge(arg_done, h + 1)
                nc.scalar.activation(dec[:, h % 2], dec[:, h % 2], ACT.Exp, scale=-1.0).then_inc(dec_done, 1)

            def g_roots(half):
                act.wait_ge(mv_done, half + 1)
                i = slice(4 * half, 4 * half + 4)
                nc.scalar.activation(groot[:, i], gmv[:, i, 1], ACT.Sqrt, bias=eps).then_inc(groot_done, 1)

            q_take(0)
            decay(0)
            decay(1)
            q_take(1)
            for h in range(RH):
                g = proj[:, 8 + h, :, :]
                if h == 0:
                    act.wait_ge(proj_out, 3 + N_IN)
                nc.scalar.activation(g, g, ACT.Silu).then_inc(sg_done, 1)

            def y_take(h):
                act.wait_ge(y_done, 2 * h + 2)
                act.wait_ge(st_done, 2 * h + 2)
                for t in range(TT):
                    nc.scalar.copy(proj[:, 4 + h, t, :], bank[:, (7, 2)[t], :]).then_inc(yraw_done, 1)

            for h in range(RH):
                y_take(h)
                if h + 2 < RH:
                    decay(h + 2)
                    if h == 1:
                        g_roots(0)
                    q_take(h + 2)
            g_roots(1)
            for i in range(8):
                act.wait_ge(y_tr, i + 1)
                h, t = i // 2, i % 2
                nc.scalar.copy(yT_hi[:, 4 * h:4 * h + 4, t * P:(t + 1) * P],
                               bank[:, 4 + i % 4, :].rearrange("p (k n) -> p k n", k=4)).then_inc(yT_hi_done, 1)
            def fin_take(a):
                v = V_PRE + V_IN + a
                if a >= ARING:
                    act.wait_ge(row_out[a % ARING], 16 * (a // ARING))
                ada_take(v, finrow[:, v % ARING, :])
                act.wait_ge(a_out, ARING + v + 1)
                act.dma_start(fin_dram[0:1, a * AC:(a + 1) * AC], finrow[0:1, v % ARING, :]).then_inc(row_out[a % ARING], 16)

            for k in range(3, 8):
                high(U_ROUT + k)
                fin_take(k - 3)
            high(U_FF)
            fin_take(5)
            fin_take(6)
            high(U_FF + 1)

            norm(1, (3, 4))
            high_T(1)
            V0 = V_PRE + V_IN + V_FIN

            def f_silu_step(cc):
                act.wait_ge(w_used, RING + U_FF + 2 if isinstance(cc, int) and cc == 0 else cc * 3 + (RING + U_FF + 1))
                act.wait_ge(f_act, cc)
                nc.scalar.activation(fsil[:, :, :], bank[:, 0:2, 0:FCH], ACT.Silu).then_inc(f_silu, 1)

            def f_high_act(cc):
                act.wait_ge(f_tr, cc + 1)
                nc.scalar.copy(faT_hi[:, :, :], bank[:, 2, :].rearrange("p (k n) -> p k n", k=2)).then_inc(f_hi, 1)

            def take_pair(col, more):
                act.wait_ge(a_sum, ARING + V0 + 2 + more)
                nc.scalar.copy(mods[:, :, :, :].rearrange("p a b d -> p (a b d)")[:, bass.ds(col, 2 * AC)],
                               bank[:, 3, :]).then_inc(a_out, 2)

            def f_chunk(it, q, pair):
                b = U_FF + 2 + 3 * q
                cc = it * 2 + 1 + q
                high(b, it * 6, it)
                f_silu_step(cc - 1)
                high(b + 1, it * 6, it)
                if pair:
                    take_pair(it * (4 * AC) + (2 * q - 2) * AC, it * 4 + (2 * q - 2))
                f_high_act(cc - 1)
                high(b + 2, it * 6, it)

            f_chunk(0, 0, False)
            fin_take(V_FIN - 1)
            f_chunk(0, 1, True)
            with act.Fori(1, (N_FF - 1) // 2) as it:
                f_chunk(it, 0, True)
                f_chunk(it, 1, True)
            f_silu_step(N_FF - 1)
            high(U_QKV - 1)
            take_pair((V_FF - 2) * AC, V_FF - 2)
            f_high_act(N_FF - 1)

            high(U_QKV)
            high(U_QKV + 1)
            norm(2, (6, 8))
            high_T(2)
            high(U_QKV + 2)
            V1 = V0 + V_FF

            def qkv_take(n):
                act.wait_ge(w_used, RING + U_QKV + 2 * n + 2)
                for t in range(TT):
                    ins = nc.scalar.copy(qkv[:, t, n * CB:(n + 1) * CB], bank[:, PAIRS[n][t], :])
                ins.then_inc(qkv_out, 1)

            for k in range(3, 6):
                high(U_QKV + k)
                if k == 4:
                    qkv_take(0)
            high(U_AOUT)
            qkv_take(1)
            high(U_AOUT + 1)
            qkv_take(2)
            ada_take(V1, mod_at(V_FF * AC))
            for t in range(TT):
                act.wait_ge(hsum, t + 1)
                nc.scalar.activation(ahs[:, t, 1, :], ahs[:, t, 0, :], ACT.Sqrt, scale=1.0 / AHD, bias=eps).then_inc(hroot, 1)
            high(U_AOUT + 2)
            ada_take(V1 + 1, mod_at((V_FF + 1) * AC))
            for i in range(5):
                act.wait_ge(aq_tr, i + 1)
                dst_ap = (aqT[:, 2 * i:2 * i + 2, :] if i < 4 else akT[:, :, :])
                nc.scalar.copy(dst_ap, bank[:, (4, 5)[i % 2], :].rearrange("p (k n) -> p k n", k=2)).then_inc(aq_out, 1)

            def soft(h):
                act.wait_ge(at_max, h + 1)
                if h >= 2:
                    act.wait_ge(at_tr, h - 1)
                for t in range(TT):
                    ins = nc.scalar.activation(prob[:, h % 2, t, :], bank[:, 4 + h % 2, t * SEQ:(t + 1) * SEQ], ACT.Exp,
                                               bias=asm[:, h, 1, t:t + 1], scale=float(AHD) ** -0.5,
                                               accum_out=asm[:, h, 2, t:t + 1])
                    ins.then_inc(at_exp, 1)

            def pT_take(h):
                act.wait_ge(at_tr, h + 1)
                if h >= 2:
                    act.wait_ge(at_o, h - 1)
                nc.scalar.copy(probT[:, h % 2], bank[:, 6 + h % 2, :].rearrange("p (k n) -> p k n", k=2)).then_inc(at_pT, 1)

            def o_take(h):
                act.wait_ge(at_o, h + 1)
                nc.scalar.copy(oT_hi[:, h, :], bank[:, h % 2, 0:SEQ]).then_inc(o_hi, 1)

            for h in range(AH + 2):
                if h < AH:
                    soft(h)
                if 1 <= h <= AH:
                    pT_take(h - 1)
                if h >= 2:
                    o_take(h - 2)
                if h in (4, 6):
                    ada_take(V1 + h // 2, mod_at((V_FF + h // 2) * AC))
            high(U_AOUT + 3)

            act.wait_ge(r_in, 32)
            nc.scalar.copy(wr_hl[:, :, 0:E], wr[:, :, :]).then_inc(r_w, 1)
            high(U_MOE)
            high(U_MOE + 1)
            norm(3, (11, 12))
            high_T(3)
            high(U_MOE + 2)
            for t in range(TT):
                nc.scalar.copy(hh[:, t, :], hs[:, t, :]).then_inc(hh_done, 1)
            act.wait_ge(r_d, 1)
            nc.scalar.activation(rsm[:, :, 5, 0:1], rsm[:, :, 4, 0:1], ACT.Exp).then_inc(r_e, 1)

            def take_gathered(w):
                act.wait_ge(gath, w * 2 + 1)
                nc.scalar.copy(hg_hi[:, :, :], bank[:, 6:8, :].rearrange("p b (k n) -> p (b k) n", k=4)).then_inc(hg_hi_done, 1)

            def take_put(w):
                act.wait_ge(put_tr, w + 1)
                nc.scalar.copy(put[:, :], bank[:, 6, 0:SEQ]).then_inc(put_done, 1)

            def e_silu_step(n, used):
                act.wait_ge(w_used, used)
                act.wait_ge(e_act, n)
                nc.scalar.activation(esil[:, :], bank[:, 0, :], ACT.Silu).then_inc(e_silu, 1)

            def e_high_act(n):
                act.wait_ge(e_tr, n + 1)
                nc.scalar.copy(eaT_hi[:, :, :], bank[:, 2, :].rearrange("p (k n) -> p k n", k=4)).then_inc(e_hi, 1)

            def take_down(n):
                act.wait_ge(w_used, n * UNITS_ITEM + (RING + U_MOE))
                nc.scalar.copy(dn_hi[:, :], bank[:, 4:6, :].rearrange("p b n -> p (b n)")).then_inc(dn_hi_done, 1)

            def item(w, first):
                m, o = w * UNITS_ITEM, w * N_EC
                if first:
                    take_gathered(0)
                else:
                    high(U_MOE, m, o)
                    high(U_MOE + 1, m, o)
                    take_down(w)
                    high(U_MOE + 2, m, o)
                high(U_MOE + 3, m, o)
                take_put(w)
                e_silu_step(w * N_EC, m + (RING + U_MOE + 2))
                with act.Fori(1, N_EC) as j:
                    jm, jo = m + j * 6 - 6, o + j - 1
                    b = U_MOE + 4
                    n = w * N_EC + j
                    high(b, jm, jo)
                    high(b + 1, jm, jo)
                    high(b + 2, jm, jo)
                    e_high_act(n - 1)
                    high(b + 3, jm, jo)
                    high(b + 4, jm, jo)
                    e_silu_step(n, jm + (RING + U_MOE + 6))
                    high(b + 5, jm, jo)
                high(U_MOE + UNITS_ITEM - 2, m, o)
                e_high_act(w * N_EC + N_EC - 1)
                high(U_MOE + UNITS_ITEM - 1, m, o)
                take_gathered(w + 1)

            item(0, True)
            passes = act.value_load(meta[0:1, 2 * N_TAB:2 * N_TAB + 1], min_val=E, max_val=E + 3)
            with act.Fori(1, passes) as w:
                item(w, False)
            take_down(passes)
            norm(4, (14, 16))
            ov = out.rearrange("a (t p) d -> p (a t) d", p=P)
            for t in range(TT):
                act.wait_ge(h_ready, 2 * 4 + t + 1)
                act.dma_start(ov[:, t, :], hs[:, t, :]).then_inc(stored, 16)
            act.wait_ge(stored, 32)

        @block.vector
        def _(dve):
            n_link = [0]

            def link(ins):
                n_link[0] += 1
                ins.then_inc(v_link, 1)
                dve.wait_ge(v_link, n_link[0])

            def low(b, more=0):
                dve.wait_ge(hi_done, b + 1 + more)
                nc.vector.tensor_tensor(lo[:, b % RING, :], stage[:, b % RING, :],
                                        hi[:, b % HRING, :].bitcast(F32), ALU.subtract).then_inc(lo_done, 1)

            def ada(b, n, half=0):
                more = half * ARING
                s = b % ARING
                own = b < V_OWN
                if own:
                    dve.wait_ge(pre_load[b], 32)
                else:
                    dve.wait_ge(a_load[s], 32 * (b // ARING + 1) + half * 32)
                dve.wait_ge(a_sum, b + 1 + more)
                wt, bias = (pre_w[:, b], pre_b[:, b, :]) if own else (ada_w[:, s], ada_b[:, s, :])
                for k in range(KT):
                    prev = bias if k == 0 else ada_acc[:, s, :]
                    ins = nc.vector.scalar_tensor_tensor(out=ada_acc[:, s, :], in0=wt[:, k, :],
                                                         scalar=cact[:, k:k + 1], in1=prev,
                                                         op0=ALU.mult, op1=ALU.add)
                    if k < KT - 1:
                        ins.then_inc(a_step, 1)
                        dve.wait_ge(a_step, (KT - 1) * n + k + 1 + more * (KT - 1))
                    else:
                        ins.then_inc(a_acc, 1)
                if not own:
                    dve.wait_ge(a_acc, n + 1 + more)
                    dve.sem_inc(a_free[s], 1)

            def scale(s, took):
                m = mods[:, s % 2]
                dve.wait_ge(g_in, 16 * (s + 1))
                if took:
                    dve.wait_ge(a_out, ARING + took)
                nc.vector.scalar_tensor_tensor(out=m[:, 1, :], in0=m[:, 1, :], scalar=1.0, in1=normg[:, :],
                                               op0=ALU.add, op1=ALU.mult).then_inc(scale_done, 1)

            def norm(s, after=(0, 0)):
                m = mods[:, s % 2]
                dve.wait_ge(scale_done, s + 1)
                def scaled(t):
                    if after[t]:
                        dve.wait_ge(resid, after[t])
                    link(nc.vector.tensor_tensor(hs[:, t, :], xs[:, t, :], m[:, 1, :], ALU.mult))

                if s:
                    scaled(0)
                    scaled(1)
                for t in range(TT):
                    if s == 0:
                        scaled(t)
                    dve.wait_ge(root_done, 2 * s + t + 1)
                    link(nc.vector.reciprocal(rstd[:, t:t + 1], root[:, t:t + 1]))
                    nc.vector.scalar_tensor_tensor(out=hs[:, t, :], in0=hs[:, t, :], scalar=rstd[:, t:t + 1],
                                                   in1=m[:, 0, :], op0=ALU.mult, op1=ALU.add).then_inc(h_ready, 1)

            def low_T(s):
                for i in range(4):
                    dve.wait_ge(hT_hi_done, 4 * s + i + 1)
                    t, g = i // 2, i % 2
                    nc.vector.tensor_tensor(hT_lo[:, 4 * g:4 * g + 4, t * P:(t + 1) * P],
                                            bank[:, 4 + i, :].rearrange("p (k n) -> p k n", k=4),
                                            hT_hi[:, 4 * g:4 * g + 4, t * P:(t + 1) * P].bitcast(F32),
                                            ALU.subtract).then_inc(hT_done, 1)

            def residual(s, order, used):
                m = mods[:, s % 2, 2]
                for (n, t, src), u in zip(order, used):
                    cols = slice(n * CB, (n + 1) * CB)
                    if u is None:
                        dve.wait_ge(t0_done, s + 1)
                    else:
                        dve.wait_ge(w_used, RING + u)
                    link(nc.vector.tensor_tensor(hs[:, t, cols], src, m[:, cols], ALU.mult))
                    nc.vector.tensor_tensor(xs[:, t, cols], xs[:, t, cols], hs[:, t, cols], ALU.add).then_inc(resid, 1)

            dve.wait_ge(c_act, 1)
            for v in range(0, V_PRE, 2):
                ada(v, v // 2)
            dve.wait_ge(x_in, 16)
            low(U_RET)
            scale(0, V_PRE)
            norm(0)
            low_T(0)
            def in_step(it, k):
                if k:
                    low(U_RET + k, it * 6)
                if k in (0, 1, 3, 4):
                    a = (0, 1, None, 2, 3)[k]
                    ada(V_PRE + a, V_PRE // 2 + a, it * 2)

            for k in range(6):
                in_step(0, k)
            with dve.Fori(1, N_IN // 3) as it:
                low(U_RET, it * 6)
                for k in range(6):
                    in_step(it, k)

            def decay_arg(h):
                b = h % 2
                link(nc.vector.tensor_scalar(dec[:, b], dst[:, 0], decln[:, h:h + 1], None, ALU.mult))
                nc.vector.scalar_tensor_tensor(out=dec[:, b], in0=dst[:, 1], scalar=decln[:, RH + h:RH + h + 1],
                                               in1=dec[:, b], op0=ALU.mult, op1=ALU.add).then_inc(arg_done, 1)

            def k_take(h):
                dve.wait_ge(qk_tr, 2 * h + 2)
                if h >= 2:
                    dve.wait_ge(sc_done, h - 1)
                nc.vector.tensor_copy(rkT[:, h % 2], bank[:, 5, :].rearrange("p (k n) -> p k n", k=2)).then_inc(kT_done, 1)

            dve.wait_ge(ln_done, 1)
            dve.wait_ge(aux_in, 48)
            dve.wait_ge(w_used, RING + U_ROUT)
            decay_arg(0)
            k_take(0)
            decay_arg(1)
            k_take(1)

            def variances(half):
                dve.wait_ge(st_done, 4 * half + 4)
                for i in range(4 * half, 4 * half + 4):
                    ins = nc.vector.bn_aggr(gmv[:, i, :], gstat[:, i, :])
                ins.then_inc(mv_done, 1)

            def g_rstd(half):
                dve.wait_ge(groot_done, half + 1)
                i = slice(4 * half, 4 * half + 4)
                link(nc.vector.reciprocal(grstd[:, i], groot[:, i]))

            def gate(i):
                h, t = i // 2, i % 2
                dve.wait_ge(yraw_done, i + 1)
                dve.wait_ge(gate_done, i + 1)
                y, g = proj[:, 4 + h, t, :], proj[:, 8 + h, t, :]
                link(nc.vector.tensor_scalar(y, y, gmv[:, i, 0:1], grstd[:, i:i + 1], ALU.subtract, ALU.mult))
                nc.vector.tensor_tensor(g, y, g, ALU.mult).then_inc(gated, 1)

            for h in range(RH):
                dve.wait_ge(sc_done, h + 1)
                dve.wait_ge(dec_done, h + 1)
                nc.vector.scalar_tensor_tensor(out=dec[:, h % 2], in0=bank[:, 6, :], scalar=float(RDK) ** -0.5,
                                               in1=dec[:, h % 2], op0=ALU.mult, op1=ALU.mult).then_inc(s_done, 1)
                if h == 0:
                    low(U_ROUT)
                if h == 2:
                    g_rstd(0)
                if h >= 2:
                    gate(2 * h - 4)
                    gate(2 * h - 3)
                for t in range(TT):
                    dve.wait_ge(y_done, 2 * h + t + 1)
                    nc.vector.bn_stats(gstat[:, 2 * h + t, :], bank[:, (7, 2)[t], :]).then_inc(st_done, 1)
                if h + 2 < RH:
                    decay_arg(h + 2)
                    low(U_ROUT + 1 + h)
                    k_take(h + 2)
                if h == 1:
                    variances(0)
            variances(1)

            def low_y(i):
                dve.wait_ge(yT_hi_done, i + 1)
                dve.wait_ge(gated, 2 * (i // 2) + 2)
                h, t = i // 2, i % 2
                nc.vector.tensor_tensor(yT_lo[:, 4 * h:4 * h + 4, t * P:(t + 1) * P],
                                        bank[:, 4 + i % 4, :].rearrange("p (k n) -> p k n", k=4),
                                        yT_hi[:, 4 * h:4 * h + 4, t * P:(t + 1) * P].bitcast(F32),
                                        ALU.subtract).then_inc(yT_done, 1)

            for i in range(8):
                if i == 1:
                    g_rstd(1)
                if i + 3 >= 4 and i + 3 < 8:
                    gate(i + 3)
                low_y(i)
            v = V_PRE + V_IN
            for k in range(8):
                if k >= 3:
                    low(U_ROUT + k)
                if k == 6:
                    residual(0, [(0, 0, bank[:, 0, :]), (0, 1, bank[:, 1, :])], [U_FF - 4] * 2)
                if k < 7:
                    ada(v + k, V_PRE // 2 + V_IN + k)
            scale(1, V_PRE + V_IN)
            low(U_FF)
            residual(0, [(1, 0, bank[:, 6, :]), (1, 1, bank[:, 7, :])], [None, U_FF])

            V0 = V_PRE + V_IN + V_FIN
            norm(1, (3, 4))
            low_T(1)
            low(U_FF + 1)
            ada(V0 - 1, V_PRE // 2 + V_IN + V_FIN - 1)

            def f_mul(cc):
                dve.wait_ge(f_silu, cc + 1)
                dve.wait_ge(f_tr, cc)
                nc.vector.tensor_tensor(fact[:, :, :], bank[:, 0:2, FCH:2 * FCH], fsil[:, :, :], ALU.mult).then_inc(f_act, 1)

            def f_low_act(cc):
                dve.wait_ge(f_hi, cc + 1)
                nc.vector.tensor_tensor(faT_lo[:, :, :], bank[:, 2, :].rearrange("p (k n) -> p k n", k=2),
                                        faT_hi[:, :, :].bitcast(F32), ALU.subtract).then_inc(f_lo, 1)

            N0 = V_PRE // 2 + V_IN + V_FIN

            def f_pair(it):
                for q in range(2):
                    b = U_FF + 2 + 3 * q
                    cc = it * 2 + 1 + q
                    low(b, it * 6)
                    f_mul(cc - 1)
                    low(b + 1, it * 6)
                    f_low_act(cc - 1)
                    low(b + 2, it * 6)
                    for a in range(2 * q, 2 * q + 2):
                        ada(V0 + a, N0 + a, it * 2)

            f_pair(0)
            with dve.Fori(1, (N_FF - 1) // 2) as it:
                f_pair(it)
            f_mul(N_FF - 1)
            low(U_QKV - 1)
            f_low_act(N_FF - 1)
            V1 = V0 + V_FF
            scale(2, V1)
            low(U_QKV)
            residual(1, [(0, 0, bank[:, 4, :]), (1, 0, bank[:, 5, :]), (0, 1, bank[:, 6, :]), (1, 1, bank[:, 7, :])],
                     [None] * 2 + [U_QKV] * 2)

            norm(2, (6, 8))
            low_T(2)
            low(U_QKV + 1)
            for k in range(2, 6):
                low(U_QKV + k)
            low(U_AOUT)
            dve.wait_ge(qkv_out, 3)
            dve.wait_ge(aux_in, 80)
            for t in range(TT):
                qk = qkv[:, t, 0:10 * AHD]
                qh = qk.rearrange("p (h d) -> p h d", h=10)
                link(nc.vector.tensor_tensor(asq[:, :], qk, qk, ALU.mult))
                nc.vector.tensor_reduce(ahs[:, t, 0, :], asq[:, :].rearrange("p (h d) -> p h d", h=10), AX.X,
                                        ALU.add).then_inc(hsum, 1)
                for n, o, m in ((0, 0, AH), (1, AH, AKV)):
                    ins = nc.vector.tensor_tensor(qh[:, o:o + m, :], qh[:, o:o + m, :],
                                                  again[:, n, :].unsqueeze(1).to_broadcast([P, m, AHD]), ALU.mult)
                    ins.then_inc(v_link, 1)
                    n_link[0] += 1
                dve.wait_ge(hroot, t + 1)
                link(nc.vector.reciprocal(ahs[:, t, 2, :], ahs[:, t, 1, :]))
                nc.vector.tensor_tensor(qh, qh, ahs[:, t, 2, :].unsqueeze(2).to_broadcast([P, 10, AHD]),
                                        ALU.mult).then_inc(qn_done, 1)
            dve.wait_ge(qn_done, TT)
            v = qkv[:, 1, 0:10 * AHD].rearrange("p (h f s i) -> p h f s i", h=10, f=2, s=2)
            ta, tb, tc = (apt[:, i, 1, :].rearrange("p (h i) -> p h i", h=10) for i in range(3))
            for f in range(2):
                co = cst[:, C_AC + (2 + f) * 32:C_AC + (3 + f) * 32].unsqueeze(1).to_broadcast([P, 10, 32])
                si = cst[:, C_AS + (2 + f) * 32:C_AS + (3 + f) * 32].unsqueeze(1).to_broadcast([P, 10, 32])
                x1, x2 = v[:, :, f, 0, :], v[:, :, f, 1, :]
                nc.vector.tensor_tensor(ta, x1, co, ALU.mult)
                nc.vector.tensor_tensor(tb, x2, si, ALU.mult)
                nc.vector.tensor_tensor(tc, x1, si, ALU.mult)
                link(nc.vector.tensor_tensor(x2, x2, co, ALU.mult))
                nc.vector.tensor_tensor(x1, ta, tb, ALU.subtract)
                link(nc.vector.tensor_tensor(x2, x2, tc, ALU.add))
            dve.sem_inc(arope, 1)
            low(U_AOUT + 1)
            low(U_AOUT + 2)

            def row_max(h):
                dve.wait_ge(at_sc, h + 1)
                link(nc.vector.tensor_reduce(asm[:, h, 0, :], bank[:, 4 + h % 2, :].rearrange("p (t n) -> p t n", t=TT),
                                             AX.X, ALU.max))
                nc.vector.tensor_scalar(asm[:, h, 1, :], asm[:, h, 0, :], -float(AHD) ** -0.5, None,
                                        ALU.mult).then_inc(at_max, 1)

            def row_norm(h):
                dve.wait_ge(at_exp, 2 * h + 2)
                link(nc.vector.reciprocal(asm[:, h, 3, :], asm[:, h, 2, :]))
                for t in range(TT):
                    p = prob[:, h % 2, t, :]
                    nc.vector.tensor_scalar(p, p, asm[:, h, 3, t:t + 1], None, ALU.mult).then_inc(at_norm, 1)

            def o_low(h):
                dve.wait_ge(o_hi, h + 1)
                nc.vector.tensor_tensor(oT_lo[:, h, :], bank[:, h % 2, 0:SEQ], oT_hi[:, h, :].bitcast(F32),
                                        ALU.subtract).then_inc(o_lo, 1)

            for h in range(AH + 2):
                if h < AH:
                    row_max(h)
                    row_norm(h)
                if h >= 2:
                    o_low(h - 2)
            low(U_AOUT + 3)
            dve.wait_ge(r_w, 1)
            nc.vector.tensor_tensor(wr_hl[:, :, E:2 * E], wr[:, :, :], wr_hl[:, :, 0:E].bitcast(F32), ALU.subtract).then_inc(r_w, 1)
            scale(3, V1)
            low(U_MOE)
            residual(2, [(0, 0, bank[:, 0, :]), (0, 1, bank[:, 1, :]), (1, 0, bank[:, 6, :]), (1, 1, bank[:, 7, :])],
                     [U_MOE - 2] * 2 + [None, U_MOE])

            norm(3, (11, 12))
            low_T(3)
            low(U_MOE + 1)
            low(U_MOE + 2)
            for t in range(TT):
                dve.wait_ge(hh_done, t + 1)
                nc.vector.tensor_tensor(hl[:, t, :], hs[:, t, :], hh[:, t, :].bitcast(F32), ALU.subtract).then_inc(hl_done, 1)
            io8 = iota[:, 0:8]
            dve.wait_ge(r_mm, 1)
            both = rsm[:, :, 0, :]
            link(nc.vector.tensor_tensor(both, bank[:, 0:2, 0:E], brt[:, :].unsqueeze(1).to_broadcast([P, TT, E]), ALU.add))
            link(nc.vector.tensor_tensor(both, bank[:, 0:2, E:2 * E], both, ALU.add))
            for step in range(4):
                for t in range(TT):
                    r = rsm[:, t]
                    if step == 0:
                        ins = nc.vector.max(r[:, 1, :], r[:, 0, :])
                    if step == 1:
                        ins = nc.vector.max_index(ridx[:, t, :], r[:, 1, :], r[:, 0, :])
                    if step == 2:
                        ins = nc.vector.tensor_copy(r[:, 2, :], ridx[:, t, :])
                    if step == 3:
                        nc.vector.tensor_scalar(r[:, 6, :], io8, r[:, 2, 0:1], None, ALU.is_equal)
                        ins = nc.vector.tensor_scalar(r[:, 7, :], io8, r[:, 2, 1:2], None, ALU.is_equal)
                link(ins)
            nc.vector.tensor_tensor(rsm[:, :, 8, :], rsm[:, :, 6, :], rsm[:, :, 7, :], ALU.add).then_inc(r_sel, 1)
            nc.vector.tensor_tensor(rsm[:, :, 4, 0:1], rsm[:, :, 1, 1:2], rsm[:, :, 1, 0:1], ALU.subtract).then_inc(r_d, 1)
            nc.vector.memset(moe[:, :, :], 0.0).then_inc(m_zero, 1)
            dve.wait_ge(r_rank, 1)
            dve.wait_ge(r_sel, 1)
            ranks = bank[:, 2, 0:16].rearrange("p (t e) -> p t e", t=TT)
            link(nc.vector.scalar_tensor_tensor(out=rsm[:, :, 3, :], in0=ranks, scalar=1000.0,
                                                in1=rsm[:, :, 8, :], op0=ALU.add, op1=ALU.mult))
            link(nc.vector.tensor_scalar(pos[:, :, 0:E], rsm[:, :, 3, :], -1000.0, None, ALU.add))
            nc.vector.tensor_scalar(pos[:, :, E:2 * E], rsm[:, :, 3, :], -1000.0 - SLOTS, None, ALU.add)
            for t in range(TT):
                ins = nc.vector.tensor_scalar(pick[:, t, :], iota, pos[:, t, 0:1], None, ALU.is_equal)
            ins.then_inc(pick_done, 1)
            q0 = slice(0, 1)
            link(nc.vector.tensor_scalar(rflag[q0, 0, :], bank[q0, 2, 16:24], float(SLOTS), None, ALU.is_gt))
            link(nc.vector.tensor_scalar(rflag[q0, 1, :], cst[q0, C_IOTA:C_IOTA + 8], -1.0, float(N_TAB), ALU.mult, ALU.add))
            link(nc.vector.tensor_tensor(rflag[q0, 2, :], rflag[q0, 0, :], rflag[q0, 1, :], ALU.mult))
            link(nc.vector.max(rflag[q0, 3, :], rflag[q0, 2, :]))
            link(nc.vector.tensor_copy(rtab[q0, 0:E], cst[q0, C_IOTA:C_IOTA + E]))
            link(nc.vector.tensor_copy(rtab[q0, N_TAB:N_TAB + E], cst[q0, C_IOTA:C_IOTA + E]))
            link(nc.vector.tensor_scalar(rtab[q0, E:N_TAB], rflag[q0, 3, :], -1.0, float(N_TAB), ALU.mult, ALU.add))
            link(nc.vector.tensor_scalar(rtab[q0, E:N_TAB], rtab[q0, E:N_TAB], float(E - 1), None, ALU.min))
            link(nc.vector.tensor_scalar(rtab[q0, N_TAB + E:2 * N_TAB], rtab[q0, E:N_TAB], float(E), None, ALU.add))
            link(nc.vector.tensor_reduce(rtab[q0, 2 * N_TAB:2 * N_TAB + 1], rflag[q0, 0, :], AX.X, ALU.add))
            link(nc.vector.tensor_scalar(rtab[q0, 2 * N_TAB:2 * N_TAB + 1], rtab[q0, 2 * N_TAB:2 * N_TAB + 1], float(E), None, ALU.add))
            nc.vector.tensor_copy(meta[q0, 0:2 * N_TAB + 1], rtab[q0, 0:2 * N_TAB + 1]).then_inc(r_meta, 1)
            dve.wait_ge(r_e, 1)
            for t in range(TT):
                r = rsm[:, t]
                link(nc.vector.tensor_scalar(r[:, 5, 1:2], r[:, 5, 0:1], 1.0, None, ALU.add))
                link(nc.vector.reciprocal(r[:, 5, 2:3], r[:, 5, 1:2]))
                link(nc.vector.tensor_tensor(r[:, 5, 3:4], r[:, 5, 0:1], r[:, 5, 2:3], ALU.mult))
                link(nc.vector.tensor_scalar(r[:, 9, :], r[:, 7, :], r[:, 5, 3:4], None, ALU.mult))
                link(nc.vector.scalar_tensor_tensor(out=comb[:, t, :], in0=r[:, 6, :], scalar=r[:, 5, 2:3],
                                                    in1=r[:, 9, :], op0=ALU.mult, op1=ALU.add))

            def choose(w, col):
                dve.wait_ge(put_tr, w)
                for t in range(TT):
                    ins = nc.vector.tensor_scalar(pick[:, t, :], iota, pos[:, t, col], None, ALU.is_equal)
                ins.then_inc(pick_done, 1)

            def low_gathered(w):
                dve.wait_ge(gath, w * 2 + 2)
                nc.vector.tensor_copy(hg_lo[:, :, :], bank[:, 0:2, :].rearrange("p b (k n) -> p (b k) n", k=4)).then_inc(hg_lo_done, 1)

            def e_mul(n, used):
                dve.wait_ge(w_used, used)
                dve.wait_ge(e_silu, n + 1)
                dve.wait_ge(e_tr, n)
                nc.vector.tensor_tensor(eact[:, :], bank[:, 1, :], esil[:, :], ALU.mult).then_inc(e_act, 1)

            def e_low_act(n):
                dve.wait_ge(e_hi, n + 1)
                nc.vector.tensor_tensor(eaT_lo[:, :, :], bank[:, 2, :].rearrange("p (k n) -> p k n", k=4),
                                        eaT_hi[:, :, :].bitcast(F32), ALU.subtract).then_inc(e_lo, 1)

            low_gathered(0)
            dve.wait_ge(r_meta, 1)

            def low_down(n):
                dve.wait_ge(dn_hi_done, n)
                nc.vector.tensor_tensor(dn_lo[:, :], bank[:, 4:6, :].rearrange("p b n -> p (b n)"),
                                        dn_hi[:, :].bitcast(F32), ALU.subtract).then_inc(dn_done, 1)

            def add(scats, e):
                dve.wait_ge(m_zero, 1)
                for t in range(TT):
                    dve.wait_ge(scat, scats[t])
                    nc.vector.scalar_tensor_tensor(out=moe[:, t, :],
                                                   in0=bank[:, (2, 4)[t]:(4, 6)[t], :].rearrange("p b n -> p (b n)"),
                                                   scalar=comb[:, t, e], in1=moe[:, t, :],
                                                   op0=ALU.mult, op1=ALU.add).then_inc(moe_add, 1)

            def item(w, first, before, col):
                m = w * UNITS_ITEM
                if not first:
                    low(U_MOE, m)
                    low(U_MOE + 1, m)
                    low_down(w)
                    low(U_MOE + 2, m)
                low(U_MOE + 3, m)
                if not first:
                    add((w * TT, w * TT + 1), before)
                choose(w + 1, col)

                def chunk(j, up):
                    jm = m + j * 6 - 6
                    b = U_MOE + 4
                    n = w * N_EC + j
                    low(b, jm)
                    e_mul(n - 1, jm + (RING + U_MOE + up))
                    low(b + 1, jm)
                    low(b + 2, jm)
                    e_low_act(n - 1)
                    low(b + 3, jm)
                    low(b + 4, jm)
                    low(b + 5, jm)

                chunk(1, 4)
                with dve.Fori(2, N_EC) as j:
                    chunk(j, 2)
                e_mul(w * N_EC + N_EC - 1, m + (RING + U_MOE + 4 + 6 * (N_EC - 2) + 4))
                low(U_MOE + UNITS_ITEM - 2, m)
                e_low_act(w * N_EC + N_EC - 1)
                low(U_MOE + UNITS_ITEM - 1, m)
                low_gathered(w + 1)

            item(0, True, None, slice(1, 2))
            dve.wait_ge(row_in, 32)
            scale(4, 0)
            passes = dve.value_load(meta[0:1, 2 * N_TAB:2 * N_TAB + 1], min_val=E, max_val=E + 3)
            with dve.Fori(1, passes) as w:
                before = dve.value_load(meta[0:1, bass.ds(w - 1, 1)], min_val=0, max_val=E - 1)
                col = dve.value_load(meta[0:1, bass.ds(w + N_TAB + 1, 1)], min_val=0, max_val=2 * E - 1)
                item(w, False, bass.ds(before, 1), bass.ds(col, 1))
            m = mods[:, 1, 2]
            dve.wait_ge(moe_add, passes * TT)
            for t in range(TT):
                ins = nc.vector.tensor_tensor(moe[:, t, :], moe[:, t, :], m, ALU.mult)
                link(ins)
                if t == TT - 1:
                    low_down(passes)
                link(nc.vector.tensor_tensor(xs[:, t, :], xs[:, t, :], moe[:, t, :], ALU.add))
            last = dve.value_load(meta[0:1, bass.ds(passes - 1, 1)], min_val=0, max_val=E - 1)
            for t in range(TT):
                dve.wait_ge(scat, passes * TT + t)
                link(nc.vector.scalar_tensor_tensor(out=hs[:, t, :],
                                                    in0=bank[:, (2, 4)[t]:(4, 6)[t], :].rearrange("p b n -> p (b n)"),
                                                    scalar=comb[:, t, bass.ds(last, 1)], in1=m,
                                                    op0=ALU.mult, op1=ALU.mult))
                nc.vector.tensor_tensor(xs[:, t, :], xs[:, t, :], hs[:, t, :], ALU.add).then_inc(resid, 2)
            norm(4, (14, 16))

        @block.tensor
        def _(pe):
            mm = nc.tensor.matmul

            def ada_whole(b, cb):
                s = b % ARING
                own = b < V_OWN
                if own:
                    pe.wait_ge(pre_load[b], 32)
                else:
                    pe.wait_ge(a_load[s], 32 * (b // ARING + 1))
                pe.wait_ge(a_out, ARING + b)
                wt, bias = (pre_w[:, b], pre_b[:, b, :]) if own else (ada_w[:, s], ada_b[:, s, :])
                dst_ap = bank[:, 3, s * AC:(s + 1) * AC]
                mm(dst_ap, ones, bias, start=True, stop=False)
                for k in range(KT):
                    ins = mm(dst_ap, cb[:, k, :], wt[:, k, :], start=False, stop=(k == KT - 1))
                ins.then_inc(a_sum, 1)
                if not own:
                    pe.wait_ge(a_sum, ARING + b + 1)
                    pe.sem_inc(a_free[s], 1)

            def ada_sum(b, n, more=0):
                pe.wait_ge(a_acc, n + 1 + more)
                pe.wait_ge(a_out, ARING + b + more)
                mm(bank[:, 3, (b % ARING) * AC:(b % ARING + 1) * AC], ones, ada_acc[:, b % ARING, :],
                   start=True, stop=True).then_inc(a_sum, 1)

            def turn(s):
                for i in range(4):
                    t, g = i // 2, i % 2
                    pe.wait_ge(h_ready, 2 * s + t + 1)
                    for k in range(4):
                        kt = 4 * g + k
                        ins = nc.tensor.transpose(bank[:, 4 + i, k * P:(k + 1) * P], hs[:, t, kt * P:(kt + 1) * P], ident)
                    ins.then_inc(tr_done, 1)

            def three(dst_ap, a_hi, a_lo, w_hi, w_lo, first, last):
                mm(dst_ap, a_hi, w_hi, start=first, stop=False)
                mm(dst_ap, a_hi, w_lo, start=False, stop=False)
                return mm(dst_ap, a_lo, w_hi, start=False, stop=last)

            def unit(b, nk, more=0):
                pe.wait_ge(lo_done, b + 1 + more)
                h = hi[:, b % HRING, :].rearrange("p (k n) -> p k n", k=nk)
                l = lo[:, b % RING, :].rearrange("p (k n) -> p k n", k=nk)
                return h, l

            def product(b, more, nk, k0, lhs_hi, lhs_lo, dsts, first, last, hT_from=None, tell=False):
                h, l = unit(b, nk, more)
                for t, dst_ap in enumerate(dsts):
                    if hT_from is not None:
                        pe.wait_ge(hT_done, 4 * hT_from + 2 * t + k0 // 4 + 1)
                    for k in range(nk):
                        tok = slice(t * P, (t + 1) * P)
                        ins = three(dst_ap, lhs_hi[:, k0 + k, tok], lhs_lo[:, k0 + k, tok], h[:, k, :], l[:, k, :],
                                    first and k == 0, last and k == nk - 1)
                    if tell and t == 0:
                        ins.then_inc(t0_done, 1)
                ins.then_inc(w_used, 1)

            pe.wait_ge(const_in, 16)
            pe.wait_ge(cb_done, 1)
            for v in range(V_PRE):
                if v % 2:
                    ada_whole(v, cb0)
                else:
                    ada_sum(v, v // 2)
            turn(0)
            pe.wait_ge(hT_done, 4)
            PAIRS = [(0, 1), (2, 4), (5, 6)]
            with pe.Fori(0, N_IN // 3) as it:
                for k in range(6):
                    i = k // 2
                    if k % 2 == 0:
                        pe.wait_ge(proj_out, it * 3 + i + 1)
                    product(U_RET + k, it * 6, 4, 4 * (k % 2), hT_hi, hT_lo, [bank[:, PAIRS[i][t], :] for t in range(TT)],
                            k % 2 == 0, k % 2 == 1)
                    if k in (0, 1, 3, 4):
                        a = (0, 1, None, 2, 3)[k]
                        ada_sum(V_PRE + a, V_PRE // 2 + a, it * 4)

            def turn_qk(h):
                for n, bk in ((0, 4), (2, 5)):
                    if h:
                        pe.wait_ge(qT_done if n == 0 else kT_done, h)
                    for k in range(2):
                        for t in range(TT):
                            o = (h % 2) * RDK + k * P
                            ins = nc.tensor.transpose(bank[:, bk, k * SEQ + t * P:k * SEQ + (t + 1) * P],
                                                      proj[:, n + h // 2, t, o:o + P], ident)
                    ins.then_inc(qk_tr, 1)

            def scores(h):
                pe.wait_ge(qT_done, h + 1)
                pe.wait_ge(kT_done, h + 1)
                if h:
                    pe.wait_ge(s_done, h)
                for jt in range(TT):
                    for k in range(2):
                        ins = mm(bank[:, 6, jt * SEQ:(jt + 1) * SEQ], rkT[:, h % 2, k, jt * P:(jt + 1) * P],
                                 rqT[:, h % 2, k, :], start=(k == 0), stop=(k == 1))
                ins.then_inc(sc_done, 1)

            def values(h):
                pe.wait_ge(s_done, h + 1)
                if h:
                    pe.wait_ge(st_done, 2 * h)
                    pe.wait_ge(yraw_done, 2 * h)
                for t in range(TT):
                    for jt in range(TT):
                        ins = mm(bank[:, (7, 2)[t], :], dec[:, h % 2, jt * SEQ + t * P:jt * SEQ + (t + 1) * P],
                                 proj[:, 4 + h, jt, :], start=(jt == 0), stop=(jt == TT - 1))
                    ins.then_inc(y_done, 1)

            pe.wait_ge(rope_done, 1)
            pe.wait_ge(proj_out, 3 + N_IN)
            turn_qk(0)
            for h in range(RH):
                scores(h)
                if h + 1 < RH:
                    turn_qk(h + 1)
                values(h)
            for i in range(8):
                h, t = i // 2, i % 2
                pe.wait_ge(gated, i + 1)
                if i == 3:
                    pe.wait_ge(st_done, 2 * RH)
                    pe.wait_ge(yraw_done, 2 * RH)
                if i >= 4:
                    pe.wait_ge(yT_done, i - 3)
                for k in range(4):
                    ins = nc.tensor.transpose(bank[:, 4 + i % 4, k * P:(k + 1) * P], proj[:, 8 + h, t, k * P:(k + 1) * P], ident)
                ins.then_inc(y_tr, 1)
            pe.wait_ge(yT_done, 8)
            v = V_PRE + V_IN
            OUT = [(0, 1), (6, 7)]
            for k in range(8):
                n, kg = k // 4, k % 4
                product(U_ROUT + k, 0, 4, 4 * kg, yT_hi, yT_lo, [bank[:, OUT[n][t], :] for t in range(TT)],
                        kg == 0, kg == 3, tell=(k == 7))
                if k < 7:
                    ada_sum(v + k, V_PRE // 2 + V_IN + k)

            V0 = V_PRE + V_IN + V_FIN
            turn(1)

            def f_gate_up(b, more, cc, hT_from=None):
                pe.wait_ge(f_act, cc)
                for j in range(2):
                    product(b + j, more, 4, 4 * j, hT_hi, hT_lo, [bank[:, t, :] for t in range(TT)], j == 0, j == 1, hT_from)

            def f_turn(cc):
                pe.wait_ge(f_act, cc + 1)
                for k in range(2):
                    for t in range(TT):
                        ins = nc.tensor.transpose(bank[:, 2, k * SEQ + t * P:k * SEQ + (t + 1) * P],
                                                  fact[:, t, k * P:(k + 1) * P], ident)
                ins.then_inc(f_tr, 1)

            def f_down(b, more, cc, first, last):
                pe.wait_ge(f_lo, cc + 1)
                h, l = unit(b, 2, more)
                for t in range(TT):
                    for n in range(2):
                        for k in range(2):
                            tok, cols = slice(t * P, (t + 1) * P), slice(n * CB, (n + 1) * CB)
                            ins = three(bank[:, 4 + 2 * t + n, :], faT_hi[:, k, tok], faT_lo[:, k, tok],
                                        h[:, k, cols], l[:, k, cols], first and k == 0, last and k == 1)
                    if last and t == 0:
                        ins.then_inc(t0_done, 1)
                ins.then_inc(w_used, 1)

            def sum_pair(more):
                pe.wait_ge(a_acc, N0 + 2 + more)
                pe.wait_ge(a_out, ARING + V0 + more)
                mm(bank[:, 3, 0:AC], ones, ada_acc[:, 0, :], start=True, stop=True)
                mm(bank[:, 3, AC:2 * AC], ones, ada_acc[:, 1, :], start=True, stop=True).then_inc(a_sum, 2)

            N0 = V_PRE // 2 + V_IN + V_FIN
            f_gate_up(U_FF, 0, 0, 1)
            ada_sum(V0 - 1, N0 - 1)
            f_turn(0)
            def f_chunk(b, more, cc, first, a):
                f_gate_up(b, more, cc)
                f_down(b + 2, more, cc - 1, first, False)
                sum_pair(a)
                f_turn(cc)

            f_chunk(U_FF + 2, 0, 1, True, 0)
            f_chunk(U_FF + 5, 0, 2, False, 2)
            with pe.Fori(1, (N_FF - 1) // 2) as it:
                for q in range(2):
                    f_chunk(U_FF + 2 + 3 * q, it * 6, it * 2 + 1 + q, False, it * 4 + 2 * q)
            f_down(U_QKV - 1, 0, N_FF - 1, False, True)

            V1 = V0 + V_FF
            turn(2)
            for k in range(6):
                n, kg = k // 2, k % 2
                product(U_QKV + k, 0, 4, 4 * kg, hT_hi, hT_lo, [bank[:, PAIRS[n][t], :] for t in range(TT)],
                        kg == 0, kg == 1, 2 if k < 2 else None)
            pe.wait_ge(cb_done, 2)
            for a in range(2):
                ada_whole(V1 + a, cb1)
            for i in range(5):
                if i == 0:
                    pe.wait_ge(arope, 2)
                    pe.wait_ge(qkv_out, 3)
                if i >= 2:
                    pe.wait_ge(aq_out, i - 1)
                for k in range(2):
                    for t in range(TT):
                        hd = 2 * i + k
                        ins = nc.tensor.transpose(bank[:, (4, 5)[i % 2], k * SEQ + t * P:k * SEQ + (t + 1) * P],
                                                  qkv[:, t, hd * AHD:(hd + 1) * AHD], ident)
                ins.then_inc(aq_tr, 1)
            pe.wait_ge(aq_out, 5)

            def a_scores(h):
                if h >= 2:
                    pe.wait_ge(at_exp, 2 * h - 2)
                for t in range(TT):
                    ins = mm(bank[:, 4 + h % 2, t * SEQ:(t + 1) * SEQ], aqT[:, h, t * P:(t + 1) * P],
                             akT[:, h // (AH // AKV), :], start=True, stop=True)
                ins.then_inc(at_sc, 1)

            def a_turn(h):
                pe.wait_ge(at_norm, 2 * h + 2)
                if h >= 2:
                    pe.wait_ge(at_pT, h - 1)
                for k in range(TT):
                    for t in range(TT):
                        ins = nc.tensor.transpose(bank[:, 6 + h % 2, k * SEQ + t * P:k * SEQ + (t + 1) * P],
                                                  prob[:, h % 2, t, k * P:(k + 1) * P], ident)
                ins.then_inc(at_tr, 1)

            def a_values(h):
                pe.wait_ge(at_pT, h + 1)
                if h >= 2:
                    pe.wait_ge(o_lo, h - 1)
                vo = (AH + AKV + h // (AH // AKV)) * AHD
                for k in range(TT):
                    ins = mm(bank[:, h % 2, 0:SEQ], qkv[:, k, vo:vo + AHD], probT[:, h % 2, k, :],
                             start=(k == 0), stop=(k == TT - 1))
                ins.then_inc(at_o, 1)

            for h in range(AH + 2):
                if h < AH:
                    a_scores(h)
                if 1 <= h <= AH:
                    a_turn(h - 1)
                if h >= 2:
                    a_values(h - 2)
                if h in (4, 6):
                    ada_whole(V1 + h // 2, cb1)
            pe.wait_ge(o_lo, AH)
            for k in range(4):
                n, kg = k // 2, k % 2
                product(U_AOUT + k, 0, 4, 4 * kg, oT_hi, oT_lo, [bank[:, OUT[n][t], :] for t in range(TT)],
                        kg == 0, kg == 1, tell=(k == 3))

            turn(3)
            pe.wait_ge(hT_done, 16)
            pe.wait_ge(r_w, 2)
            for t in range(TT):
                tok = slice(t * P, (t + 1) * P)
                for k in range(KT):
                    mm(bank[:, t, 0:2 * E], hT_hi[:, k, tok], wr_hl[:, k, :], start=(k == 0), stop=False)
                    ins = mm(bank[:, t, 0:2 * E], hT_lo[:, k, tok], wr_hl[:, k, :], start=False, stop=(k == KT - 1))
            ins.then_inc(r_mm, 1)
            pe.wait_ge(r_sel, 1)
            mm(bank[:, 2, 0:8], tri, rsm[:, 0, 8, :], start=True, stop=True)
            mm(bank[:, 2, 8:16], tri, rsm[:, 1, 8, :], start=True, stop=False)
            mm(bank[:, 2, 8:16], ones, rsm[:, 0, 8, :], start=False, stop=True)
            mm(bank[:, 2, 16:24], ones, rsm[:, 0, 8, :], start=True, stop=False)
            mm(bank[:, 2, 16:24], ones, rsm[:, 1, 8, :], start=False, stop=True).then_inc(r_rank, 1)

            def gather(w):
                pe.wait_ge(pick_done, w + 1)
                pe.wait_ge(put_done, w)
                for part, b0 in ((hh, 6), (hl, 0)):
                    for k in range(KT):
                        for t in range(TT):
                            ins = mm(bank[:, b0 + k // 4, (k % 4) * P:(k % 4 + 1) * P], part[:, t, k * P:(k + 1) * P],
                                     pick[:, t, :], start=(t == 0), stop=(t == TT - 1))
                    ins.then_inc(gath, 1)

            def turn_pick(w):
                pe.wait_ge(hg_hi_done, w + 1)
                for t in range(TT):
                    ins = nc.tensor.transpose(bank[:, 6, t * P:(t + 1) * P], pick[:, t, :].bitcast(F32), ident)
                ins.then_inc(put_tr, 1)

            def e_turn(n):
                pe.wait_ge(e_act, n + 1)
                for k in range(4):
                    ins = nc.tensor.transpose(bank[:, 2, k * P:(k + 1) * P], eact[:, k * P:(k + 1) * P], ident)
                ins.then_inc(e_tr, 1)

            def e_down_step(b, more, n, first, last):
                pe.wait_ge(e_lo, n + 1)
                for g in range(2):
                    h, l = unit(b + g, 2, more)
                    for c2 in range(2):
                        for k in range(2):
                            cols = slice(c2 * CB, (c2 + 1) * CB)
                            ins = three(bank[:, 4 + c2, :], eaT_hi[:, 2 * g + k, :], eaT_lo[:, 2 * g + k, :], h[:, k, cols],
                                        l[:, k, cols], first and g == 0 and k == 0, last and g == 1 and k == 1)
                    ins.then_inc(w_used, 1)

            def scatter(n):
                pe.wait_ge(dn_done, n)
                pe.wait_ge(put_done, n)
                for t in range(TT):
                    for n in range(2):
                        cols = slice(n * CB, (n + 1) * CB)
                        mm(bank[:, (2, 4)[t] + n, :], put[:, t * P:(t + 1) * P], dn_hi[:, cols], start=True, stop=False)
                        ins = mm(bank[:, (2, 4)[t] + n, :], put[:, t * P:(t + 1) * P], dn_lo[:, cols], start=False, stop=True)
                    ins.then_inc(scat, 1)

            def e_half(b, j, more):
                for g in range(2):
                    h, l = unit(b + 2 * j + g, 4, more)
                    for k in range(4):
                        ins = three(bank[:, j, :], hg_hi[:, 4 * g + k, :], hg_lo[:, 4 * g + k, :], h[:, k, :], l[:, k, :],
                                    g == 0 and k == 0, g == 1 and k == 3)
                    ins.then_inc(w_used, 1)

            def e_gate_up(b, more, n):
                pe.wait_ge(e_act, n)
                e_half(b, 0, more)
                e_half(b, 1, more)

            def item(w, first):
                m = w * UNITS_ITEM
                pe.wait_ge(hg_hi_done, w + 1)
                pe.wait_ge(hg_lo_done, w + 1)
                e_half(U_MOE, 0, m)
                if not first:
                    scatter(w)
                turn_pick(w)
                e_half(U_MOE, 1, m)
                if not first:
                    pe.wait_ge(moe_add, w * TT + TT)
                e_turn(w * N_EC)
                e_gate_up(U_MOE + 4, m, w * N_EC + 1)
                e_down_step(U_MOE + 8, m, w * N_EC, True, False)
                e_turn(w * N_EC + 1)
                with pe.Fori(2, N_EC) as j:
                    jm = m + j * 6 - 6
                    e_gate_up(U_MOE + 4, jm, w * N_EC + j)
                    e_down_step(U_MOE + 8, jm, w * N_EC + j - 1, False, False)
                    e_turn(w * N_EC + j)
                gather(w + 1)
                e_down_step(U_MOE + UNITS_ITEM - 2, m, w * N_EC + N_EC - 1, False, True)

            pe.wait_ge(hl_done, 2)
            gather(0)
            item(0, True)
            pe.wait_ge(r_meta, 1)
            passes = pe.value_load(meta[0:1, 2 * N_TAB:2 * N_TAB + 1], min_val=E, max_val=E + 3)
            with pe.Fori(1, passes) as w:
                item(w, False)
            scatter(passes)


_INS = ['x', 'c', 'l0_ada_w', 'l0_ada_b', 'l0_norm1_g', 'l0_norm2_g', 'l0_ret_w_in', 'l0_ret_decay_logit',
        'l0_ret_gn_g', 'l0_ret_w_out', 'l0_ffn_w_gate', 'l0_ffn_w_up', 'l0_ffn_w_down', 'l1_ada_w', 'l1_ada_b',
        'l1_norm1_g', 'l1_norm2_g', 'l1_attn_w_qkv', 'l1_attn_q_norm_g', 'l1_attn_k_norm_g', 'l1_attn_w_out',
        'l1_moe_w_router', 'l1_moe_b_router', 'l1_moe_w_gate', 'l1_moe_w_up', 'l1_moe_w_down',
        'final_ada_w', 'final_ada_b', 'final_norm_g']


def kernel(**inputs):
    import concourse.bacc as _bacc
    from concourse.bass_utils import run_bass_kernel_spmd as _run

    nc = _bacc.Bacc("TRN2", target_bir_lowering=False, num_devices=1)
    given = {name: np.ascontiguousarray(inputs[name]) for name in _INS}
    given["consts"], given["dist"] = shape_constants()
    arrays, args = {}, []
    for name, a in given.items():
        arrays[f"in_{name}"] = a
        args.append(nc.dram_tensor(f"in_{name}", a.shape, mybir.dt.from_np(a.dtype), kind="ExternalInput").ap())
    out = nc.dram_tensor("out_0", (1, SEQ, D), F32, kind="ExternalOutput").ap()
    encoder(nc, *args, out)
    r = _run(nc, [arrays], core_ids=[0])
    return r.results[0]["out_0"]
```
